# Optimizing a Trainium2 kernel written in Bass

```python
import math
import jax, jax.numpy as jnp
from jax import lax
import numpy as np

D_MODEL = 1024
BATCH = 1
SEQ = 1024
DEPTH = 2
DEC_BATCH = 8
DEC_SEQ = 8
PAST_LEN = 1024
PAGE_SIZE = 128

N_A_LAYERS = DEPTH // 2
N_B_LAYERS = DEPTH - N_A_LAYERS
EXPAND = 2
D_INNER = EXPAND * D_MODEL
SSM_HEADDIM = 64
SSM_HEADS = D_INNER // SSM_HEADDIM
SSM_GROUPS = 4
D_STATE = 128
CONV_K = 4
CONV_DIM = D_INNER + 2 * SSM_GROUPS * D_STATE
SSD_CHUNK = 128
M_IN_DIM = D_INNER + CONV_DIM + SSM_HEADS
ATT_HEAD_DIM = 64
ATT_HEADS = D_MODEL // ATT_HEAD_DIM
ATT_KV_HEADS = 4
ATT_REP = ATT_HEADS // ATT_KV_HEADS
DILATION_GROUPS = ((128, 1), (512, 4), (2048, 16))
N_DGROUPS = len(DILATION_GROUPS)
ATT_WIDTH = ATT_HEADS * ATT_HEAD_DIM
KV_DIM = 2 * N_DGROUPS * ATT_KV_HEADS * ATT_HEAD_DIM
Q_BLOCK = 128
ROPE_THETA = 10000.0
PLE_DIM = 256
EPS = 1e-6

kernel_name = 'yoco_ssd_dilated_swa_decoder_step'

def rms_norm(x, w):
    xf = x.astype(jnp.float32)
    y = xf * lax.rsqrt(jnp.mean(xf * xf, axis=-1, keepdims=True) + EPS)
    return (y * w.astype(jnp.float32)).astype(x.dtype)

def rope(x, pos):
    half = x.shape[-1] // 2
    inv = 1.0 / (ROPE_THETA ** (jnp.arange(half, dtype=jnp.float32) / half))
    ang = pos.astype(jnp.float32)[:, None] * inv[None, :]
    ang = ang.reshape((ang.shape[0],) + (1,) * (x.ndim - 3) + (half,))
    cos, sin = jnp.cos(ang), jnp.sin(ang)
    xf = x.astype(jnp.float32)
    x1, x2 = xf[..., :half], xf[..., half:]
    return jnp.concatenate([x1 * cos - x2 * sin, x2 * cos + x1 * sin], axis=-1).astype(x.dtype)

def ssd(x, dt, A, B, C, h0, chunk):
    b, L, nh, p = x.shape
    g, n = B.shape[2], B.shape[3]
    r = nh // g
    c = L // chunk
    f32 = jnp.float32
    x = x.astype(f32).reshape(b, c, chunk, g, r, p)
    dt = dt.astype(f32).reshape(b, c, chunk, g, r)
    B = B.astype(f32).reshape(b, c, chunk, g, n)
    C = C.astype(f32).reshape(b, c, chunk, g, n)
    acum = jnp.cumsum(dt * A.reshape(g, r), axis=2)
    causal = jnp.tril(jnp.ones((chunk, chunk), dtype=bool))
    seg = acum[:, :, :, None] - acum[:, :, None, :]
    decay_ls = jnp.exp(jnp.where(causal[None, None, :, :, None, None], seg, -jnp.inf))
    xdt = x * dt[..., None]
    cb = jnp.einsum('bclgn,bcsgn->bclsg', C, B)
    y_diag = jnp.einsum('bclsgr,bcsgrp->bclgrp', cb[..., None] * decay_ls, xdt)
    decay_end = jnp.exp(acum[:, :, -1:] - acum)
    states = jnp.einsum('bcsgn,bcsgrp->bcgrpn', B, xdt * decay_end[..., None])
    chunk_decay = jnp.exp(acum[:, :, -1])

    def step(h, inp):
        dec, st = inp
        return h * dec[..., None, None] + st, h

    h_final, h_in = lax.scan(step, h0.astype(f32).reshape(b, g, r, p, n),
                             (jnp.moveaxis(chunk_decay, 1, 0), jnp.moveaxis(states, 1, 0)))
    y_off = jnp.einsum('bclgn,cbgrpn->bclgrp', C, h_in) * jnp.exp(acum)[..., None]
    y = (y_diag + y_off).reshape(b, L, nh, p)
    return y, h_final.reshape(b, nh, p, n)

def mamba_mixer(u, conv_state, ssm_state, in_w, conv_w, conv_b, dt_bias, A_log, d_skip, norm_w, out_w):
    b, L, _ = u.shape
    proj = u @ in_w
    z = proj[..., :D_INNER]
    xbc = proj[..., D_INNER:D_INNER + CONV_DIM]
    dt_raw = proj[..., D_INNER + CONV_DIM:]
    xpad = jnp.concatenate([conv_state.astype(xbc.dtype), xbc], axis=1)
    new_conv = xpad[:, xpad.shape[1] - (CONV_K - 1):]
    acc = conv_b + xpad[:, 0:L] * conv_w[0]
    for k in range(1, CONV_K):
        acc = acc + xpad[:, k:k + L] * conv_w[k]
    xbc = jax.nn.silu(acc)
    xs = xbc[..., :D_INNER]
    Bm = xbc[..., D_INNER:D_INNER + SSM_GROUPS * D_STATE].reshape(b, L, SSM_GROUPS, D_STATE)
    Cm = xbc[..., D_INNER + SSM_GROUPS * D_STATE:].reshape(b, L, SSM_GROUPS, D_STATE)
    dt = jax.nn.softplus((dt_raw + dt_bias).astype(jnp.float32))
    A = -jnp.exp(A_log.astype(jnp.float32))
    xh = xs.reshape(b, L, SSM_HEADS, SSM_HEADDIM)
    y, h = ssd(xh, dt, A, Bm, Cm, ssm_state, math.gcd(L, SSD_CHUNK))
    y = y + xh.astype(jnp.float32) * d_skip.astype(jnp.float32)[:, None]
    y = y.reshape(b, L, D_INNER) * jax.nn.silu(z.astype(jnp.float32))
    yg = y.reshape(b, L, SSM_GROUPS, D_INNER // SSM_GROUPS)
    yg = yg * lax.rsqrt(jnp.mean(yg * yg, axis=-1, keepdims=True) + EPS)
    y = yg.reshape(b, L, D_INNER) * norm_w.astype(jnp.float32)
    return y.astype(u.dtype) @ out_w, new_conv, h.astype(ssm_state.dtype)

def shared_kv(h, pos, kv_norm_w, kv_w, k_norm_w):
    b, L, _ = h.shape
    kv = (rms_norm(h, kv_norm_w) @ kv_w).reshape(b, L, 2, N_DGROUPS, ATT_KV_HEADS, ATT_HEAD_DIM)
    k = rope(rms_norm(kv[:, :, 0], k_norm_w), pos)
    return k, kv[:, :, 1]

def dilated_attend(q, kv_groups, rows_groups):
    b, Lq = q.shape[:2]
    outs, lses = [], []
    for gi in range(N_DGROUPS):
        window, dil = DILATION_GROUPS[gi]
        k, v = kv_groups[gi]
        n_keys = window // dil + 1
        idx = rows_groups[gi][:, None] - dil * jnp.arange(n_keys, dtype=jnp.int32)[None, :]
        valid = idx >= 0
        idx = jnp.maximum(idx, 0)
        kg = jnp.take(k, idx, axis=1)
        vg = jnp.take(v, idx, axis=1)
        qg = q[:, :, gi].reshape(b, Lq, ATT_KV_HEADS, ATT_REP, ATT_HEAD_DIM)
        s = jnp.einsum('bqkrd,bqjkd->bqkrj', qg, kg).astype(jnp.float32)
        s = jnp.where(valid[None, :, None, None, :], s, -jnp.inf)
        lse = jax.nn.logsumexp(s, axis=-1)
        pr = jnp.exp(s - lse[..., None])
        o = jnp.einsum('bqkrj,bqjkd->bqkrd', pr.astype(vg.dtype), vg)
        outs.append(o.astype(jnp.float32))
        lses.append(lse)
    wts = jax.nn.softmax(jnp.stack(lses, axis=0), axis=0)
    o = jnp.sum(jnp.stack(outs, axis=0) * wts[..., None], axis=0)
    return o.reshape(b, Lq, ATT_HEADS, ATT_HEAD_DIM)

def prompt_attend(q, k, v):
    b, L = q.shape[:2]
    nb = L // Q_BLOCK
    kvs = [(k[:, :, g], v[:, :, g]) for g in range(N_DGROUPS)]
    qb = jnp.moveaxis(q.reshape((b, nb, Q_BLOCK) + q.shape[2:]), 1, 0)
    starts = jnp.arange(nb, dtype=jnp.int32) * Q_BLOCK

    def blk(args):
        qi, st = args
        rows = st + jnp.arange(Q_BLOCK, dtype=jnp.int32)
        return dilated_attend(qi, kvs, [rows] * N_DGROUPS)

    o = lax.map(blk, (qb, starts))
    return jnp.moveaxis(o, 0, 1).reshape(b, L, ATT_HEADS, ATT_HEAD_DIM)

def attn_mixer(u, pos, attend, in_w, q_norm_w, out_w):
    b, L, _ = u.shape
    proj = u @ in_w
    q = proj[..., :N_DGROUPS * ATT_WIDTH].reshape(b, L, N_DGROUPS, ATT_HEADS, ATT_HEAD_DIM)
    gate = proj[..., N_DGROUPS * ATT_WIDTH:]
    q = rope(rms_norm(q, q_norm_w), pos) * (ATT_HEAD_DIM ** -0.5)
    o = attend(q)
    y = o.reshape(b, L, ATT_WIDTH) * jax.nn.silu(gate.astype(jnp.float32))
    return y.astype(u.dtype) @ out_w

def ple_add(h, p_i, ple_w_i, gate_w_i, ple_norm_i):
    gate = jax.nn.sigmoid((rms_norm(h, ple_norm_i) @ gate_w_i).astype(jnp.float32))
    return h + (gate * (p_i @ ple_w_i).astype(jnp.float32)).astype(h.dtype)

def trunk(x, p, pos, conv_states, ssm_states, make_attend, W):
    h = x
    new_conv, new_ssm = [], []
    k_sh, v_sh, attend = None, None, None
    for i in range(DEPTH):
        if i < N_A_LAYERS:
            u = rms_norm(h, W['norm_w'][i])
            out, c_new, s_new = mamba_mixer(u, conv_states[i], ssm_states[i], W['m_in_w'][i], W['m_conv_w'][i],
                                            W['m_conv_b'][i], W['m_dt_bias'][i], W['m_A_log'][i], W['m_D'][i],
                                            W['m_norm_w'][i], W['m_out_w'][i])
            new_conv.append(c_new)
            new_ssm.append(s_new)
        else:
            if i == N_A_LAYERS:
                k_sh, v_sh = shared_kv(h, pos, W['kv_norm_w'], W['kv_w'], W['k_norm_w'])
                attend = make_attend(k_sh, v_sh)
            j = i - N_A_LAYERS
            u = rms_norm(h, W['norm_w'][i])
            out = attn_mixer(u, pos, attend, W['a_in_w'][j], W['a_q_norm_w'][j], W['a_out_w'][j])
        h = h + out
        h = ple_add(h, p[i], W['ple_w'][i], W['ple_gate_w'][i], W['ple_norm_w'][i])
    return h, jnp.stack(new_conv, axis=0), jnp.stack(new_ssm, axis=0), k_sh, v_sh

def setup_inputs(seed: int = 0) -> dict:
    key = jax.random.key(seed)
    ks = jax.random.split(key, 32)
    f32 = jnp.float32

    def nrm(k, shape):
        return jax.random.normal(k, shape, f32)

    dt0 = jnp.exp(jax.random.uniform(ks[0], (N_A_LAYERS, SSM_HEADS), f32) * (math.log(0.1) - math.log(0.001)) + math.log(0.001))
    dt_bias = dt0 + jnp.log(-jnp.expm1(-dt0))
    A_log = jnp.log(jax.random.uniform(ks[1], (N_A_LAYERS, SSM_HEADS), f32, 1.0, 16.0))
    win_len = [min(w, PAST_LEN) for (w, _) in DILATION_GROUPS]
    return {
        'x_prompt': nrm(ks[2], (BATCH, SEQ, D_MODEL)),
        'x_sample': nrm(ks[3], (DEC_BATCH, DEC_SEQ, D_MODEL)),
        'state_ssm': 0.1 * nrm(ks[4], (N_A_LAYERS, DEC_BATCH, SSM_HEADS, SSM_HEADDIM, D_STATE)),
        'state_conv': nrm(ks[5], (N_A_LAYERS, DEC_BATCH, CONV_K - 1, CONV_DIM)),
        'cache_kv_g1': nrm(ks[6], (DEC_BATCH, win_len[0], 2, ATT_KV_HEADS, ATT_HEAD_DIM)),
        'cache_kv_g2': nrm(ks[7], (DEC_BATCH, win_len[1], 2, ATT_KV_HEADS, ATT_HEAD_DIM)),
        'cache_kv_g3': nrm(ks[8], (DEC_BATCH, win_len[2], 2, ATT_KV_HEADS, ATT_HEAD_DIM)),
        'p_prompt': nrm(ks[9], (DEPTH, BATCH, SEQ, PLE_DIM)),
        'p_sample': nrm(ks[10], (DEPTH, DEC_BATCH, DEC_SEQ, PLE_DIM)),
        'norm_w': 1.0 + 0.02 * nrm(ks[11], (DEPTH, D_MODEL)),
        'm_in_w': nrm(ks[12], (N_A_LAYERS, D_MODEL, M_IN_DIM)) * D_MODEL ** -0.5,
        'm_conv_w': nrm(ks[13], (N_A_LAYERS, CONV_K, CONV_DIM)) * CONV_K ** -0.5,
        'm_conv_b': 0.02 * nrm(ks[14], (N_A_LAYERS, CONV_DIM)),
        'm_dt_bias': dt_bias,
        'm_A_log': A_log,
        'm_D': 1.0 + 0.02 * nrm(ks[15], (N_A_LAYERS, SSM_HEADS)),
        'm_norm_w': 1.0 + 0.02 * nrm(ks[16], (N_A_LAYERS, D_INNER)),
        'm_out_w': nrm(ks[17], (N_A_LAYERS, D_INNER, D_MODEL)) * D_INNER ** -0.5,
        'kv_norm_w': 1.0 + 0.02 * nrm(ks[18], (D_MODEL,)),
        'kv_w': nrm(ks[19], (D_MODEL, KV_DIM)) * D_MODEL ** -0.5,
        'k_norm_w': 1.0 + 0.02 * nrm(ks[20], (ATT_HEAD_DIM,)),
        'a_in_w': nrm(ks[21], (N_B_LAYERS, D_MODEL, (N_DGROUPS + 1) * ATT_WIDTH)) * D_MODEL ** -0.5,
        'a_q_norm_w': 1.0 + 0.02 * nrm(ks[22], (N_B_LAYERS, ATT_HEAD_DIM)),
        'a_out_w': nrm(ks[23], (N_B_LAYERS, ATT_WIDTH, D_MODEL)) * ATT_WIDTH ** -0.5,
        'ple_w': nrm(ks[24], (DEPTH, PLE_DIM, D_MODEL)) * PLE_DIM ** -0.5,
        'ple_gate_w': nrm(ks[25], (DEPTH, D_MODEL, D_MODEL)) * D_MODEL ** -0.5,
        'ple_norm_w': 1.0 + 0.02 * nrm(ks[26], (DEPTH, D_MODEL)),
    }

def reference(x_prompt, x_sample, state_ssm, state_conv, cache_kv_g1, cache_kv_g2, cache_kv_g3,
              p_prompt, p_sample, norm_w, m_in_w, m_conv_w, m_conv_b, m_dt_bias, m_A_log, m_D,
              m_norm_w, m_out_w, kv_norm_w, kv_w, k_norm_w, a_in_w, a_q_norm_w, a_out_w,
              ple_w, ple_gate_w, ple_norm_w):
    W = {'norm_w': norm_w, 'm_in_w': m_in_w, 'm_conv_w': m_conv_w, 'm_conv_b': m_conv_b,
         'm_dt_bias': m_dt_bias, 'm_A_log': m_A_log, 'm_D': m_D, 'm_norm_w': m_norm_w,
         'm_out_w': m_out_w, 'kv_norm_w': kv_norm_w, 'kv_w': kv_w, 'k_norm_w': k_norm_w,
         'a_in_w': a_in_w, 'a_q_norm_w': a_q_norm_w, 'a_out_w': a_out_w, 'ple_w': ple_w,
         'ple_gate_w': ple_gate_w, 'ple_norm_w': ple_norm_w}

    b_p, seq = x_prompt.shape[0], x_prompt.shape[1]
    pos_p = jnp.arange(seq, dtype=jnp.int32)
    conv0 = jnp.zeros((N_A_LAYERS, b_p, CONV_K - 1, CONV_DIM), x_prompt.dtype)
    ssm0 = jnp.zeros((N_A_LAYERS, b_p, SSM_HEADS, SSM_HEADDIM, D_STATE), x_prompt.dtype)
    y_prompt, conv_p, ssm_p, k_p, v_p = trunk(x_prompt, p_prompt, pos_p, conv0, ssm0,
                                              lambda k, v: (lambda q: prompt_attend(q, k, v)), W)
    lw = [min(w, seq) for (w, _) in DILATION_GROUPS]
    kv_p1 = jnp.stack([k_p[:, seq - lw[0]:, 0], v_p[:, seq - lw[0]:, 0]], axis=2)
    kv_p2 = jnp.stack([k_p[:, seq - lw[1]:, 1], v_p[:, seq - lw[1]:, 1]], axis=2)
    kv_p3 = jnp.stack([k_p[:, seq - lw[2]:, 2], v_p[:, seq - lw[2]:, 2]], axis=2)

    dec_seq = x_sample.shape[1]
    pos_s = PAST_LEN + jnp.arange(dec_seq, dtype=jnp.int32)
    caches = (cache_kv_g1, cache_kv_g2, cache_kv_g3)

    def sample_make_attend(k, v):
        kvs = [(jnp.concatenate([caches[g][:, :, 0].astype(k.dtype), k[:, :, g]], axis=1),
                jnp.concatenate([caches[g][:, :, 1].astype(v.dtype), v[:, :, g]], axis=1))
               for g in range(N_DGROUPS)]
        rows = [caches[g].shape[1] + jnp.arange(dec_seq, dtype=jnp.int32) for g in range(N_DGROUPS)]
        return lambda q: dilated_attend(q, kvs, rows)

    y_sample, conv_s, ssm_s, k_s, v_s = trunk(x_sample, p_sample, pos_s, state_conv, state_ssm,
                                              sample_make_attend, W)
    kv_s1 = jnp.stack([k_s[:, :, 0], v_s[:, :, 0]], axis=2)
    kv_s2 = jnp.stack([k_s[:, :, 1], v_s[:, :, 1]], axis=2)
    kv_s3 = jnp.stack([k_s[:, :, 2], v_s[:, :, 2]], axis=2)
    return (y_prompt, y_sample, ssm_p, conv_p, ssm_s, conv_s, kv_p1, kv_p2, kv_p3, kv_s1, kv_s2, kv_s3)


_drawn_inputs = setup_inputs


def setup_inputs(seed=0):
    import zlib

    import numpy as np

    out = dict(_drawn_inputs(seed))
    spreads = {}
    factors = {'cache_kv_g1': 2.676,
     'cache_kv_g2': 2.74,
     'cache_kv_g3': 3.831,
     'm_D': 8.0,
     'm_norm_w': 4.26,
     'kv_norm_w': 2.868,
     'k_norm_w': 4.146,
     'a_q_norm_w': 8.0,
     'ple_norm_w': 45.692}
    for name, (base, spread) in spreads.items():
        noise = np.random.default_rng([zlib.crc32(name.encode()), seed]).standard_normal(out[name].shape)
        drawn = base * np.exp(spread * noise) if base else spread * noise
        out[name] = __import__('jax').numpy.asarray(drawn.astype(out[name].dtype))
    for name, factor in factors.items():
        out[name] = (out[name] * factor).astype(out[name].dtype)
    return out
```

```python
from contextlib import ExitStack

import numpy as np

import concourse.bass as bass
from concourse import mybir

F32 = mybir.dt.float32
ALU = mybir.AluOpType
ACT = mybir.ActivationFunctionType
AX_X = mybir.AxisListType.X
P = 128
EPS = 1e-6
NEG = -1e30

D = 1024
KT = D // P
SEQ, NSEQ, DSEQ, PAST = 1024, 8, 8, 1024
PT = SEQ // P
NT = PT + 1
SAMP = NSEQ * DSEQ
TOK = SEQ + SAMP
ROWS = [P] * PT + [SAMP]
DI, HD, NH, NG, DS = 2048, 64, 32, 4, 128
HG = NH // NG
GW = HG * HD
XF = GW // P
CF = XF + 2
CONVF = (DI + 2 * NG * DS) // P
CK = 4
LC = SEQ // P
RAWW = CK - 1 + SEQ + NSEQ * (CK - 1 + DSEQ)
SOFF = CK - 1 + SEQ
TAIL = (CK - 1) * (1 + NSEQ)
AH, KVH, REP = 16, 4, 4
NGR = 3
DIL = (1, 4, 16)
PLE = 256


def shape_constants():
    i = np.arange(P)
    seq = i // DSEQ
    same = seq[:, None] == seq[None, :]
    c = {}
    c["ident"] = np.eye(P)
    c["tri"] = (i[:, None] <= i[None, :])
    c["after"] = (i[:, None] > i[None, :])
    c["tri8"] = (i[:, None] <= i[None, :]) & same
    c["after8"] = (i[:, None] > i[None, :]) & same
    c["same8"] = same
    s = np.arange(NSEQ)
    c["inseq"] = seq[:, None] == s[None, :]
    c["first"] = i[:, None] == DSEQ * s[None, :]
    half = HD // 2
    inv = 1.0 / (10000.0 ** (np.arange(half, dtype=np.float32) / np.float32(half)))
    pos = np.concatenate([np.arange(SEQ), PAST + np.arange(P) % DSEQ]).astype(np.float32)
    ang = pos[:, None] * inv[None, :].astype(np.float32)
    cos = np.cos(ang).reshape(NT, P, half).transpose(1, 0, 2)
    sin = np.sin(ang).reshape(NT, P, half).transpose(1, 0, 2)
    c["cos"] = np.concatenate([cos, cos], -1).reshape(P, -1)
    c["sin"] = np.concatenate([-sin, sin], -1).reshape(P, -1)
    q, k = i[:, None], i[None, :]
    c["win"] = np.concatenate([np.where(k >= q, 0, NEG), np.where(k <= q, 0, NEG)], 1)
    c["pair"] = np.where((k <= q) & (k // 64 == q // 64), 0, NEG)
    t = (i % DSEQ)[:, None]
    new = np.arange(DSEQ)[None, :]
    parts = [np.where(k >= t, 0, NEG)]
    for dil in DIL:
        parts.append(np.where((new <= t) & ((t - new) % dil == 0), 0, NEG))
    for r in range(4):
        parts.append(np.where(((t % 4) == r) & (4 * k + r >= t), 0, NEG))
    for a in range(4):
        parts.append(np.where((2 * a + k // 64) == t, 0, NEG) + 0.0 * k)
    c["smask"] = np.concatenate([p + np.zeros((P, p.shape[1])) for p in parts], 1)
    return {n: np.ascontiguousarray(v, np.float32) for n, v in c.items()}


LAYOUT, _at = {}, 0
for _n, _w in (("ident", P), ("tri", P), ("after", P), ("tri8", P), ("after8", P), ("same8", P),
               ("inseq", NSEQ), ("first", NSEQ), ("cos", NT * HD), ("sin", NT * HD),
               ("win", 2 * P), ("pair", P), ("smask", P + 3 * DSEQ + 8 * P)):
    LAYOUT[_n] = (_at, _w)
    _at += _w
NCONST = _at
NMASK = LAYOUT["cos"][0]


class Chain:

    def __init__(self, eng, sem):
        self.eng, self.sem, self.n, self.i, self.start, self.stride = eng, sem, 0, None, 0, 0

    def enter(self, i, stride):
        self.i, self.start, self.stride = i, self.n, stride

    def leave(self, times):
        assert self.n - self.start == self.stride, (self.n - self.start, self.stride)
        self.n = self.start + times * self.stride
        self.i = None

    def __call__(self, ins):
        ins.then_inc(self.sem, 1)
        self.n += 1
        if self.i is None:
            self.eng.wait_ge(self.sem, self.n)
        else:
            self.eng.wait_ge(self.sem, self.i * self.stride + self.n)


def trunk_kernel(nc, a, o, s):
    outer = ExitStack()
    with outer:
        def sem(name):
            return outer.enter_context(nc.semaphore(name))

        def sb_in(ctx):
            def sb(name, shape, dt=F32):
                return ctx.enter_context(nc.sbuf_tensor(name, shape, dt))
            return sb

        keep = sb_in(outer)
        bank = outer.enter_context(nc.psum_tensor("bank", [P, 8, 512], F32))
        h = keep("h", [P, NT, D])
        uT = keep("uT", [P, KT, TOK])
        cst = keep("cst", [P, NMASK])
        gain = keep("gain", [P, D])
        u = keep("u", [P, 2, D])
        ss = keep("ss", [P, 16])
        ms = keep("ms", [P, 16])
        rstd = keep("rstd", [P, 16])
        mhalf = keep("mhalf", [P, 16])
        square = keep("square", [P, D])

        def con(name, rows=P):
            at, w = LAYOUT[name]
            return cst[0:rows, at:at + w]

        ident = con("ident")

        s1 = ExitStack()
        sb = sb_in(s1)
        wx = sb("wx", [P, 2, KT, P])
        wz = sb("wz", [P, KT, GW])
        wo = sb("wo", [P, XF, D])
        wdt = sb("wdt", [P, KT, NH])
        raw = sb("raw", [P, 2, RAWW])
        xbc = sb("xbc", [P, CF, TOK])
        sct = sb("sct", [P, CONVF, NSEQ * (CK - 1)])
        tail = sb("tail", [P, CONVF, TAIL])
        cw = sb("cw", [P, (CK + 1) * CONVF])
        cwg = sb("cwg", [P, CF, CK + 1])
        vec = sb("vec", [P, 3 * NH])
        dtv = sb("dtv", [P, NT, NH])
        dta = sb("dta", [P, NT, NH])
        ea = sb("ea", [P, NT, NH])
        dend = sb("dend", [P, NT, NH])
        dec = sb("dec", [P, NT, NH])
        nwg = gain[:, 0:GW]
        ones = sb("ones", [P, P])
        xt = sb("xt", [P, GW])
        btok = sb("btok", [P, DS])
        cbm = sb("cbm", [P, P])
        mix = sb("mix", [P, 2, HG * P])
        xdt = sb("xdt", [P, GW])
        xdtd = sb("xdtd", [P, GW])
        y = square[:, GW:2 * GW]
        zs = sb("zs", [P, GW])
        yT = sb("yT", [P, XF, P])
        hT = gain[:, GW:2 * GW]
        ybuf = sb("ybuf", [P, 4])
        bseq = u[0:SAMP, 0, :].rearrange("p (s n) -> p s n", s=NSEQ)
        cseq = u[:, 1, 0:GW].rearrange("p (s t) -> p s t", s=NSEQ)
        dexp = u[0:SAMP, 1, GW:2 * GW]
        st = sb("st", [P, 4, XF, DS])
        h0T = sb("h0T", [P, 2, GW])
        sdec = sb("sdec", [P, XF, NSEQ])
        tiny = xbc[:, 3:5, :].rearrange("p a b -> p (a b)")[:, 0:5 * NT * NH].rearrange("p (a b) -> p a b", a=5)
        cw_rows = xdt[0:(CK + 1) * CONVF, 0:P]
        sc_rows = xbc[0:NSEQ * (CK - 1), 0:3, 0:D]
        tail_rows = xbc[0:TAIL, 0:3, 0:D]
        s1.close()

        ss_ready = sem("ss_ready")
        ms_ready = sem("ms_ready")
        rstd_ready = sem("rstd_ready")
        gain_landed = sem("gain_landed")
        gain_used = sem("gain_used")
        u_ready = sem("u_ready")
        uT_full = sem("uT_full")
        uT_ready = sem("uT_ready")
        section = sem("section")
        names = """res_loaded const_loaded vec_loaded cw_loaded sc_loaded wdt_loaded memset_done
            cwT_full cwT_ready scT_full scT_ready dt_full dt_ready acum_full acum_ready
            wz_landed wo_landed nw_landed xg_full raw_ready conv_done conv_ready
            x_full xt_ready bc_full btok_ready cbm_ready sum_ready seg_full e_ready m_ready z_full z_ready
            xdt_ready xdtd_ready skip_ready yd_full st_full hT_ready gated ssy_ready msy_ready ry_ready yn_ready
            yT_full yT_ready out_full out_added cwg_ready dexp_ready sdec_full sdec_ready bseq_ready cseq_ready
            h0_full h0_ready snew_full snew_ready yo_used fin_full fin_ready fin_stored state_stored tail_full
            tail_ready tail_stored vchain achain waits_passed"""
        q = {n: sem(n) for n in names.split()}
        wx_landed = [sem(f"wx_landed{i}") for i in range(2)]
        st_landed = [sem(f"st_landed{i}") for i in range(4)]

        in_w = a["m_in_w"][0].rearrange("(k p) n -> p k n", p=P)
        out_w = a["m_out_w"][0].rearrange("(k p) n -> p k n", p=P)
        st_in = a["state_ssm"].rearrange("x s h p n -> (x h p) s n")
        st_out = o["ssm_sample"].rearrange("x s h p n -> (x h p) s n")
        st_prompt = o["ssm_prompt"].rearrange("x b h p n -> (x b h p) n")
        XCOL, BCOL, CCOL, DTCOL = DI, 2 * DI, 2 * DI + NG * DS, 2 * DI + 2 * NG * DS

        VSTEPS = 1 + CF * (CK - 1) + 2 + NSEQ + 3 * NT + LC
        block = outer.enter_context(nc.Block())

        def cols(t):
            return slice(t * P, t * P + ROWS[t])

        def bc(ap, rows, n, m):
            return ap.unsqueeze(2).broadcast_to([rows, n, m])

        def over(ap, rows, n, m):
            return ap.unsqueeze(1).broadcast_to([rows, n, m])

        def alone(eng):
            eng.sem_inc(q["waits_passed"], 1)

        def norm_scalar(act, k, squares=True):
            if squares:
                for t in range(NT):
                    r = ROWS[t]
                    act.wait_ge(ss_ready, NT * (rstd_count[k] - 1) + t)
                    act.activation(square[0:r, :], h[0:r, t, :], ACT.Square,
                                   accum_out=ss[0:r, t:t + 1]).then_inc(ss_ready, 1)
            for t in range(NT):
                r = ROWS[t]
                act.wait_ge(uT_full, NT * k + t + 1)
                for half in range(2):
                    b = bank[:, 2 * (t % 2) + half, :].rearrange("p (k r) -> p k r", k=4)[:, :, 0:r]
                    act.copy(uT[:, 4 * half:4 * half + 4, cols(t)], b).then_inc(uT_ready, 1)

        rstd_count = {0: 1, 1: 2, 2: 3, 3: 3, 4: 4}

        def norm_vector(dve, k, squares=True):
            if squares:
                dve.wait_ge(ss_ready, NT * rstd_count[k])
                dve.tensor_scalar(ms[:, 0:NT], ss[:, 0:NT], 1.0 / D, EPS, ALU.mult,
                                  ALU.add).then_inc(ms_ready, 1)
            dve.wait_ge(rstd_ready, rstd_count[k])
            dve.wait_ge(gain_landed, 16 * (k + 1))
            for t in range(NT):
                r = ROWS[t]
                if NT * k + t >= 2:
                    dve.wait_ge(uT_full, NT * k + t - 1)
                dve.scalar_tensor_tensor(u[0:r, t % 2, :], h[0:r, t, :], rstd[0:r, t:t + 1], gain[0:r, :],
                                         ALU.mult, ALU.mult).then_inc(u_ready, 1)

        def norm_gpsimd(pool, k):
            pool.wait_ge(ms_ready, rstd_count[k])
            if k:
                pool.wait_ge(u_ready, NT * k)
            pool.tensor_tensor(rstd[:, 0:NT], ms[:, 0:NT], mhalf[:, 0:NT], ALU.pow).then_inc(rstd_ready, 1)

        def norm_tensor(pe, k):
            for t in range(NT):
                r = ROWS[t]
                pe.wait_ge(u_ready, NT * k + t + 1)
                if t >= 2:
                    pe.wait_ge(uT_ready, 2 * (NT * k + t - 1))
                for f in range(KT):
                    last = pe.transpose(bank[:, 2 * (t % 2) + f // 4, (f % 4) * P:(f % 4) * P + r],
                                        u[0:r, t % 2, f * P:(f + 1) * P], ident[0:r, 0:r])
                last.then_inc(uT_full, 1)

        def load_gain(sp, k, row):
            if k:
                sp.wait_ge(u_ready, NT * k)
            sp.dma_start(gain[:, :], row.broadcast_to([P, D])).then_inc(gain_landed, 16)

        def add_out(dve, c, m):
            r = ROWS[c]
            for half in range(2):
                dve.wait_ge(q["out_full"], m * 2 + half + 1)
                d = h[0:r, c, 512 * half:512 * (half + 1)]
                dve.tensor_tensor(d, d, bank[0:r, 2 + half, :], ALU.add).then_inc(q["out_added"], 1)

        s2 = ExitStack()
        sb = sb_in(s2)
        wg = sb("wg", [P, 2, KT, 512])
        wp = sb("wp", [P, PLE // P, D])
        pin = sb("pin", [P, NT, PLE])
        pT = sb("pT", [P, PLE // P, TOK])
        gs = sb("gs", [P, 2, 512])
        s2.close()
        e = {n: sem("ple_" + n) for n in """w_landed p_landed pT_full pT_ready full gate_ready gated
            added stored""".split()}

        def meet(eng, k):
            eng.drain().then_inc(section, 1)
            eng.wait_ge(section, 5 * k)

        def ple_sync(sp, i, k, last):
            meet(sp, 1 if i == 0 else 5)
            load_gain(sp, k, a["ple_norm_w"][i:i + 1, :])
            sp.dma_start(pin[:, 0:PT, :], a["p_prompt"][i, 0].rearrange("(t p) d -> p t d", p=P)).then_inc(e["p_landed"], 16)
            sp.dma_start(pin[0:SAMP, PT, :], a["p_sample"][i].rearrange("b t d -> (b t) d")).then_inc(e["p_landed"], 16)
            sp.dma_start(wp[:, :, :], a["ple_w"][i].rearrange("(k p) n -> p k n", p=P)).then_inc(e["w_landed"], 16)
            for j in range(2):
                sp.dma_start(wg[:, j, :, :], a["ple_gate_w"][i].rearrange("(k p) n -> p k n", p=P)[:, :, 512 * j:512 * (j + 1)]).then_inc(e["w_landed"], 16)
            if last:
                for t in range(NT):
                    sp.wait_ge(e["added"], 2 * NT * i + NT + t + 1)
                    dst = o["y_prompt"][0, t * P:(t + 1) * P, :] if t < PT else o["y_sample"].rearrange("b t d -> (b t) d")
                    sp.dma_start(dst, h[0:ROWS[t], t, :]).then_inc(e["stored"], 16)
                sp.wait_ge(e["stored"], 16 * NT)

        def ple_scalar(act, i, k):
            meet(act, 1 if i == 0 else 5)
            for t in range(NT):
                r = ROWS[t]
                act.wait_ge(e["pT_full"], NT * i + t + 1)
                act.copy(pT[:, :, cols(t)], bank[:, 4 + t % 2, 0:PLE].rearrange("p (k r) -> p k r", k=2)[:, :, 0:r]).then_inc(e["pT_ready"], 1)
            norm_scalar(act, k)
            with act.Fori(0, 2) as j:
                for t in range(NT):
                    r = ROWS[t]
                    v = j * NT + t
                    act.wait_ge(e["full"], v + (2 * NT * i + 1))
                    act.wait_ge(e["added"], v + 2 * NT * i if t < 2 else v + (2 * NT * i - 1))
                    act.activation(gs[0:r, t % 2, :], bank[0:r, 2 * (t % 3), :], ACT.Sigmoid).then_inc(e["gate_ready"], 1)

        def ple_gpsimd(pool, i, k):
            meet(pool, 1 if i == 0 else 5)
            norm_gpsimd(pool, k)

        def ple_vector(dve, i, k):
            meet(dve, 1 if i == 0 else 5)
            norm_vector(dve, k)
            with dve.Fori(0, 2) as j:
                for t in range(NT):
                    r = ROWS[t]
                    v = j * NT + t
                    g_ = gs[0:r, t % 2, :]
                    dve.wait_ge(e["gate_ready"], v + (2 * NT * i + 1))
                    dve.tensor_tensor(g_, g_, bank[0:r, 2 * (t % 3) + 1, :], ALU.mult).then_inc(e["gated"], 1)
                    dve.wait_ge(e["gated"], v + (2 * NT * i + 1))
                    hv = h[0:r, t, bass.ds(j * 512, 512)]
                    dve.tensor_tensor(hv, hv, g_, ALU.add).then_inc(e["added"], 1)

        def ple_tensor(pe, i, k):
            meet(pe, 1 if i == 0 else 5)
            pe.wait_ge(e["p_landed"], 32 * (i + 1))
            for t in range(NT):
                r = ROWS[t]
                if t > 1:
                    pe.wait_ge(e["pT_ready"], NT * i + t - 1)
                for f in range(PLE // P):
                    last = pe.transpose(bank[:, 4 + t % 2, f * P:f * P + r], pin[0:r, t, f * P:(f + 1) * P], ident[0:r, 0:r])
                last.then_inc(e["pT_full"], 1)
            norm_tensor(pe, k)
            pe.wait_ge(e["pT_ready"], NT * (i + 1))
            pe.wait_ge(e["w_landed"], 48 * (i + 1))
            pe.wait_ge(uT_ready, 2 * NT * (k + 1))
            with pe.Fori(0, 2) as j:
                for t in range(NT):
                    r = ROWS[t]
                    v = j * NT + t
                    pe.wait_ge(e["gated"], v + 2 * NT * i if t < 3 else v + (2 * NT * i - 2))
                    alone(pe)
                    for kk in range(KT):
                        pe.matmul(bank[0:r, 2 * (t % 3), :], uT[:, kk, cols(t)],
                                  wg[:, bass.ds(j, 1), kk, :].rearrange("p a n -> p (a n)"), start=(kk == 0), stop=(kk == KT - 1))
                    for kk in range(PLE // P):
                        last = pe.matmul(bank[0:r, 2 * (t % 3) + 1, :], pT[:, kk, cols(t)], wp[:, kk, bass.ds(j * 512, 512)],
                                         start=(kk == 0), stop=(kk == PLE // P - 1))
                    last.then_inc(e["full"], 1)

        s3 = ExitStack()
        sb = sb_in(s3)
        wr = sb("wr", [P, 2, KT, 512])
        rope = sb("rope", [P, 2, NT, HD])
        tab = sb("tab", [P, 4, NT, HD])
        nw = sb("nw", [P, 2, HD])
        raws = sb("raws", [P, 2, 512])
        sqr = sb("sqr", [P, 2, 512])
        rot = sb("rot", [P, 2, 512])
        swp = sb("swp", [P, 512])
        hs3 = sb("hs3", [P, 3, 8])
        s3.close()
        j3 = {n: sem("proj_" + n) for n in """full raw_ready ms_ready r_ready rot_ready t_landed tab_ready
            kv_out""".split()}
        w3_landed = [sem(f"w3_landed{i}") for i in range(2)]
        stored3 = [sem(f"stored3_{i}") for i in range(2)]
        KVB, QB, GB = 3, 6, 2
        UNITS3 = (KVB + QB + GB) * NT
        kv_flat = s["kv"].rearrange("t c g n -> t (c g n)")
        q_flat = s["q"].rearrange("t g n -> t (g n)")
        kw_src = a["kv_w"].rearrange("(k p) n -> p k n", p=P)
        qw_src = a["a_in_w"][0].rearrange("(k p) n -> p k n", p=P)

        def turn_of(i, times, const):
            return const if i is None else i * times + const

        def blocks3(eng, body, between=lambda: None):
            for b in range(KVB):
                body(None, b, (8, 4, 0)[b], 0)
            between()
            with eng.Fori(0, QB // 2) as i:
                for d in range(2):
                    body(i, KVB + d, 8, 2)
            for b in range(KVB + QB, KVB + QB + GB):
                body(None, b, 0, None)

        def section3_sync(sp):
            meet(sp, 2)
            load_gain(sp, 2, a["kv_norm_w"].unsqueeze(0))
            for j, n in enumerate(("cos", "sin")):
                at, w = LAYOUT[n]
                sp.dma_start(rope[:, j, :, :], a["consts"][:, at:at + w].rearrange("p (t d) -> p t d", t=NT)).then_inc(j3["t_landed"], 16)
            sp.dma_start(nw[:, 0, :], a["k_norm_w"].unsqueeze(0).broadcast_to([P, HD])).then_inc(j3["t_landed"], 16)
            sp.dma_start(nw[:, 1, :], a["a_q_norm_w"].broadcast_to([P, HD])).then_inc(j3["t_landed"], 16)
            sp.dma_start(wr[:, 0, :, :], kw_src[:, :, 0:512]).then_inc(w3_landed[0], 16)

            def body(i, b, m, tb):
                nb = b + 1
                if nb < KVB + QB + GB:
                    sp.wait_ge(j3["full"], turn_of(i, 2 * NT, b * NT))
                    alone(sp)
                    src = kw_src[:, :, 512 * nb:512 * (nb + 1)] if nb < KVB else \
                        qw_src[:, :, bass.ds(turn_of(i, 1024, 512 * (nb - KVB)), 512)]
                    sp.dma_start(wr[:, nb % 2, :, :], src).then_inc(w3_landed[nb % 2], 16)
                for t in range(NT):
                    r = ROWS[t]
                    par = (b * NT + t) % 2
                    sp.wait_ge(j3["rot_ready"], turn_of(i, 2 * NT, b * NT + t + 1))
                    alone(sp)
                    if b < KVB:
                        dst = kv_flat[cols(t), 512 * b:512 * (b + 1)]
                    elif i is None:
                        dst = s["gate"][cols(t), 512 * (b - KVB - QB):512 * (b - KVB - QB + 1)]
                    else:
                        dst = q_flat[cols(t), bass.ds(turn_of(i, 1024, 512 * (b - KVB)), 512)]
                    sp.dma_start(dst, rot[0:r, par, :]).then_inc(stored3[par], 16)

            def between():
                kvn = KVB * NT
                sp.wait_ge(stored3[0], 16 * ((kvn + 1) // 2))
                sp.wait_ge(stored3[1], 16 * (kvn // 2))
                for g in range(NGR):
                    w = min((128, 512, 2048)[g], SEQ)
                    sp.dma_start(o[f"kv_prompt_g{g + 1}"][0].rearrange("t c h d -> t c (h d)"), s["kv"][SEQ - w:SEQ, :, g, :]).then_inc(j3["kv_out"], 16)
                    sp.dma_start(o[f"kv_sample_g{g + 1}"].rearrange("b t c h d -> (b t) c (h d)"), s["kv"][SEQ:TOK, :, g, :]).then_inc(j3["kv_out"], 16)
                load_gain(sp, 3, a["norm_w"][1:2, :])

            blocks3(sp, body, between)
            sp.wait_ge(stored3[0], 16 * ((UNITS3 + 1) // 2))
            sp.wait_ge(stored3[1], 16 * (UNITS3 // 2))
            sp.wait_ge(j3["kv_out"], 16 * 2 * NGR)

        def section3_tensor(pe):
            meet(pe, 2)
            norm_tensor(pe, 2)
            pe.wait_ge(uT_ready, 2 * NT * 3)

            def body(i, b, m, tb):
                pe.wait_ge(w3_landed[b % 2], turn_of(i, 16, 16 * (b // 2 + 1)))
                for t in range(NT):
                    r = ROWS[t]
                    if b or t > 2:
                        pe.wait_ge(j3["raw_ready"], turn_of(i, 2 * NT, b * NT + t - 2))
                    alone(pe)
                    for k in range(KT):
                        last = pe.matmul(bank[0:r, 4 + t % 3, :], uT[:, k, cols(t)], wr[:, b % 2, k, :],
                                         start=(k == 0), stop=(k == KT - 1))
                    last.then_inc(j3["full"], 1)

            def between():
                norm_tensor(pe, 3)
                pe.wait_ge(uT_ready, 2 * NT * 4)

            blocks3(pe, body, between)

        def section3_scalar(act):
            meet(act, 2)
            norm_scalar(act, 2)

            def body(i, b, m, tb):
                for t in range(NT):
                    r = ROWS[t]
                    par = (b * NT + t) % 2
                    act.wait_ge(j3["full"], turn_of(i, 2 * NT, b * NT + t + 1))
                    if b or t > 1:
                        act.wait_ge(j3["rot_ready"], turn_of(i, 2 * NT, b * NT + t - 1))
                    if tb is None:
                        ins = act.activation(raws[0:r, par, :], bank[0:r, 4 + t % 3, :], ACT.Silu)
                    else:
                        ins = act.copy(raws[0:r, par, :], bank[0:r, 4 + t % 3, :])
                    if m:
                        ins = act.activation(sqr[0:r, par, 0:m * HD], bank[0:r, 4 + t % 3, 0:m * HD], ACT.Square)
                    ins.then_inc(j3["raw_ready"], 1)

            blocks3(act, body, lambda: norm_scalar(act, 3, squares=False))

        def section3_gpsimd(pool):
            meet(pool, 2)
            norm_gpsimd(pool, 2)
            count = 0
            for b, m in ((0, 8), (1, 4)):
                for t in range(NT):
                    count += 1
                    pool.wait_ge(j3["ms_ready"], count)
                    pool.tensor_tensor(hs3[0:ROWS[t], 2, 0:m], hs3[0:ROWS[t], 1, 0:m], mhalf[0:ROWS[t], 0:m], ALU.pow).then_inc(j3["r_ready"], 1)
            with pool.Fori(0, QB) as i:
                for t in range(NT):
                    pool.wait_ge(j3["ms_ready"], i * NT + (2 * NT + t + 1))
                    pool.tensor_tensor(hs3[0:ROWS[t], 2, :], hs3[0:ROWS[t], 1, :], mhalf[0:ROWS[t], 0:8], ALU.pow).then_inc(j3["r_ready"], 1)

        def section3_vector(dve, chain):
            meet(dve, 2)
            dve.wait_ge(j3["t_landed"], 64)
            half = HD // 2
            chain(dve.tensor_scalar(nw[:, 1, :], nw[:, 1, :], HD ** -0.5, None, ALU.mult))
            for tb in range(2):
                dve.tensor_tensor(tab[:, 2 * tb, :, :], rope[:, 0, :, :], over(nw[:, tb, :], P, NT, HD), ALU.mult)
                for x in range(2):
                    o_ = slice(x * half, (x + 1) * half)
                    i_ = slice((1 - x) * half, (2 - x) * half)
                    last = dve.tensor_tensor(tab[:, 2 * tb + 1, :, o_], rope[:, 1, :, o_], over(nw[:, tb, i_], P, NT, half), ALU.mult)
            last.then_inc(j3["tab_ready"], 1)
            dve.wait_ge(j3["tab_ready"], 1)
            norm_vector(dve, 2)

            def body(i, b, m, tb):
                for t in range(NT):
                    r = ROWS[t]
                    v0 = b * NT + t
                    par = v0 % 2
                    dve.wait_ge(j3["raw_ready"], turn_of(i, 2 * NT, v0 + 1))
                    if v0 > 1:
                        dve.wait_ge(stored3[par], turn_of(i, 16 * NT, 16 * (v0 // 2)))
                    if m:
                        hv = lambda x: x[0:r, 0:m * HD].rearrange("p (m d) -> p m d", m=m)
                        x, out, sw = hv(raws[:, par, :]), hv(rot[:, par, :]), hv(swp[:, :])
                        chain(dve.tensor_reduce(hs3[0:r, 0, 0:m], hv(sqr[:, par, :]), AX_X, ALU.add))
                        dve.tensor_scalar(hs3[0:r, 1, 0:m], hs3[0:r, 0, 0:m], 1.0 / HD, EPS, ALU.mult, ALU.add).then_inc(j3["ms_ready"], 1)
                        dve.tensor_tensor(out, x, over(tab[0:r, tb, t, :], r, m, HD), ALU.mult)
                        dve.tensor_tensor(sw[:, :, 0:half], x[:, :, half:], over(tab[0:r, tb + 1, t, 0:half], r, m, half), ALU.mult)
                        chain(dve.tensor_tensor(sw[:, :, half:], x[:, :, 0:half], over(tab[0:r, tb + 1, t, half:], r, m, half), ALU.mult))
                        chain(dve.tensor_tensor(out, out, sw, ALU.add))
                        nm = v0 if b < 2 else turn_of(i, 2 * NT, v0 - NT)
                        dve.wait_ge(j3["r_ready"], nm + 1)
                        ins = dve.tensor_tensor(out, out, bc(hs3[0:r, 2, 0:m], r, m, HD), ALU.mult)
                    if m < 8:
                        ins = dve.tensor_copy(rot[0:r, par, m * HD:], raws[0:r, par, m * HD:])
                    ins.then_inc(j3["rot_ready"], 1)
                    if m:
                        dve.wait_ge(j3["rot_ready"], turn_of(i, 2 * NT, v0 + 1))

            def between():
                norm_vector(dve, 3, squares=False)

            for b in range(KVB):
                body(None, b, (8, 4, 0)[b], 0)
            between()
            with dve.Fori(0, QB // 2) as i:
                chain.enter(i, 3 * 2 * NT)
                for d in range(2):
                    body(i, KVB + d, 8, 2)
                chain.leave(QB // 2)
            for b in range(KVB + QB, KVB + QB + GB):
                body(None, b, 0, None)

        s4 = ExitStack()
        sb = sb_in(s4)
        HP = AH // 2
        UN = NGR * PT
        win = sb("win", [P, 2 * P])
        pair = sb("pair", [P, P])
        qn = sb("qn", [P, 2, D])
        kn = sb("kn", [P, 2, KVH * HD])
        kd = sb("kd", [P, KVH, 2, HD])
        vv = sb("vv", [P, 2, 2, KVH * HD])
        kT = sb("kT", [P, 2, KVH, 2, P])
        qT = sb("qT", [P, 2, HP, P])
        sc = sb("sc", [P, 4, 512])
        pT4 = sb("pT4", [P, 2, 512])
        mxs = sb("mxs", [P, 2, 2 * AH])
        nmx = sb("nmx", [P, 2, AH])
        ub = sb("ub", [P, 2, D])
        NTILE = 10
        NEW = NGR * DSEQ
        SW = P + NEW + 8 * P
        smask = sb("smask", [P, SW])
        ck = sb("ck", [P, 2, 9, 2 * KVH * HD])
        nk = sb("nk", [NEW, 2, 2 * KVH * HD])
        ssc = sb("ssc", [P, SW])
        pTs = sb("pTs", [P, NTILE, P])
        qTs = sb("qTs", [P, NGR, 2, P])
        osb = sb("osb", [P, 2, HD])
        qzs = sb("qzs", [P, 2, NGR, 2, P])
        st4 = sb("st4", [P, 8])
        qz = uT[:, :, :].rearrange("p k t -> p (k t)")[:, 0:NSEQ * NGR * 2 * P].rearrange("p (s g a d) -> p s g a d", s=NSEQ, g=NGR, a=2)
        kTs = uT[:, :, :].rearrange("p k t -> p (k t)")[:, NSEQ * NGR * 2 * P:NSEQ * NGR * 2 * P + 2 * SW].rearrange("p (a n) -> p a n", a=2)
        s4.close()
        f4 = {n: sem("att_" + n) for n in """m_landed s_full masked p_ready t_full pt_ready pv_done u_taken tr_full
            tr_ready kd_ready kp_ready zeroed qz_landed os_stored qzs_ready
            ktr_full ktr_ready ss_full ss_masked se_ready rd_ready st_full spt_ready so_full so_ready schain""".split()}
        qk_landed = [sem(f"qk_landed{i}") for i in range(2)]
        v_landed = [sem(f"v_landed{i}") for i in range(2)]
        vp_landed = [sem(f"vp_landed{i}") for i in range(2)]
        ub_stored = [sem(f"ub_stored{i}") for i in range(2)]
        ck_landed = [sem(f"ck_landed{i}") for i in range(2)]

        OWN, FULL = 1, 2

        def head(j, x):
            return 4 * (j // 2) + 2 * x + j % 2

        def units4(eng, body):
            body(None, 0, OWN, None, 0)
            body(None, 1, FULL, OWN, 1)
            with eng.Fori(0, 3) as i:
                body(i, 2, FULL, FULL, 1)
                body(i, 3, FULL, FULL, 2)
            body(None, 8, OWN, FULL, 0)
            body(None, 9, FULL, OWN, 5)
            with eng.Fori(0, 3) as i:
                body(i, 10, OWN, FULL, 0)
                body(i, 11, FULL, OWN, 6)
            body(None, 16, OWN, FULL, 0)
            body(None, 17, OWN, OWN, 0)
            with eng.Fori(0, 2) as i:
                body(i, 18, OWN, OWN, 0)
                body(i, 19, OWN, OWN, 0)
            body(None, 22, OWN, OWN, 0)
            body(None, 23, OWN, OWN, 0)

        def sequences(eng, body):
            with eng.Fori(0, NSEQ // 2 - 1) as i:
                for d in range(2):
                    body(i, d)
            for d in (NSEQ - 2, NSEQ - 1):
                body(None, d)

        def rows4(table, i, un, hi):
            g = un // PT
            if g == 0:
                return table[bass.ds(turn_of(i, 2 * P, un * P + 64 * hi), 64), :]
            j = un - g * PT
            if g == 1:
                x = table[0:SEQ, :].rearrange("(p r) n -> r p n", r=4)
                res, at = turn_of(i, 1, j // 2), (j % 2) * P + 64 * hi
            else:
                x = table[0:SEQ, :].rearrange("(p r) n -> r p n", r=16)
                res, at = turn_of(i, 4, 2 * j + hi), 0
            return x[bass.ds(res, 1), at:at + 64, :].rearrange("r p n -> (r p) n")

        def section4_sync(sp):
            meet(sp, 3)
            for tile, name in ((win, "win"), (pair, "pair"), (smask, "smask")):
                at, w = LAYOUT[name]
                sp.dma_start(tile[:, :], a["consts"][:, at:at + w]).then_inc(f4["m_landed"], 16)

            def body(i, un, kind, before, nth):
                g, sl = un // PT, un % 2
                if un > 1:
                    sp.wait_ge(f4["tr_full"], turn_of(i, 6, 3 * (un - 1)))
                    alone(sp)
                    sp.wait_ge(f4["kd_ready"], turn_of(i, 2, un - 1))
                    alone(sp)
                    sp.wait_ge(f4["pv_done"], turn_of(i, 16, 8 * (un - 1)))
                alone(sp)
                for hi in range(2):
                    ps = slice(64 * hi, 64 * hi + 64)
                    sp.dma_start(qn[ps, sl, :], rows4(s["q"][:, g, :], i, un, hi)).then_inc(qk_landed[sl], 16)
                    sp.dma_start(kn[ps, sl, :], rows4(s["kv"][:, 0, g, :], i, un, hi)).then_inc(qk_landed[sl], 16)
                    sp.dma_start(vv[ps, sl, 1, :], rows4(s["kv"][:, 1, g, :], i, un, hi)).then_inc(v_landed[sl], 16)
                    if kind == FULL:
                        sp.dma_start(vv[ps, sl, 0, :], rows4(s["kv"][:, 1, g, :], i, un - 1, hi)).then_inc(vp_landed[sl], 16)

            units4(sp, body)
            sp.wait_ge(f4["zeroed"], 1)
            for x in range(AH):
                kv = x // REP
                for g in range(NGR):
                    src = s["q"][SEQ:TOK, g, x * HD:(x + 1) * HD].rearrange("(s t) d -> t s d", t=DSEQ)
                    sp.dma_start(qz[x * DSEQ:(x + 1) * DSEQ, :, g, kv // 2, (kv % 2) * HD:(kv % 2 + 1) * HD], src).then_inc(f4["qz_landed"], 16)
            caches = [a[f"cache_kv_g{g}"].rearrange("s t c h d -> s t (c h d)") for g in (1, 2, 3)]

            def load_sequence(i, d):
                sl, one = d % 2, bass.ds(turn_of(i, 2, d), 1)
                c1, c2, c3 = (c[one].rearrange("s t n -> (s t) n") for c in caches)
                sp.dma_start(ck[:, sl, 0, :], c1).then_inc(ck_landed[sl], 16)
                sp.dma_start(ck[:, sl, 1:5, :], c2.rearrange("(i r) n -> i r n", r=4)).then_inc(ck_landed[sl], 16)
                for hi in range(2):
                    sp.dma_start(ck[64 * hi:64 * hi + 64, sl, 5:9, :],
                                 c3.rearrange("(i r) n -> i r n", r=16)[:, hi:8:2, :]).then_inc(ck_landed[sl], 16)
                for g in range(NGR):
                    sp.dma_start(nk[g * DSEQ:(g + 1) * DSEQ, sl, :].rearrange("t (c n) -> t c n", c=2),
                                 s["kv"][bass.ds(turn_of(i, 2 * DSEQ, SEQ + d * DSEQ), DSEQ), :, g, :]).then_inc(ck_landed[sl], 16)

            load_sequence(None, 0)
            load_sequence(None, 1)

            def sample(i, d):
                if d < NSEQ - 2:
                    sp.wait_ge(f4["so_full"], turn_of(i, 2, d + 1))
                    alone(sp)
                    load_sequence(i, d + 2)

            sequences(sp, sample)

        def section4_gpsimd(pool):
            meet(pool, 3)
            pool.memset(qz, 0.0).then_inc(f4["zeroed"], 1)

            def double(i, un):
                sl = un % 2
                pool.wait_ge(qk_landed[sl], turn_of(i, 64, 64 * (un // 2 + 1)))
                if un:
                    pool.wait_ge(f4["tr_full"], turn_of(i, 6, 3 * (un - 1) + 1))
                alone(pool)
                pool.tensor_copy(kd[:, :, :, :], kn[:, sl, :].rearrange("p (h d) -> p h d", h=KVH).unsqueeze(2).broadcast_to([P, KVH, 2, HD])).then_inc(f4["kd_ready"], 1)

            double(None, 0)

            def body(i, un, kind, before, nth):
                if un < UN - 1:
                    nx = un + 1
                    double(i, nx)
                    pool.wait_ge(f4["tr_ready"], turn_of(i, 6, 3 * un + 1))
                    pool.wait_ge(f4["s_full"], turn_of(i, 16, 8 * un))
                    alone(pool)
                    pool.tensor_copy(kT[:, nx % 2, :, 0, :], kT[:, un % 2, :, 1, :]).then_inc(f4["kp_ready"], 1)

            units4(pool, body)
            pool.wait_ge(f4["qz_landed"], 16 * AH * NGR)

            def pick(i, d):
                if d > 1 or i is not None:
                    pool.wait_ge(f4["ktr_full"], turn_of(i, 14, 7 * max(0, d - 1)))
                alone(pool)
                pool.tensor_copy(qzs[:, d % 2, :, :, :], qz[:, bass.ds(turn_of(i, 2, d), 1), :, :, :].rearrange("p s g a d -> p (s g) a d")).then_inc(f4["qzs_ready"], 1)

            sequences(pool, pick)

        def section4_scalar(act):
            meet(act, 3)

            def take(i, un, part):
                sl = un % 2
                act.wait_ge(f4["tr_full"], turn_of(i, 6, 3 * un + part + 1))
                if part == 0:
                    if un:
                        act.wait_ge(f4["kp_ready"], turn_of(i, 2, un - 1))
                    act.copy(kT[:, sl, :, 1, :], bank[:, 6, :].rearrange("p (h n) -> p h n", h=KVH)).then_inc(f4["tr_ready"], 1)
                else:
                    act.copy(qT[:, sl, 4 * (part - 1):4 * part, :], bank[:, 8 - part, :].rearrange("p (h n) -> p h n", h=4)).then_inc(f4["tr_ready"], 1)

            def hand_out(i, un):
                g, sl = un // PT, un % 2
                act.wait_ge(f4["pv_done"], turn_of(i, 16, 8 * (un + 1)))
                if un > 1:
                    act.wait_ge(ub_stored[sl], turn_of(i, 64, 64 * (un // 2)))
                act.copy(ub[:, sl, :].rearrange("p (b n) -> p b n", b=2), bank[:, 4:6, :]).then_inc(f4["u_taken"], 1)
                act.wait_ge(f4["u_taken"], turn_of(i, 2, un + 1))
                for hi in range(2):
                    ps = slice(64 * hi, 64 * hi + 64)
                    act.dma_start(rows4(s["u"][g], i, un, hi), ub[ps, sl, :]).then_inc(ub_stored[sl], 16)
                    act.dma_start(rows4(s["ms"][g], i, un, hi), mxs[ps, sl, :]).then_inc(ub_stored[sl], 16)

            for part in range(3):
                take(None, 0, part)

            def body(i, un, kind, before, nth):
                sl = un % 2
                n = kind * P
                for j in range(HP):
                    st0 = HP * un + j
                    act.wait_ge(f4["masked"], turn_of(i, 16, st0 + 1))
                    if j == 0 and un > 1:
                        act.wait_ge(ub_stored[sl], turn_of(i, 64, 64 * (un // 2)))
                    for x in range(2):
                        v = sc[:, st0 % 4, 256 * x:256 * x + n]
                        last = act.activation(v, v, ACT.Exp, bias=nmx[:, sl, head(j, x):head(j, x) + 1],
                                              accum_out=mxs[:, sl, AH + head(j, x):AH + head(j, x) + 1])
                    last.then_inc(f4["p_ready"], 1)
                    if j == 2 and un:
                        hand_out(i, un - 1)
                    if j in (3, 5, 7) and un < UN - 1:
                        take(i, un + 1, (j - 3) // 2)

            units4(act, body)
            hand_out(None, UN - 1)

            def turned(i, d, k):
                act.wait_ge(f4["ktr_full"], turn_of(i, 14, 7 * d + k + 1))
                b = bank[:, 6 + (7 * d + k) % 2, :]
                if k < 5:
                    kTs_copy(act, k, b)
                elif k == 5:
                    act.copy(qTs[:, 0:2, :, :].rearrange("p g a n -> p (g a) n"), b.rearrange("p (x n) -> p x n", x=4)).then_inc(f4["ktr_ready"], 1)
                else:
                    act.copy(qTs[:, 2, :, :], b[:, 0:2 * P].rearrange("p (x n) -> p x n", x=2)).then_inc(f4["ktr_ready"], 1)

            def kTs_copy(act, k, b):
                if k < 4:
                    at = P + NEW + 2 * k * P
                    act.copy(kTs[:, :, at:at + 2 * P], b.rearrange("p (a n) -> p a n", a=2)).then_inc(f4["ktr_ready"], 1)
                else:
                    act.copy(kTs[:, :, 0:P + NEW], b.rearrange("p (a n) -> p a n", a=2)[:, :, 0:P + NEW]).then_inc(f4["ktr_ready"], 1)

            for k in range(7):
                turned(None, 0, k)

            def sample(i, d):
                act.wait_ge(f4["ss_masked"], turn_of(i, 2, d + 1))
                act.activation(ssc[:, :], ssc[:, :], ACT.Exp, bias=st4[:, 4:5], accum_out=st4[:, 5:6]).then_inc(f4["se_ready"], 1)
                if d < NSEQ - 1:
                    for k in range(7):
                        turned(i, d + 1, k)
                act.wait_ge(f4["rd_ready"], turn_of(i, 2, d + 1))
                act.wait_ge(f4["so_full"], turn_of(i, 2, d + 1))
                act.wait_ge(f4["os_stored"], turn_of(i, 32 * AH, 16 * AH * d))
                for kv in range(KVH):
                    ps = slice(32 * kv, 32 * kv + 32)
                    last = act.activation(osb[ps, d % 2, :], bank[ps, 0, kv * HD:(kv + 1) * HD], ACT.Copy, scale=st4[ps, 6:7])
                last.then_inc(f4["so_ready"], 1)
                act.wait_ge(f4["so_ready"], turn_of(i, 2, d + 1))
                for x in range(AH):
                    act.dma_start(s["os"][bass.ds(turn_of(i, 2 * DSEQ, d * DSEQ), DSEQ), x * HD:(x + 1) * HD],
                                  osb[x * DSEQ:(x + 1) * DSEQ, d % 2, :]).then_inc(f4["os_stored"], 16)

            sequences(act, sample)
            act.wait_ge(f4["os_stored"], 16 * AH * NSEQ)
            act.wait_ge(ub_stored[0], 64 * (UN // 2))
            act.wait_ge(ub_stored[1], 64 * (UN // 2))

        def section4_vector(dve, chain):
            meet(dve, 3)
            dve.wait_ge(f4["m_landed"], 48)

            def evacuate(i, st0, kind):
                dve.wait_ge(f4["t_full"], turn_of(i, 16, st0 + 1))
                if st0 > 1:
                    dve.wait_ge(f4["pv_done"], turn_of(i, 16, st0 - 1))
                dve.tensor_copy(pT4[:, st0 % 2, 0:2 * kind * P], bank[:, 2 + st0 % 2, 0:2 * kind * P]).then_inc(f4["pt_ready"], 1)

            state = {}

            def body(i, un, kind, before, nth):
                sl, n = un % 2, kind * P
                mask = pair[:, :] if un >= 2 * PT else win[:, 2 * P - n:2 * P]
                if i is not None and un % 2 == 0:
                    chain.enter(i, 2 * HP)
                for j in range(HP):
                    st0 = HP * un + j
                    dve.wait_ge(f4["s_full"], turn_of(i, 16, st0 + 1))
                    if st0 > 3:
                        dve.wait_ge(f4["t_full"], turn_of(i, 16, st0 - 3))
                    if j == 0 and un > 1:
                        dve.wait_ge(ub_stored[sl], turn_of(i, 64, 64 * (un // 2)))
                    alone(dve)
                    for x in range(2):
                        last = dve.tensor_tensor_reduce(sc[:, st0 % 4, 256 * x:256 * x + n], bank[:, st0 % 2, 256 * x:256 * x + n], mask,
                                                        1.0, -3e38, ALU.add, ALU.max, mxs[:, sl, head(j, x):head(j, x) + 1])
                    chain(last)
                    two = slice(head(j, 0), head(j, 1) + 1, 2)
                    dve.tensor_scalar(nmx[:, sl, two], mxs[:, sl, two], -1.0, None, ALU.mult).then_inc(f4["masked"], 1)
                    if st0:
                        evacuate(i, st0 - 1, kind if j else before)
                if i is not None and un % 2 == 1:
                    chain.leave({3: 3, 11: 3, 19: 2}[un])

            units4(dve, body)
            evacuate(None, HP * UN - 1, OWN)

            def sample(i, d):
                dve.wait_ge(f4["ss_full"], turn_of(i, 2, d + 1))
                dve.wait_ge(f4["st_full"], turn_of(i, 6, 3 * d))
                dve.wait_ge(f4["so_ready"], turn_of(i, 2, d))
                alone(dve)
                for b, (c0, c1) in enumerate(((0, P + NEW), (P + NEW, P + NEW + 512), (P + NEW + 512, SW))):
                    last = dve.tensor_tensor_reduce(ssc[:, c0:c1], bank[:, b, 0:c1 - c0], smask[:, c0:c1], 1.0, -3e38,
                                                    ALU.add, ALU.max, st4[:, b:b + 1])
                last.then_inc(f4["schain"], 1)
                dve.wait_ge(f4["schain"], turn_of(i, 4, 2 * d + 1))
                dve.tensor_reduce(st4[:, 3:4], st4[:, 0:3], AX_X, ALU.max).then_inc(f4["schain"], 1)
                dve.wait_ge(f4["schain"], turn_of(i, 4, 2 * d + 2))
                dve.tensor_scalar(st4[:, 4:5], st4[:, 3:4], -1.0, None, ALU.mult).then_inc(f4["ss_masked"], 1)
                dve.wait_ge(f4["se_ready"], turn_of(i, 2, d + 1))
                dve.reciprocal(st4[:, 6:7], st4[:, 5:6]).then_inc(f4["rd_ready"], 1)
                for b in range(3):
                    dve.wait_ge(f4["st_full"], turn_of(i, 6, 3 * d + b + 1))
                    dve.wait_ge(f4["so_full"], turn_of(i, 2, d))
                    if b < 2:
                        ins = dve.tensor_copy(pTs[:, 2 + 4 * b:6 + 4 * b, :].rearrange("p x n -> p (x n)"), bank[:, 3 + b, :])
                    else:
                        dve.tensor_copy(pTs[:, 0, :], bank[:, 5, 0:P])
                        ins = dve.tensor_copy(pTs[0:NEW, 1, :], bank[0:NEW, 5, P:2 * P])
                    ins.then_inc(f4["spt_ready"], 1)

            sequences(dve, sample)

        def section4_tensor(pe):
            meet(pe, 3)

            def turn(i, un, part):
                sl = un % 2
                if part == 0:
                    pe.wait_ge(f4["kd_ready"], turn_of(i, 2, un + 1))
                    if un:
                        pe.wait_ge(f4["tr_ready"], turn_of(i, 6, 3 * un))
                    for x in range(KVH):
                        last = pe.transpose(bank[:, 6, x * P:(x + 1) * P], kd[:, x, :, :].rearrange("p a d -> p (a d)"), ident)
                else:
                    if part == 1:
                        pe.wait_ge(qk_landed[sl], turn_of(i, 64, 64 * (un // 2 + 1)))
                    else:
                        pe.wait_ge(f4["tr_ready"], turn_of(i, 6, 3 * un + 1))
                    for x in range(4):
                        f = 4 * (part - 1) + x
                        last = pe.transpose(bank[:, 8 - part, x * P:(x + 1) * P], qn[:, sl, f * P:(f + 1) * P], ident)
                last.then_inc(f4["tr_full"], 1)

            def turn_scores(i, st0, kind):
                pe.wait_ge(f4["p_ready"], turn_of(i, 16, st0 + 1))
                if st0 > 1:
                    pe.wait_ge(f4["pt_ready"], turn_of(i, 16, st0 - 1))
                for x in range(2):
                    for k in range(kind):
                        last = pe.transpose(bank[:, 2 + st0 % 2, (x * kind + k) * P:(x * kind + k + 1) * P],
                                            sc[:, st0 % 4, 256 * x + k * P:256 * x + (k + 1) * P], ident)
                last.then_inc(f4["t_full"], 1)

            def values(i, un, j, kind, nth):
                st0 = HP * un + j
                sl = un % 2
                pe.wait_ge(f4["pt_ready"], turn_of(i, 16, st0 + 1))
                if j == 0:
                    pe.wait_ge(v_landed[sl], turn_of(i, 32, 32 * (un // 2 + 1)))
                    if kind == FULL:
                        pe.wait_ge(vp_landed[sl], turn_of(i, 32, 32 * nth))
                    pe.wait_ge(f4["u_taken"], turn_of(i, 2, un))
                for x in range(2):
                    hd = head(j, x)
                    for k in range(kind):
                        last = pe.matmul(bank[:, 4 + hd // 8, (hd % 8) * HD:(hd % 8 + 1) * HD],
                                         pT4[:, st0 % 2, (x * kind + k) * P:(x * kind + k + 1) * P],
                                         vv[:, sl, k + 2 - kind, (j // 2) * HD:(j // 2 + 1) * HD], start=(k == 0), stop=(k == kind - 1))
                last.then_inc(f4["pv_done"], 1)

            for part in range(3):
                turn(None, 0, part)

            def body(i, un, kind, before, nth):
                sl, n = un % 2, kind * P
                pe.wait_ge(f4["tr_ready"], turn_of(i, 6, 3 * (un + 1)))
                if un:
                    pe.wait_ge(f4["kp_ready"], turn_of(i, 2, un))
                for j in range(HP):
                    st0 = HP * un + j
                    if st0 > 1:
                        pe.wait_ge(f4["masked"], turn_of(i, 16, st0 - 1))
                    for x in range(2):
                        hs_ = slice(64 * (j % 2), 64 * (j % 2) + 64)
                        last = pe.matmul(bank[:, st0 % 2, 256 * x:256 * x + n], qT[hs_, sl, head(j, x) // 2, :],
                                         kT[hs_, sl, j // 2, 2 - kind:2, :].rearrange("p a n -> p (a n)"), start=True, stop=True)
                    last.then_inc(f4["s_full"], 1)
                    if st0:
                        turn_scores(i, st0 - 1, kind if j else before)
                    if st0 > 1:
                        if j > 1:
                            values(i, un, j - 2, kind, nth)
                        else:
                            values(i, un - 1, j + HP - 2, before, 0)
                    if j in (2, 4, 6) and un < UN - 1:
                        turn(i, un + 1, j // 2 - 1)

            units4(pe, body)
            turn_scores(None, HP * UN - 1, OWN)
            values(None, UN - 1, HP - 2, OWN, 0)
            values(None, UN - 1, HP - 1, OWN, 0)

            def turn_keys(i, d):
                sl = d % 2
                pe.wait_ge(ck_landed[sl], turn_of(i, 112, 112 * (d // 2 + 1)))
                for k in range(7):
                    n0 = 7 * d + k
                    if n0 > 1:
                        pe.wait_ge(f4["ktr_ready"], turn_of(i, 14, n0 - 1))
                    b = bank[:, 6 + n0 % 2, :]
                    if k < 4:
                        for x in range(2):
                            for pr in range(2):
                                last = pe.transpose(b[:, (2 * pr + x) * P:(2 * pr + x + 1) * P], ck[:, sl, 1 + 2 * k + x, pr * P:(pr + 1) * P], ident)
                    elif k == 4:
                        for pr in range(2):
                            pe.transpose(b[:, 2 * pr * P:(2 * pr + 1) * P], ck[:, sl, 0, pr * P:(pr + 1) * P], ident)
                            last = pe.transpose(b[:, (2 * pr + 1) * P:(2 * pr + 1) * P + NEW], nk[:, sl, pr * P:(pr + 1) * P], ident[0:NEW, 0:NEW])
                    else:
                        if k == 5:
                            pe.wait_ge(f4["qzs_ready"], turn_of(i, 2, d + 1))
                        for x in range(4 if k == 5 else 2):
                            g = 2 * (k - 5) + x // 2
                            last = pe.transpose(b[:, x * P:(x + 1) * P], qzs[:, sl, g, x % 2, :], ident)
                    last.then_inc(f4["ktr_full"], 1)

            def sample(i, d):
                sl = d % 2
                pe.wait_ge(f4["ktr_ready"], turn_of(i, 14, 7 * (d + 1)))
                pe.wait_ge(f4["so_ready"], turn_of(i, 2, d))
                pe.wait_ge(f4["ss_masked"], turn_of(i, 2, d))
                new = [(g, 0, P + g * DSEQ, P + (g + 1) * DSEQ, P + g * DSEQ) for g in range(NGR)]
                for g, b, c0, c1, at in [(0, 0, 0, P, 0)] + new + [(1, 1, P + NEW, P + NEW + 512, 0), (2, 2, P + NEW + 512, SW, 0)]:
                    for pr in range(2):
                        last = pe.matmul(bank[:, b, at:at + c1 - c0], qTs[:, g, pr, :], kTs[:, pr, c0:c1], start=(pr == 0), stop=(pr == 1))
                last.then_inc(f4["ss_full"], 1)
                if d < NSEQ - 1:
                    turn_keys(i, d + 1)
                pe.wait_ge(f4["se_ready"], turn_of(i, 2, d + 1))
                pe.wait_ge(f4["spt_ready"], turn_of(i, 6, 3 * d))
                for b in range(2):
                    for x in range(4):
                        at = P + NEW + (4 * b + x) * P
                        last = pe.transpose(bank[:, 3 + b, x * P:(x + 1) * P], ssc[:, at:at + P], ident)
                    last.then_inc(f4["st_full"], 1)
                pe.transpose(bank[:, 5, 0:P], ssc[:, 0:P], ident)
                pe.transpose(bank[0:NEW, 5, P:2 * P], ssc[:, P:P + NEW], ident).then_inc(f4["st_full"], 1)
                pe.wait_ge(f4["spt_ready"], turn_of(i, 6, 3 * (d + 1)))
                vals = [ck[:, sl, 0, KVH * HD:]] + [nk[:, sl, KVH * HD:]] + [ck[:, sl, 1 + x, KVH * HD:] for x in range(8)]
                for x, v in enumerate(vals):
                    r = NEW if x == 1 else P
                    last = pe.matmul(bank[:, 0, 0:KVH * HD], pTs[0:r, x, :], v, start=(x == 0), stop=(x == NTILE - 1))
                last.then_inc(f4["so_full"], 1)

            turn_keys(None, 0)
            sequences(pe, sample)

        s5 = ExitStack()
        sb = sb_in(s5)
        wo5 = sb("wo5", [P, KT, D])
        u3 = sb("u3", [P, 2, NGR, D])
        m3 = sb("m3", [P, 2, NGR, 2 * AH])
        gate = sb("gate", [P, 2, D])
        wts = sb("wts", [P, 5, NGR, AH])
        y5 = sb("y5", [P, 2, D])
        yT5 = sb("yT5", [P, 2, KT, P])
        s5.close()
        f5 = {n: sem("last_" + n) for n in """w_landed e_in e_ready w_ready third y_ready t_full t_ready
            full added""".split()}
        in5 = [sem(f"in5_{i}") for i in range(2)]

        def tiles5(eng, body):
            with eng.Fori(0, PT // 2) as i:
                for t in range(2):
                    body(i, t)
            body(None, PT)

        def section5_sync(sp):
            meet(sp, 4)
            ow = a["a_out_w"][0].rearrange("(k p) n -> p k n", p=P)
            sp.dma_start(wo5[:, :, :], ow).then_inc(f5["w_landed"], 16)

            def body(i, t):
                sl, r = t % 2, ROWS[t]
                rows = bass.ds(turn_of(i, 2 * P, t * P), r)
                sp.wait_ge(f5["y_ready"], turn_of(i, 2, 0) if t < 2 else PT)
                alone(sp)
                sp.dma_start(gate[0:r, sl, :], s["gate"][rows, :]).then_inc(in5[sl], 16)
                if t < PT:
                    for g in range(NGR):
                        sp.dma_start(u3[:, sl, g, :], s["u"][g][rows, :]).then_inc(in5[sl], 16)
                        sp.dma_start(m3[:, sl, g, :], s["ms"][g][rows, :]).then_inc(in5[sl], 16)
                else:
                    sp.wait_ge(f5["t_full"], PT)
                    sp.dma_start(y5[0:r, sl, :], s["os"]).then_inc(in5[sl], 16)

            tiles5(sp, body)

        def section5_gpsimd(pool):
            meet(pool, 4)

            def body(i, t):
                if t == PT:
                    return
                pool.wait_ge(f5["w_ready"], turn_of(i, 2, t + 1))
                v = u3[:, t % 2, 2, :].rearrange("p (h d) -> p h d", h=AH)
                pool.tensor_tensor(v, v, bc(wts[:, 4, 2, :], P, AH, HD), ALU.mult).then_inc(f5["third"], 1)

            tiles5(pool, body)

        def section5_scalar(act):
            meet(act, 4)

            def body(i, t):
                sl, r = t % 2, ROWS[t]
                if t < PT:
                    act.wait_ge(f5["e_in"], turn_of(i, 2, t + 1))
                    act.activation(wts[:, 1, :, :], wts[:, 0, :, :], ACT.Exp).then_inc(f5["e_ready"], 1)
                act.wait_ge(f5["t_full"], turn_of(i, 2, t + 1))
                for half in range(2):
                    b = bank[:, 2 * sl + half, :].rearrange("p (k n) -> p k n", k=4)[:, :, 0:r]
                    last = act.copy(yT5[:, sl, 4 * half:4 * half + 4, 0:r], b)
                last.then_inc(f5["t_ready"], 1)

            tiles5(act, body)

        def section5_vector(dve, chain):
            meet(dve, 4)

            def finish(i, t):
                sl, r = t % 2, ROWS[t]
                dve.wait_ge(f5["full"], turn_of(i, 2, t + 1))
                for half in range(2):
                    hv = h[0:r, bass.ds(turn_of(i, 2, t), 1), 512 * half:512 * (half + 1)].rearrange("p t n -> p (t n)")
                    last = dve.tensor_tensor(hv, hv, bank[0:r, 4 + 2 * sl + half, :], ALU.add)
                last.then_inc(f5["added"], 1)

            def body(i, t):
                sl, r = t % 2, ROWS[t]
                if t == PT:
                    dve.wait_ge(in5[0], 16 * 7 * (PT // 2) + 32)
                    dve.tensor_tensor(y5[0:r, sl, :], y5[0:r, sl, :], gate[0:r, sl, :], ALU.mult).then_inc(f5["y_ready"], 1)
                else:
                    dve.wait_ge(in5[sl], turn_of(i, 112, 112))
                    mx = lambda g: m3[:, sl, g, 0:AH]
                    top = wts[:, 2, 0, :]
                    chain(dve.tensor_tensor(top, mx(0), mx(1), ALU.max))
                    chain(dve.tensor_tensor(top, top, mx(2), ALU.max))
                    dve.tensor_tensor(wts[:, 0, :, :], m3[:, sl, :, 0:AH], over(top, P, NGR, AH), ALU.subtract).then_inc(f5["e_in"], 1)
                    dve.wait_ge(f5["e_ready"], turn_of(i, 2, t + 1))
                    chain(dve.tensor_tensor(wts[:, 3, :, :], wts[:, 1, :, :], m3[:, sl, :, AH:], ALU.mult))
                    chain(dve.tensor_tensor(top, wts[:, 3, 0, :], wts[:, 3, 1, :], ALU.add))
                    chain(dve.tensor_tensor(top, top, wts[:, 3, 2, :], ALU.add))
                    chain(dve.reciprocal(top, top))
                    dve.wait_ge(f5["third"], turn_of(i, 2, t))
                    dve.tensor_tensor(wts[:, 4, :, :], wts[:, 1, :, :], over(top, P, NGR, AH), ALU.mult).then_inc(f5["w_ready"], 1)
                    dve.wait_ge(f5["w_ready"], turn_of(i, 2, t + 1))
                    uv = lambda g: u3[:, sl, g, :].rearrange("p (h d) -> p h d", h=AH)
                    yv = y5[:, sl, :]
                    if t < 2:
                        dve.wait_ge(f5["t_full"], turn_of(i, 2, 0))
                    dve.tensor_tensor(yv.rearrange("p (h d) -> p h d", h=AH), uv(0), bc(wts[:, 4, 0, :], P, AH, HD), ALU.mult)
                    chain(dve.tensor_tensor(uv(1), uv(1), bc(wts[:, 4, 1, :], P, AH, HD), ALU.mult))
                    chain(dve.tensor_tensor(yv, yv, u3[:, sl, 1, :], ALU.add))
                    dve.wait_ge(f5["third"], turn_of(i, 2, t + 1))
                    chain(dve.tensor_tensor(yv, yv, u3[:, sl, 2, :], ALU.add))
                    dve.tensor_tensor(yv, yv, gate[:, sl, :], ALU.mult).then_inc(f5["y_ready"], 1)

            with dve.Fori(0, PT // 2) as i:
                chain.enter(i, 18)
                body(i, 0)
                body(i, 1)
                finish(i, 0)
                finish(i, 1)
                chain.leave(PT // 2)
            body(None, PT)
            finish(None, PT)

        def section5_tensor(pe):
            meet(pe, 4)

            def body(i, t):
                sl, r = t % 2, ROWS[t]
                pe.wait_ge(f5["y_ready"], turn_of(i, 2, t + 1))
                pe.wait_ge(f5["t_ready"], turn_of(i, 2, max(0, t - 1)))
                for f in range(KT):
                    last = pe.transpose(bank[:, 2 * sl + f // 4, (f % 4) * P:(f % 4) * P + r], y5[0:r, sl, f * P:(f + 1) * P], ident[0:r, 0:r])
                last.then_inc(f5["t_full"], 1)
                pe.wait_ge(f5["t_ready"], turn_of(i, 2, t + 1))
                pe.wait_ge(f5["w_landed"], 16)
                pe.wait_ge(f5["added"], turn_of(i, 2, 0) if t < 2 else PT)
                for half in range(2):
                    for k in range(KT):
                        last = pe.matmul(bank[0:r, 4 + 2 * sl + half, :], yT5[:, sl, k, 0:r], wo5[:, k, 512 * half:512 * (half + 1)],
                                         start=(k == 0), stop=(k == KT - 1))
                last.then_inc(f5["full"], 1)

            tiles5(pe, body)


        @block.sync
        def _(sp):
            sp.dma_start(h[:, 0:PT, :], a["x_prompt"][0].rearrange("(t p) d -> p t d", p=P)).then_inc(q["res_loaded"], 16)
            sp.dma_start(h[0:SAMP, PT, :], a["x_sample"].rearrange("b t d -> (b t) d")).then_inc(q["res_loaded"], 16)
            load_gain(sp, 0, a["norm_w"][0:1, :])
            sp.dma_start(cst[:, :], a["consts"][:, 0:NMASK]).then_inc(q["const_loaded"], 16)
            sp.dma_start(wdt[:, :, :], in_w[:, :, DTCOL:DTCOL + NH]).then_inc(q["wdt_loaded"], 16)
            for j, n in enumerate(("m_dt_bias", "m_A_log", "m_D")):
                sp.dma_start(vec[:, j * NH:(j + 1) * NH], a[n].broadcast_to([P, NH])).then_inc(q["vec_loaded"], 16)
            sp.dma_start(cw_rows[0:CK * CONVF, :], a["m_conv_w"][0].rearrange("k (f p) -> (k f) p", p=P)).then_inc(q["cw_loaded"], 16)
            sp.dma_start(cw_rows[CK * CONVF:(CK + 1) * CONVF, :], a["m_conv_b"][0].rearrange("(f p) -> f p", p=P)).then_inc(q["cw_loaded"], 16)
            sp.dma_start(sc_rows, a["state_conv"].rearrange("x s k (c n) -> (x s k) c n", c=3)).then_inc(q["sc_loaded"], 16)
            with sp.Fori(0, NG) as g:
                for f in range(CF):
                    col = [g * GW + XCOL + f * P, g * DS + BCOL, g * DS + CCOL][max(0, f - XF + 1)]
                    sp.wait_ge(q["xg_full"], g * CF + max(0, f - 1))
                    alone(sp)
                    sp.dma_start(wx[:, f % 2, :, :], in_w[:, :, bass.ds(col, P)]).then_inc(wx_landed[f % 2], 16)
                    if f == 2:
                        sp.wait_ge(q["z_full"], g * NT)
                        alone(sp)
                        sp.dma_start(wz[:, :, :], in_w[:, :, bass.ds(g * GW, GW)]).then_inc(q["wz_landed"], 16)
                        sp.wait_ge(q["out_full"], g * 2 * NT)
                        alone(sp)
                        sp.dma_start(wo[:, :, :], out_w[:, bass.ds(g * XF, XF), :]).then_inc(q["wo_landed"], 16)
                        sp.wait_ge(q["yn_ready"], g * NT)
                        alone(sp)
                        sp.dma_start(nwg[:, :], a["m_norm_w"][:, bass.ds(g * GW, GW)].broadcast_to([P, GW])).then_inc(q["nw_landed"], 16)

                def load_state(n):
                    sp.dma_start(st[:, n % 4, :, :],
                                 st_in[bass.ds(g * GW, GW), n, :].rearrange("(f p) n -> p f n", p=P)).then_inc(st_landed[n % 4], 16)

                for n in range(4):
                    load_state(n)
                for n in range(NSEQ):
                    sp.wait_ge(q["snew_ready"], g * NSEQ + n + 1)
                    alone(sp)
                    sp.dma_start(st_out[bass.ds(g * GW, GW), n, :].rearrange("(f p) n -> p f n", p=P),
                                 st[:, n % 4, :, :]).then_inc(q["state_stored"], 16)
                    if n + 4 < NSEQ:
                        sp.wait_ge(q["state_stored"], g * (16 * NSEQ) + 16 * (n + 1))
                        alone(sp)
                        load_state(n + 4)
                sp.wait_ge(q["fin_ready"], g + 1)
                alone(sp)
                sp.wait_ge(q["state_stored"], g * (16 * NSEQ) + 16 * NSEQ)
                alone(sp)
                sp.dma_start(st_prompt[bass.ds(g * GW, GW), :].rearrange("(f p) n -> p f n", p=P),
                             h0T[:, 0, :].rearrange("p (f n) -> p f n", f=XF)).then_inc(q["fin_stored"], 16)
            sp.wait_ge(q["fin_stored"], 16 * NG)
            sp.wait_ge(q["tail_ready"], CONVF // 4)
            sp.dma_start(o["conv_prompt"].rearrange("x b k (c n) -> (x b k) c n", c=3), tail_rows[0:CK - 1, :, :]).then_inc(q["tail_stored"], 16)
            sp.dma_start(o["conv_sample"].rearrange("x s k (c n) -> (x s k) c n", c=3), tail_rows[CK - 1:TAIL, :, :]).then_inc(q["tail_stored"], 16)
            sp.wait_ge(q["tail_stored"], 32)
            ple_sync(sp, 0, 1, False)
            section3_sync(sp)
            section4_sync(sp)
            section5_sync(sp)
            ple_sync(sp, 1, 4, True)

        @block.gpsimd
        def _(pool):
            pool.memset(mhalf[:, :], -0.5).then_inc(q["memset_done"], 1)
            pool.memset(ss[:, :], 1.0).then_inc(q["memset_done"], 1)
            pool.memset(ones[:, :], 1.0).then_inc(q["memset_done"], 1)
            pool.memset(raw[:, :, 0:CK - 1], 0.0).then_inc(q["memset_done"], 1)
            pool.wait_ge(q["memset_done"], 4)
            norm_gpsimd(pool, 0)
            pool.wait_ge(q["dt_ready"], 2)
            pool.wait_ge(q["const_loaded"], 16)
            pool.wait_ge(q["vec_loaded"], 48)

            def decay_sums(g, c, n):
                r = ROWS[c]
                alone(pool)
                tri = con("tri" if c < LC else "tri8", r)[:, 0:r]
                out = mix[0:r, c % 2, 0:HG * r].rearrange("p (h l) -> p h l", h=HG)
                pool.tensor_tensor(out, over(tri, r, HG, r), bc(dta[0:r, c, bass.ds(g * HG, HG)], r, HG, r),
                                   ALU.mult).then_inc(q["sum_ready"], 1)

            with pool.Fori(0, NG) as g:
                for c in range(NT):
                    n = g * NT + c
                    r = ROWS[c]
                    if c == 0:
                        pool.wait_ge(q["yd_full"], n)
                        decay_sums(g, 0, n)
                    v = xt[0:r, :].rearrange("p (h d) -> p h d", h=HG)
                    pool.wait_ge(q["xdt_ready"], n + 1)
                    alone(pool)
                    pool.tensor_tensor(v, v,
                                       bc(vec[0:r, bass.ds(g * HG + 2 * NH, HG)], r, HG, HD), ALU.mult).then_inc(q["skip_ready"], 1)
                    if c:
                        pool.wait_ge(q["st_full"], g * LC + c)
                    else:
                        pool.wait_ge(q["snew_full"], g * NSEQ)
                    alone(pool)
                    pool.tensor_tensor(xdtd[0:r, :].rearrange("p (h d) -> p h d", h=HG),
                                       xdt[0:r, :].rearrange("p (h d) -> p h d", h=HG),
                                       bc(dend[0:r, c, bass.ds(g * HG, HG)], r, HG, HD), ALU.mult).then_inc(q["xdtd_ready"], 1)
                    if c + 1 < NT:
                        if c:
                            pool.wait_ge(q["yd_full"], n)
                        decay_sums(g, c + 1, n + 1)
                    pool.wait_ge(q["msy_ready"], n + 1)
                    pool.tensor_tensor(ybuf[0:r, 2:3], ybuf[0:r, 1:2], mhalf[0:r, 0:1], ALU.pow).then_inc(q["ry_ready"], 1)
            ple_gpsimd(pool, 0, 1)
            section3_gpsimd(pool)
            section4_gpsimd(pool)
            section5_gpsimd(pool)
            ple_gpsimd(pool, 1, 4)

        @block.scalar
        def _(act):
            act.wait_ge(q["memset_done"], 4)
            act.wait_ge(q["res_loaded"], 32)
            norm_scalar(act, 0)
            act.wait_ge(q["cwT_full"], 1)
            act.copy(cw[:, :], bank[:, 4, 0:(CK + 1) * CONVF]).then_inc(q["cwT_ready"], 1)
            for j in range(2):
                act.wait_ge(q["scT_full"], j + 1)
                w = NSEQ * (CK - 1)
                act.copy(sct[:, 12 * j:12 * j + 12, :].rearrange("p f w -> p (f w)"), bank[:, 5 + j, 0:12 * w]).then_inc(q["scT_ready"], 1)
            chain = Chain(act, q["achain"])
            act.wait_ge(q["dt_ready"], 1)
            chain(act.activation(tiny[:, 1, :], tiny[:, 0, :], ACT.Abs))
            chain(act.activation(tiny[:, 2, :], tiny[:, 1, :], ACT.Exp, scale=-1.0))
            act.activation(tiny[:, 3, :], tiny[:, 2, :], ACT.Ln, bias=1.0).then_inc(q["acum_ready"], 1)
            act.activation(vec[:, NH:2 * NH], vec[:, NH:2 * NH], ACT.Exp).then_inc(q["acum_ready"], 1)
            act.wait_ge(q["acum_full"], 2)
            for b, dst in ((5, ea), (6, dec)):
                act.activation(dst[:, 0:PT, :], bank[:, b, 0:PT * NH].rearrange("p (t h) -> p t h", t=PT), ACT.Exp)
                act.activation(dst[0:SAMP, PT, :], bank[0:SAMP, b, PT * NH:NT * NH], ACT.Exp).then_inc(q["acum_ready"], 1)
            act.wait_ge(q["dt_ready"], 3)
            act.activation(dend[:, :, :].rearrange("p t h -> p (t h)"), tiny[:, 4, :], ACT.Exp).then_inc(q["acum_ready"], 1)
            act.wait_ge(q["memset_done"], 4)
            act.wait_ge(q["scT_ready"], 2)
            W = CK + 1
            with act.Fori(0, NG) as g:
                cwv = cw[:, :].rearrange("p (k f) -> p f k", k=W)
                act.wait_ge(q["conv_done"], g * CF)
                act.copy(cwg[:, 0:XF, :], cwv[:, bass.ds(g * XF, XF), :])
                act.copy(cwg[:, XF, :], cwv[:, bass.ds(g + NG * XF, 1), :].rearrange("p f k -> p (f k)"))
                act.copy(cwg[:, XF + 1, :], cwv[:, bass.ds(g + NG * XF + NG, 1), :].rearrange("p f k -> p (f k)")).then_inc(q["cwg_ready"], 1)
                for f in range(CF + 1):
                    if f < CF:
                        ft = [g * XF + f, g + NG * XF, g + NG * XF + NG][max(0, f - XF + 1)]
                        act.wait_ge(q["conv_done"], g * CF + max(0, f - 1))
                        rs = raw[:, f % 2, SOFF:RAWW].rearrange("p (s w) -> p s w", s=NSEQ)
                        act.copy(rs[:, :, 0:CK - 1], sct[:, bass.ds(ft, 1), :].rearrange("p f (s w) -> p (f s) w", s=NSEQ))
                        act.wait_ge(q["xg_full"], g * CF + f + 1)
                        b = 3 * (f % 2)
                        act.copy(raw[:, f % 2, CK - 1:CK - 1 + 512], bank[:, b, :])
                        act.copy(raw[:, f % 2, CK - 1 + 512:SOFF], bank[:, b + 1, :])
                        act.copy(rs[:, :, CK - 1:], bank[:, b + 2, 0:SAMP].rearrange("p (s w) -> p s w", s=NSEQ)).then_inc(q["raw_ready"], 1)
                    if f:
                        act.wait_ge(q["conv_done"], g * CF + f)
                        act.activation(xbc[:, f - 1, :], xbc[:, f - 1, :], ACT.Silu).then_inc(q["conv_ready"], 1)

                def turn(c, n):
                    r = ROWS[c]
                    act.wait_ge(q["yT_full"], n + 1)
                    act.wait_ge(q["out_full"], n * 2)
                    act.copy(yT[:, :, 0:r], bank[:, 0, :].rearrange("p (f r) -> p f r", f=XF)[:, :, 0:r]).then_inc(q["yT_ready"], 1)

                for c in range(NT):
                    n = g * NT + c
                    r = ROWS[c]
                    act.wait_ge(q["x_full"], n + 1)
                    act.wait_ge(q["gated"], n)
                    act.copy(xt[0:r, :], bank[0:r, 0, :]).then_inc(q["xt_ready"], 1)
                    act.wait_ge(q["bc_full"], n + 1)
                    if c:
                        act.wait_ge(q["st_full"], g * LC + c)
                    else:
                        act.wait_ge(q["bseq_ready"], g)
                    act.copy(btok[0:r, :], bank[0:r, 1, 0:DS]).then_inc(q["btok_ready"], 1)
                    act.wait_ge(q["seg_full"], n + 1)
                    if c < LC:
                        act.activation(mix[:, c % 2, :], bank[:, 2:4, :].rearrange("p b n -> p (b n)"), ACT.Exp).then_inc(q["e_ready"], 1)
                    else:
                        act.activation(mix[0:r, c % 2, 0:HG * r], bank[0:r, 2, :], ACT.Exp).then_inc(q["e_ready"], 1)
                    act.wait_ge(q["z_full"], n + 1)
                    act.activation(zs[0:r, :], bank[0:r, 4, :], ACT.Silu).then_inc(q["z_ready"], 1)
                    if c:
                        turn(c - 1, n - 1)
                    if c == LC:
                        for sq in range(NSEQ):
                            act.wait_ge(q["h0_full"], g * NSEQ + sq + 1)
                            if sq == 0:
                                act.wait_ge(q["fin_stored"], g * 16)
                            else:
                                if sq >= 2:
                                    act.wait_ge(q["yo_used"], g * NSEQ + sq - 1)
                            act.copy(h0T[:, sq % 2, :], bank[:, 7, :]).then_inc(q["h0_ready"], 1)
                    act.wait_ge(q["gated"], n + 1)
                    act.wait_ge(q["ssy_ready"], n)
                    act.activation(square[0:r, 0:GW], y[0:r, :], ACT.Square, accum_out=ybuf[0:r, 0:1]).then_inc(q["ssy_ready"], 1)
                act.wait_ge(q["fin_full"], g + 1)
                act.wait_ge(q["yo_used"], g * NSEQ + NSEQ)
                act.copy(h0T[:, 0, :], bank[:, 7, :]).then_inc(q["fin_ready"], 1)
                turn(NT - 1, g * NT + NT - 1)
            act.wait_ge(q["out_full"], 2 * NT * NG)
            for j in range(CONVF // 4):
                act.wait_ge(q["tail_full"], j + 1)
                act.copy(tail_rows[:, j // 2, 512 * (j % 2):512 * (j % 2) + 512], bank[0:TAIL, 4 + j % 2, :]).then_inc(q["tail_ready"], 1)
            ple_scalar(act, 0, 1)
            section3_scalar(act)
            section4_scalar(act)
            section5_scalar(act)
            ple_scalar(act, 1, 4)

        @block.vector
        def _(dve):
            chain = Chain(dve, q["vchain"])
            norm_vector(dve, 0)
            n = NT * NH
            dve.wait_ge(q["dt_full"], 1)
            dve.wait_ge(q["vec_loaded"], 48)
            chain(dve.memset(tiny[:, :, :], 0.0))
            for t in range(NT):
                r = ROWS[t]
                last = dve.tensor_tensor(tiny[0:r, 0, t * NH:(t + 1) * NH], bank[0:r, 7, t * NH:(t + 1) * NH], vec[0:r, 0:NH], ALU.add)
            last.then_inc(q["dt_ready"], 1)
            dve.wait_ge(q["dt_ready"], 1)
            dve.wait_ge(q["acum_ready"], 2)
            w, e, x = tiny[:, 1, :], tiny[:, 2, :], tiny[:, 0, :]
            chain(dve.tensor_scalar(w, e, 1.0, None, ALU.add))
            chain(dve.tensor_scalar(tiny[:, 4, :], w, -1.0, None, ALU.add))
            chain(dve.tensor_tensor(tiny[:, 4, :], e, tiny[:, 4, :], ALU.subtract))
            chain(dve.reciprocal(w, w))
            chain(dve.tensor_tensor(w, w, tiny[:, 4, :], ALU.mult))
            chain(dve.tensor_tensor(w, w, tiny[:, 3, :], ALU.add))
            flat = dtv[:, :, :].rearrange("p t h -> p (t h)")
            chain(dve.scalar_tensor_tensor(flat, x, 0.0, w, ALU.max, ALU.add))
            chain(dve.tensor_scalar(vec[:, NH:2 * NH], vec[:, NH:2 * NH], -1.0, None, ALU.mult))
            dve.tensor_tensor(dta[:, :, :], dtv[:, :, :], over(vec[:, NH:2 * NH], P, NT, NH), ALU.mult).then_inc(q["dt_ready"], 1)
            dve.wait_ge(q["acum_full"], 2)
            dve.wait_ge(q["acum_ready"], 4)
            for r, c0, c1 in ((P, 0, PT * NH), (SAMP, PT * NH, n)):
                chain(dve.tensor_copy(tiny[0:r, 4, c0:c1], bank[0:r, 6, c0:c1]))
                last = dve.tensor_tensor(tiny[0:r, 4, c0:c1], tiny[0:r, 4, c0:c1], bank[0:r, 5, c0:c1], ALU.subtract)
            last.then_inc(q["dt_ready"], 1)
            dve.wait_ge(q["scT_ready"], 2)
            with dve.Fori(0, NG) as g:
                chain.enter(g, VSTEPS)
                dve.wait_ge(q["cwg_ready"], g + 1)
                dve.wait_ge(q["fin_full"], g)
                chain(dve.memset(hT[:, :], 0.0))
                for f in range(CF):
                    ft = [g * XF + f, g + NG * XF, g + NG * XF + NG][max(0, f - XF + 1)]
                    dve.wait_ge(q["raw_ready"], g * CF + f + 1)
                    rs = raw[:, f % 2, SOFF:RAWW].rearrange("p (s w) -> p s w", s=NSEQ)
                    dst = xbc[:, f, SEQ:TOK].rearrange("p (s w) -> p s w", s=NSEQ)
                    dve.tensor_copy(tail[:, bass.ds(ft, 1), 0:CK - 1], raw[:, f % 2, SOFF - (CK - 1):SOFF].unsqueeze(1))
                    dve.tensor_copy(tail[:, bass.ds(ft, 1), CK - 1:].rearrange("p f (s w) -> p (f s) w", s=NSEQ), rs[:, :, DSEQ:])
                    for k in range(CK):
                        wk = cwg[:, f, k:k + 1]
                        parts = ((xbc[:, f, 0:SEQ], raw[:, f % 2, k:k + SEQ]), (dst, rs[:, :, k:k + DSEQ]))
                        for m, (d, src) in enumerate(parts):
                            if k == 0:
                                ins = dve.tensor_scalar(d, src, wk, cwg[:, f, CK:CK + 1], ALU.mult, ALU.add)
                            else:
                                ins = dve.scalar_tensor_tensor(d, src, wk, d, ALU.mult, ALU.add)
                        if k < CK - 1:
                            chain(ins)
                    ins.then_inc(q["conv_done"], 1)
                dve.wait_ge(q["nw_landed"], g * 16 + 16)
                for c in range(NT):
                    m = g * NT + c
                    r = ROWS[c]
                    hv = lambda t: t.rearrange("p (h d) -> p h d", h=HG)
                    hs = bass.ds(g * HG, HG)
                    dve.wait_ge(q["btok_ready"], m + 1)
                    dve.tensor_tensor(cbm[0:r, 0:r], bank[0:r, 1, DS:DS + r], con("tri" if c < LC else "tri8", r)[:, 0:r], ALU.mult).then_inc(q["cbm_ready"], 1)
                    dve.wait_ge(q["xt_ready"], m + 1)
                    dve.wait_ge(q["yd_full"], m)
                    dve.wait_ge(q["xdtd_ready"], m)
                    dve.tensor_tensor(hv(xdt[0:r, :]), hv(xt[0:r, :]), bc(dtv[0:r, c, hs], r, HG, HD), ALU.mult).then_inc(q["xdt_ready"], 1)
                    dve.wait_ge(q["e_ready"], m + 1)
                    dve.wait_ge(q["cbm_ready"], m + 1)
                    mv = mix[0:r, c % 2, 0:HG * r].rearrange("p (h l) -> p h l", h=HG)
                    dve.tensor_tensor(mv, mv, over(cbm[0:r, 0:r], r, HG, r), ALU.mult).then_inc(q["m_ready"], 1)
                    if c == LC:
                        dve.wait_ge(q["btok_ready"], m + 1)
                        dve.tensor_tensor(bseq[:, :, :], over(btok[0:r, :], r, NSEQ, DS), bc(con("inseq", r), r, NSEQ, DS), ALU.mult).then_inc(q["bseq_ready"], 1)
                        chain(dve.memset(cseq[:, :, :], 0.0))
                        diag = cseq[:, :, :].rearrange("p s t -> p (s t)")
                        for sq in range(NSEQ):
                            ins = dve.tensor_copy(cseq[:, sq, sq * DSEQ:(sq + 1) * DSEQ], xbc[:, XF + 1, SEQ + sq * DSEQ:SEQ + (sq + 1) * DSEQ])
                        ins.then_inc(q["cseq_ready"], 1)
                        dve.tensor_copy(hv(dexp[:, :]), bc(dec[0:r, c, hs], r, HG, HD)).then_inc(q["dexp_ready"], 1)
                        dve.wait_ge(q["sdec_full"], g + 1)
                        chain(dve.tensor_copy(sdec[:, :, :], bank[:, 6, 0:XF * NSEQ].rearrange("p (f s) -> p f s", f=XF)))
                        for sq in range(NSEQ):
                            dve.wait_ge(q["snew_full"], g * NSEQ + sq + 1)
                            sv = st[:, sq % 4, :, :]
                            chain(dve.tensor_tensor(sv, sv, bc(sdec[:, :, sq], P, XF, DS), ALU.mult))
                            dve.tensor_tensor(sv, sv, bank[:, 1 + 2 * (sq % 2), :].rearrange("p (f n) -> p f n", f=XF), ALU.add).then_inc(q["snew_ready"], 1)
                    dve.wait_ge(q["yd_full"], m + 1)
                    dve.wait_ge(q["yn_ready"], m)
                    dve.wait_ge(q["yT_full"], m)
                    chain(dve.tensor_tensor(hv(y[0:r, :]), hv(bank[0:r, 5, :]), bc(ea[0:r, c, hs], r, HG, HD), ALU.mult))
                    chain(dve.tensor_tensor(y[0:r, :], y[0:r, :], bank[0:r, 6, :], ALU.add))
                    dve.wait_ge(q["skip_ready"], m + 1)
                    chain(dve.tensor_tensor(y[0:r, :], y[0:r, :], xt[0:r, :], ALU.add))
                    dve.wait_ge(q["z_ready"], m + 1)
                    dve.tensor_tensor(y[0:r, :], y[0:r, :], zs[0:r, :], ALU.mult).then_inc(q["gated"], 1)
                    if c < LC:
                        dve.wait_ge(q["st_full"], g * LC + c + 1)
                        chain(dve.tensor_tensor(hv(hT[:, :]), hv(hT[:, :]), bc(dec[:, c, hs], P, HG, HD), ALU.mult))
                        dve.tensor_tensor(hT[:, :], hT[:, :], bank[:, 7, :], ALU.add).then_inc(q["hT_ready"], 1)
                    if c:
                        add_out(dve, c - 1, m - 1)
                    dve.wait_ge(q["ssy_ready"], m + 1)
                    dve.tensor_scalar(ybuf[0:r, 1:2], ybuf[0:r, 0:1], 1.0 / GW, EPS, ALU.mult, ALU.add).then_inc(q["msy_ready"], 1)
                    dve.wait_ge(q["ry_ready"], m + 1)
                    dve.scalar_tensor_tensor(y[0:r, :], y[0:r, :], ybuf[0:r, 2:3], nwg[0:r, :], ALU.mult, ALU.mult).then_inc(q["yn_ready"], 1)
                add_out(dve, NT - 1, g * NT + NT - 1)
                chain.leave(NG)
            ple_vector(dve, 0, 1)
            section3_vector(dve, chain)
            section4_vector(dve, chain)
            section5_vector(dve, chain)
            ple_vector(dve, 1, 4)

        @block.tensor
        def _(pe):
            pe.wait_ge(q["const_loaded"], 16)
            norm_tensor(pe, 0)
            pe.wait_ge(q["cw_loaded"], 32)
            pe.transpose(bank[:, 4, 0:(CK + 1) * CONVF], cw_rows, ident[0:(CK + 1) * CONVF, 0:(CK + 1) * CONVF]).then_inc(q["cwT_full"], 1)
            pe.wait_ge(q["sc_loaded"], 16)
            w = NSEQ * (CK - 1)
            for f in range(CONVF):
                last = pe.transpose(bank[:, 5 + f // 12, (f % 12) * w:(f % 12 + 1) * w], sc_rows[:, f // 8, (f % 8) * P:(f % 8 + 1) * P], ident[0:w, 0:w])
                if f % 12 == 11:
                    last.then_inc(q["scT_full"], 1)
            pe.wait_ge(uT_ready, 2 * NT)
            pe.wait_ge(q["wdt_loaded"], 16)
            for t in range(NT):
                r = ROWS[t]
                for k in range(KT):
                    last = pe.matmul(bank[0:r, 7, t * NH:(t + 1) * NH], uT[:, k, cols(t)], wdt[:, k, :], start=(k == 0), stop=(k == KT - 1))
            last.then_inc(q["dt_full"], 1)
            pe.wait_ge(q["dt_ready"], 2)
            pe.wait_ge(q["scT_ready"], 2)
            pe.wait_ge(q["memset_done"], 4)
            for b, full, part in ((5, "tri", "tri8"), (6, None, "same8")):
                for t in range(NT):
                    r = ROWS[t]
                    m = (con(full) if full else ones[:, :]) if t < PT else con(part, r)[:, 0:r]
                    last = pe.matmul(bank[0:r, b, t * NH:(t + 1) * NH], m, dta[0:r, t, :], start=True, stop=True)
                last.then_inc(q["acum_full"], 1)
            pe.wait_ge(q["acum_ready"], 5)
            pe.wait_ge(q["cwT_ready"], 1)
            with pe.Fori(0, NG) as g:
                pe.wait_ge(q["out_added"], g * (2 * NT))
                pe.wait_ge(q["fin_ready"], g)
                for f in range(CF):
                    pe.wait_ge(wx_landed[f % 2], g * 48 + 16 * (f // 2 + 1))
                    if f > 1:
                        pe.wait_ge(q["raw_ready"], g * CF + f - 1)
                    for j, (c0, c1) in enumerate(((0, 512), (512, 1024), (SEQ, TOK))):
                        for k in range(KT):
                            last = pe.matmul(bank[:, 3 * (f % 2) + j, 0:c1 - c0], wx[:, f % 2, k, :], uT[:, k, c0:c1],
                                             start=(k == 0), stop=(k == KT - 1))
                    last.then_inc(q["xg_full"], 1)
                pe.wait_ge(q["conv_ready"], g * CF + CF)
                pe.wait_ge(q["raw_ready"], g * CF + CF)

                def turn_y(c, n):
                    r = ROWS[c]
                    pe.wait_ge(q["yn_ready"], n + 1)
                    alone(pe)
                    for f in range(XF):
                        last = pe.transpose(bank[:, 0, f * P:f * P + r], y[0:r, f * P:(f + 1) * P], ident[0:r, 0:r])
                    last.then_inc(q["yT_full"], 1)

                def multiply_out(c, n):
                    r = ROWS[c]
                    pe.wait_ge(q["yT_ready"], n + 1)
                    if c == 0:
                        pe.wait_ge(q["wo_landed"], g * 16 + 16)
                    alone(pe)
                    for half in range(2):
                        for k in range(XF):
                            last = pe.matmul(bank[0:r, 2 + half, :], yT[:, k, 0:r], wo[:, k, 512 * half:512 * (half + 1)],
                                             start=(k == 0), stop=(k == XF - 1))
                        last.then_inc(q["out_full"], 1)

                for c in range(NT):
                    n = g * NT + c
                    r = ROWS[c]
                    cs = cols(c)
                    if c > 1:
                        pe.wait_ge(q["yT_ready"], n - 1)
                    if c == LC:
                        alone(pe)
                    for f in range(XF):
                        last = pe.transpose(bank[0:r, 0, f * P:(f + 1) * P], xbc[:, f, cs], ident)
                    last.then_inc(q["x_full"], 1)
                    pe.wait_ge(q["btok_ready"], n)
                    pe.wait_ge(q["cbm_ready"], n)
                    if c == LC:
                        alone(pe)
                    pe.transpose(bank[0:r, 1, 0:DS], xbc[:, XF, cs], ident)
                    pe.matmul(bank[0:r, 1, DS:DS + r], xbc[:, XF, cs], xbc[:, XF + 1, cs], start=True, stop=True).then_inc(q["bc_full"], 1)
                    pe.wait_ge(q["sum_ready"], n + 1)
                    if c > 1:
                        pe.wait_ge(q["out_added"], n * 2 - 2)
                    if c == LC:
                        alone(pe)
                    if c < LC:
                        for half in range(2):
                            last = pe.matmul(bank[:, 2 + half, :], con("after"), mix[:, c % 2, 512 * half:512 * (half + 1)], start=True, stop=True)
                    else:
                        last = pe.matmul(bank[0:r, 2, :], con("after8", r)[:, 0:r], mix[0:r, c % 2, 0:HG * r], start=True, stop=True)
                    last.then_inc(q["seg_full"], 1)
                    if c == 0:
                        pe.wait_ge(q["wz_landed"], g * 16 + 16)
                    pe.wait_ge(q["z_ready"], n)
                    if c == LC:
                        alone(pe)
                    for k in range(KT):
                        last = pe.matmul(bank[0:r, 4, :], uT[:, k, cs], wz[:, k, :], start=(k == 0), stop=(k == KT - 1))
                    last.then_inc(q["z_full"], 1)
                    if c:
                        pe.wait_ge(q["xt_ready"], n + 1)
                        turn_y(c - 1, n - 1)
                    pe.wait_ge(q["gated"], n)
                    pe.wait_ge(q["m_ready"], n + 1)
                    pe.wait_ge(q["xdt_ready"], n + 1)
                    if c == LC:
                        pe.wait_ge(q["hT_ready"], g * LC + LC)
                        pe.wait_ge(q["dexp_ready"], g + 1)
                        alone(pe)
                        for f in range(XF):
                            last = pe.matmul(bank[:, 6, f * NSEQ:(f + 1) * NSEQ], dexp[:, f * P:(f + 1) * P], con("first", r), start=True, stop=True)
                        last.then_inc(q["sdec_full"], 1)
                        pe.wait_ge(q["cseq_ready"], g + 1)
                        pe.wait_ge(q["bseq_ready"], g + 1)
                        pe.wait_ge(q["xdtd_ready"], n + 1)
                        pe.wait_ge(q["btok_ready"], n + 1)
                        pe.wait_ge(q["cbm_ready"], n + 1)
                        pe.wait_ge(q["e_ready"], n + 1)

                        def turn_state(sq):
                            pe.wait_ge(st_landed[sq % 4], g * 32 + 16 * (sq // 4 + 1))
                            if sq:
                                pe.wait_ge(q["h0_ready"], g * NSEQ + sq)
                            for f in range(XF):
                                last = pe.transpose(bank[:, 7, f * P:(f + 1) * P], st[:, sq % 4, f, :], ident)
                            last.then_inc(q["h0_full"], 1)

                        turn_state(0)
                        for sq in range(NSEQ):
                            if sq > 1:
                                pe.wait_ge(q["snew_ready"], g * NSEQ + sq - 1)
                            alone(pe)
                            for f in range(XF):
                                last = pe.matmul(bank[:, 1 + 2 * (sq % 2), f * P:(f + 1) * P], xdtd[0:r, f * P:(f + 1) * P], bseq[:, sq, :], start=True, stop=True)
                            last.then_inc(q["snew_full"], 1)
                            if sq + 1 < NSEQ:
                                turn_state(sq + 1)
                            pe.wait_ge(q["h0_ready"], g * NSEQ + sq + 1)
                            alone(pe)
                            pe.matmul(bank[0:r, 5, :], cseq[:, sq, :], h0T[:, sq % 2, :], start=(sq == 0), stop=(sq == NSEQ - 1)).then_inc(q["yo_used"], 1)
                        pe.wait_ge(q["snew_ready"], g * NSEQ + NSEQ)
                    else:
                        if c:
                            pe.wait_ge(q["hT_ready"], g * LC + c)
                        else:
                            pe.wait_ge(q["raw_ready"], g * CF + CF)
                        pe.matmul(bank[:, 5, :], xbc[:, XF + 1, cs], hT[:, :], start=True, stop=True)
                    if c == LC:
                        alone(pe)
                    for hh in range(HG):
                        last = pe.matmul(bank[0:r, 6, hh * HD:(hh + 1) * HD], mix[0:r, c % 2, hh * r:(hh + 1) * r],
                                         xdt[0:r, hh * HD:(hh + 1) * HD], start=True, stop=True)
                    last.then_inc(q["yd_full"], 1)
                    if c < LC:
                        pe.wait_ge(q["xdtd_ready"], n + 1)
                        pe.wait_ge(q["btok_ready"], n + 1)
                        pe.matmul(bank[:, 7, :], btok[:, :], xdtd[:, :], start=True, stop=True).then_inc(q["st_full"], 1)
                    if c:
                        multiply_out(c - 1, n - 1)
                pe.wait_ge(q["h0_ready"], g * NSEQ + NSEQ)
                for f in range(XF):
                    last = pe.transpose(bank[:, 7, f * P:(f + 1) * P], hT[:, f * P:(f + 1) * P], ident)
                last.then_inc(q["fin_full"], 1)
                turn_y(NT - 1, g * NT + NT - 1)
                multiply_out(NT - 1, g * NT + NT - 1)
            for j in range(CONVF // 4):
                if j > 1:
                    pe.wait_ge(q["tail_ready"], j - 1)
                for i in range(4):
                    last = pe.transpose(bank[0:TAIL, 4 + j % 2, i * P:(i + 1) * P], tail[:, 4 * j + i, :], ident)
                last.then_inc(q["tail_full"], 1)
            ple_tensor(pe, 0, 1)
            section3_tensor(pe)
            section4_tensor(pe)
            section5_tensor(pe)
            ple_tensor(pe, 1, 4)


_INS = ["x_prompt", "x_sample", "state_ssm", "state_conv", "cache_kv_g1", "cache_kv_g2", "cache_kv_g3",
        "p_prompt", "p_sample", "norm_w", "m_in_w", "m_conv_w", "m_conv_b", "m_dt_bias", "m_A_log", "m_D",
        "m_norm_w", "m_out_w", "kv_norm_w", "kv_w", "k_norm_w", "a_in_w", "a_q_norm_w", "a_out_w",
        "ple_w", "ple_gate_w", "ple_norm_w"]
KV = (2, KVH, HD)
_OUTS = {"y_prompt": (1, SEQ, D), "y_sample": (NSEQ, DSEQ, D), "ssm_prompt": (1, 1, NH, HD, DS),
         "conv_prompt": (1, 1, CK - 1, CONVF * P), "ssm_sample": (1, NSEQ, NH, HD, DS),
         "conv_sample": (1, NSEQ, CK - 1, CONVF * P),
         "kv_prompt_g1": (1, 128) + KV, "kv_prompt_g2": (1, 512) + KV, "kv_prompt_g3": (1, 1024) + KV,
         "kv_sample_g1": (NSEQ, DSEQ) + KV, "kv_sample_g2": (NSEQ, DSEQ) + KV, "kv_sample_g3": (NSEQ, DSEQ) + KV}
_SCRATCH = {"kv": (TOK, 2, NGR, KVH * HD), "q": (TOK, NGR, D), "gate": (TOK, D), "u": (NGR, SEQ, D), "ms": (NGR, SEQ, 2 * AH),
            "os": (SAMP, D)}


def kernel(**inputs):
    import concourse.bacc as bacc
    from concourse.bass_utils import run_bass_kernel_spmd

    nc = bacc.Bacc("TRN2", target_bir_lowering=False, num_devices=1)
    arrays, a = {}, {}
    for name in _INS:
        x = np.ascontiguousarray(inputs[name])
        arrays[f"in_{name}"] = x
        a[name] = nc.dram_tensor(f"in_{name}", x.shape, mybir.dt.from_np(x.dtype), kind="ExternalInput").ap()
    table = np.concatenate([v for v in shape_constants().values()], 1)
    arrays["in_consts"] = table
    a["consts"] = nc.dram_tensor("in_consts", table.shape, F32, kind="ExternalInput").ap()
    o = {n: nc.dram_tensor(f"out_{n}", shape, F32, kind="ExternalOutput").ap() for n, shape in _OUTS.items()}
    s = {n: nc.dram_tensor(f"scratch_{n}", shape, F32).ap() for n, shape in _SCRATCH.items()}
    trunk_kernel(nc, a, o, s)
    r = run_bass_kernel_spmd(nc, [arrays], core_ids=[0])
    return tuple(r.results[0][f"out_{n}"] for n in _OUTS)
```

```python
from contextlib import ExitStack

import numpy as np

import concourse.bass as bass
from concourse import mybir

F32 = mybir.dt.float32
ALU = mybir.AluOpType
ACT = mybir.ActivationFunctionType
AX_X = mybir.AxisListType.X
P = 128
EPS = 1e-6
FR = mybir.dt.float32r
NEG = -1e30

D = 1024
KT = D // P
SEQ, NSEQ, DSEQ, PAST = 1024, 8, 8, 1024
PT = SEQ // P
NT = PT + 1
SAMP = NSEQ * DSEQ
TOK = SEQ + SAMP
ROWS = [P] * PT + [SAMP]
DI, HD, NH, NG, DS = 2048, 64, 32, 4, 128
HG = NH // NG
GW = HG * HD
XF = GW // P
CF = XF + 2
CONVF = (DI + 2 * NG * DS) // P
CK = 4
LC = SEQ // P
RAWW = CK - 1 + SEQ + NSEQ * (CK - 1 + DSEQ)
SOFF = CK - 1 + SEQ
TAIL = (CK - 1) * (1 + NSEQ)
AH, KVH, REP = 16, 4, 4
NGR = 3
DIL = (1, 4, 16)
PLE = 256


def shape_constants():
    i = np.arange(P)
    seq = i // DSEQ
    same = seq[:, None] == seq[None, :]
    c = {}
    c["ident"] = np.eye(P)
    c["tri"] = (i[:, None] <= i[None, :])
    c["after"] = (i[:, None] > i[None, :])
    c["tri8"] = (i[:, None] <= i[None, :]) & same
    c["after8"] = (i[:, None] > i[None, :]) & same
    c["same8"] = same
    s = np.arange(NSEQ)
    c["inseq"] = seq[:, None] == s[None, :]
    c["first"] = i[:, None] == DSEQ * s[None, :]
    half = HD // 2
    inv = 1.0 / (10000.0 ** (np.arange(half, dtype=np.float32) / np.float32(half)))
    pos = np.concatenate([np.arange(SEQ), PAST + np.arange(P) % DSEQ]).astype(np.float32)
    ang = pos[:, None] * inv[None, :].astype(np.float32)
    cos = np.cos(ang).reshape(NT, P, half).transpose(1, 0, 2)
    sin = np.sin(ang).reshape(NT, P, half).transpose(1, 0, 2)
    c["cos"] = np.concatenate([cos, cos], -1).reshape(P, -1)
    c["sin"] = np.concatenate([-sin, sin], -1).reshape(P, -1)
    q, k = i[:, None], i[None, :]
    c["win"] = np.concatenate([np.where(k >= q, 0, NEG), np.where(k <= q, 0, NEG)], 1)
    c["pair"] = np.where((k <= q) & (k // 64 == q // 64), 0, NEG)
    t = (i % DSEQ)[:, None]
    new = np.arange(DSEQ)[None, :]
    parts = [np.where(k >= t, 0, NEG)]
    for dil in DIL:
        parts.append(np.where((new <= t) & ((t - new) % dil == 0), 0, NEG))
    for r in range(4):
        parts.append(np.where(((t % 4) == r) & (4 * k + r >= t), 0, NEG))
    for a in range(4):
        parts.append(np.where((2 * a + k // 64) == t, 0, NEG) + 0.0 * k)
    c["smask"] = np.concatenate([p + np.zeros((P, p.shape[1])) for p in parts], 1)
    return {n: np.ascontiguousarray(v, np.float32) for n, v in c.items()}


LAYOUT, _at = {}, 0
for _n, _w in (("ident", P), ("tri", P), ("after", P), ("tri8", P), ("after8", P), ("same8", P),
               ("inseq", NSEQ), ("first", NSEQ), ("cos", NT * HD), ("sin", NT * HD),
               ("win", 2 * P), ("pair", P), ("smask", P + 3 * DSEQ + 8 * P)):
    LAYOUT[_n] = (_at, _w)
    _at += _w
NCONST = _at
NMASK = LAYOUT["cos"][0]


class Chain:

    def __init__(self, eng, sem):
        self.eng, self.sem, self.n, self.i, self.start, self.stride = eng, sem, 0, None, 0, 0

    def enter(self, i, stride):
        self.i, self.start, self.stride = i, self.n, stride

    def leave(self, times):
        assert self.n - self.start == self.stride, (self.n - self.start, self.stride)
        self.n = self.start + times * self.stride
        self.i = None

    def __call__(self, ins):
        ins.then_inc(self.sem, 1)
        self.n += 1
        if self.i is None:
            self.eng.wait_ge(self.sem, self.n)
        else:
            self.eng.wait_ge(self.sem, self.i * self.stride + self.n)


def trunk_kernel(nc, a, o, s):
    outer = ExitStack()
    with outer:
        def sem(name):
            return outer.enter_context(nc.semaphore(name))

        def sb_in(ctx):
            def sb(name, shape, dt=F32):
                return ctx.enter_context(nc.sbuf_tensor(name, shape, dt))
            return sb

        keep = sb_in(outer)
        bank = outer.enter_context(nc.psum_tensor("bank", [P, 8, 512], F32))
        h = keep("h", [P, NT, D])
        cst = keep("cst", [P, NMASK])
        gain = keep("gain", [P, D])
        u = keep("u", [P, 2, D])
        ss = keep("ss", [P, 16])
        ms = keep("ms", [P, 16])
        rstd = keep("rstd", [P, 16])
        mhalf = keep("mhalf", [P, 16])
        square = keep("square", [P, D])
        same = ExitStack()
        uT = sb_in(same)("uT", [P, KT, TOK])
        same.close()
        uH = keep("uH", [P, KT, TOK], FR)

        def con(name, rows=P):
            at, w = LAYOUT[name]
            return cst[0:rows, at:at + w]

        ident = con("ident")

        s1 = ExitStack()
        sb = sb_in(s1)
        wx = sb("wx", [P, 2, KT, P])
        wz = sb("wz", [P, KT, GW])
        wo = sb("wo", [P, XF, D])
        wdt = sb("wdt", [P, KT, NH])
        raw = sb("raw", [P, 2, RAWW])
        xbc = sb("xbc", [P, CF, TOK])
        sct = sb("sct", [P, CONVF, NSEQ * (CK - 1)])
        tail = sb("tail", [P, CONVF, TAIL])
        cw = sb("cw", [P, (CK + 1) * CONVF])
        cwg = sb("cwg", [P, CF, CK + 1])
        vec = sb("vec", [P, 3 * NH])
        dtv = sb("dtv", [P, NT, NH])
        dta = sb("dta", [P, NT, NH])
        ea = sb("ea", [P, NT, NH])
        dend = sb("dend", [P, NT, NH])
        dec = sb("dec", [P, NT, NH])
        nwg = gain[:, 0:GW]
        ones = sb("ones", [P, P])
        xt = sb("xt", [P, GW])
        btok = sb("btok", [P, DS])
        cbm = sb("cbm", [P, P])
        mix = sb("mix", [P, 2, HG * P])
        xdt = sb("xdt", [P, GW])
        xdtd = sb("xdtd", [P, GW])
        y = square[:, GW:2 * GW]
        zs = sb("zs", [P, GW])
        yT = sb("yT", [P, XF, P])
        hT = gain[:, GW:2 * GW]
        ybuf = sb("ybuf", [P, 4])
        bseq = u[0:SAMP, 0, :].rearrange("p (s n) -> p s n", s=NSEQ)
        cseq = u[:, 1, 0:GW].rearrange("p (s t) -> p s t", s=NSEQ)
        dexp = u[0:SAMP, 1, GW:2 * GW]
        st = sb("st", [P, 4, XF, DS])
        h0T = sb("h0T", [P, 2, GW])
        sdec = sb("sdec", [P, XF, NSEQ])
        tiny = xbc[:, 3:5, :].rearrange("p a b -> p (a b)")[:, 0:5 * NT * NH].rearrange("p (a b) -> p a b", a=5)
        cw_rows = xdt[0:(CK + 1) * CONVF, 0:P]
        sc_rows = xbc[0:NSEQ * (CK - 1), 0:3, 0:D]
        tail_rows = xbc[0:TAIL, 0:3, 0:D]
        s1.close()

        ss_ready = sem("ss_ready")
        ms_ready = sem("ms_ready")
        rstd_ready = sem("rstd_ready")
        gain_landed = sem("gain_landed")
        gain_used = sem("gain_used")
        u_ready = sem("u_ready")
        uT_full = sem("uT_full")
        uT_ready = sem("uT_ready")
        uL_ready = sem("uL_ready")
        section = sem("section")
        names = """res_loaded const_loaded vec_loaded cw_loaded wdt_loaded memset_done
            cwT_full cwT_ready scT_full scT_ready dt_full dt_ready acum_full acum_ready
            wz_landed wo_landed nw_landed xg_full raw_ready conv_done conv_ready
            x_full xt_ready bc_full btok_ready cbm_ready sum_ready seg_full e_ready m_ready z_full z_ready
            xdt_ready xdtd_ready skip_ready yd_full st_full hT_ready gated ssy_ready msy_ready ry_ready yn_ready
            yT_full yT_ready out_full out_added cwg_ready dexp_ready sdec_full sdec_ready bseq_ready cseq_ready
            h0_full h0_ready snew_full snew_ready yo_used fin_full fin_ready fin_stored state_stored tail_full
            tail_ready vchain achain waits_passed"""
        q = {n: sem(n) for n in names.split()}
        wx_landed = [sem(f"wx_landed{i}") for i in range(2)]
        st_landed = [sem(f"st_landed{i}") for i in range(4)]

        in_w = a["m_in_w"][0].rearrange("(k p) n -> p k n", p=P)
        out_w = a["m_out_w"][0].rearrange("(k p) n -> p k n", p=P)
        st_in = a["state_ssm"].rearrange("x s h p n -> (x h p) s n")
        st_out = o["ssm_sample"].rearrange("x s h p n -> (x h p) s n")
        st_prompt = o["ssm_prompt"].rearrange("x b h p n -> (x b h p) n")
        XCOL, BCOL, CCOL, DTCOL = DI, 2 * DI, 2 * DI + NG * DS, 2 * DI + 2 * NG * DS

        VSTEPS = 1 + CF * (CK - 1) + 2 + NSEQ + 3 * NT + LC
        block = outer.enter_context(nc.Block())

        def cols(t):
            return slice(t * P, t * P + ROWS[t])

        def bc(ap, rows, n, m):
            return ap.unsqueeze(2).broadcast_to([rows, n, m])

        def over(ap, rows, n, m):
            return ap.unsqueeze(1).broadcast_to([rows, n, m])

        def alone(eng):
            eng.sem_inc(q["waits_passed"], 1)

        def norm_scalar(act, k, squares=True, split=False):
            if squares:
                for t in range(NT):
                    r = ROWS[t]
                    act.wait_ge(ss_ready, NT * (rstd_count[k] - 1) + t)
                    act.activation(square[0:r, :], h[0:r, t, :], ACT.Square,
                                   accum_out=ss[0:r, t:t + 1]).then_inc(ss_ready, 1)
            for t in range(NT):
                r = ROWS[t]
                act.wait_ge(uT_full, NT * k + t + 1)
                for half in range(2):
                    b = bank[:, 2 * (t % 2) + half, :].rearrange("p (k r) -> p k r", k=4)[:, :, 0:r]
                    act.copy((uH if split else uT)[:, 4 * half:4 * half + 4, cols(t)], b).then_inc(uT_ready, 1)

        rstd_count = {0: 1, 1: 2, 2: 3, 3: 3, 4: 4}

        def low_part(dve, k, t):
            dve.wait_ge(uT_ready, 2 * (NT * k + t + 1))
            for half in range(2):
                part = (slice(None), slice(4 * half, 4 * half + 4), cols(t))
                b = bank[:, 2 * (t % 2) + half, :].rearrange("p (k r) -> p k r", k=4)[:, :, 0:ROWS[t]]
                last = dve.tensor_tensor(uL[part], b, uH[part].bitcast(F32), ALU.subtract)
            last.then_inc(uL_ready, 1)

        def norm_vector(dve, k, squares=True, split=False):
            if squares:
                dve.wait_ge(ss_ready, NT * rstd_count[k])
                dve.tensor_scalar(ms[:, 0:NT], ss[:, 0:NT], 1.0 / D, EPS, ALU.mult,
                                  ALU.add).then_inc(ms_ready, 1)
            dve.wait_ge(rstd_ready, rstd_count[k])
            dve.wait_ge(gain_landed, 16 * (k + 1))
            for t in range(NT):
                r = ROWS[t]
                if NT * k + t >= 2:
                    dve.wait_ge(uT_full, NT * k + t - 1)
                dve.scalar_tensor_tensor(u[0:r, t % 2, :], h[0:r, t, :], rstd[0:r, t:t + 1], gain[0:r, :],
                                         ALU.mult, ALU.mult).then_inc(u_ready, 1)
                if split and t:
                    low_part(dve, k, t - 1)
            if split:
                low_part(dve, k, NT - 1)

        def norm_gpsimd(pool, k):
            pool.wait_ge(ms_ready, rstd_count[k])
            if k:
                pool.wait_ge(u_ready, NT * k)
            pool.tensor_tensor(rstd[:, 0:NT], ms[:, 0:NT], mhalf[:, 0:NT], ALU.pow).then_inc(rstd_ready, 1)

        def norm_tensor(pe, k, split=False):
            for t in range(NT):
                r = ROWS[t]
                pe.wait_ge(u_ready, NT * k + t + 1)
                if t >= 2:
                    pe.wait_ge(uT_ready, 2 * (NT * k + t - 1))
                    if split:
                        pe.wait_ge(uL_ready, NT * (k - 2) + t - 1)
                for f in range(KT):
                    last = pe.transpose(bank[:, 2 * (t % 2) + f // 4, (f % 4) * P:(f % 4) * P + r],
                                        u[0:r, t % 2, f * P:(f + 1) * P], ident[0:r, 0:r])
                last.then_inc(uT_full, 1)

        def load_gain(sp, k, row):
            if k:
                sp.wait_ge(u_ready, NT * k)
            sp.dma_start(gain[:, :], row.broadcast_to([P, D])).then_inc(gain_landed, 16)

        def add_out(dve, c, m):
            r = ROWS[c]
            for half in range(2):
                dve.wait_ge(q["out_full"], m * 2 + half + 1)
                d = h[0:r, c, 512 * half:512 * (half + 1)]
                dve.tensor_tensor(d, d, bank[0:r, 2 + half, :], ALU.add).then_inc(q["out_added"], 1)

        s2 = ExitStack()
        sb = sb_in(s2)
        wg = sb("wg", [P, 2, KT, 512])
        wp = sb("wp", [P, PLE // P, D])
        pin = sb("pin", [P, NT, PLE])
        pT = sb("pT", [P, PLE // P, TOK])
        gs = sb("gs", [P, 2, 512])
        s2.close()
        e = {n: sem("ple_" + n) for n in """w_landed p_landed pT_full pT_ready full gate_ready gated
            added stored""".split()}

        def meet(eng, k):
            eng.drain().then_inc(section, 1)
            eng.wait_ge(section, 5 * k)

        def ple_sync(sp, i, k, last):
            meet(sp, 1 if i == 0 else 5)
            load_gain(sp, k, a["ple_norm_w"][i:i + 1, :])
            sp.dma_start(pin[:, 0:PT, :], a["p_prompt"][i, 0].rearrange("(t p) d -> p t d", p=P)).then_inc(e["p_landed"], 16)
            sp.dma_start(pin[0:SAMP, PT, :], a["p_sample"][i].rearrange("b t d -> (b t) d")).then_inc(e["p_landed"], 16)
            sp.dma_start(wp[:, :, :], a["ple_w"][i].rearrange("(k p) n -> p k n", p=P)).then_inc(e["w_landed"], 16)
            for j in range(2):
                sp.dma_start(wg[:, j, :, :], a["ple_gate_w"][i].rearrange("(k p) n -> p k n", p=P)[:, :, 512 * j:512 * (j + 1)]).then_inc(e["w_landed"], 16)
            if last:
                for t in range(NT):
                    sp.wait_ge(e["added"], 2 * NT * i + NT + t + 1)
                    dst = o["y_prompt"][0, t * P:(t + 1) * P, :] if t < PT else o["y_sample"].rearrange("b t d -> (b t) d")
                    sp.dma_start(dst, h[0:ROWS[t], t, :]).then_inc(e["stored"], 16)
                sp.wait_ge(e["stored"], 16 * NT)

        def ple_scalar(act, i, k):
            meet(act, 1 if i == 0 else 5)
            for t in range(NT):
                r = ROWS[t]
                act.wait_ge(e["pT_full"], NT * i + t + 1)
                act.copy(pT[:, :, cols(t)], bank[:, 4 + t % 2, 0:PLE].rearrange("p (k r) -> p k r", k=2)[:, :, 0:r]).then_inc(e["pT_ready"], 1)
            norm_scalar(act, k)
            with act.Fori(0, 2) as j:
                for t in range(NT):
                    r = ROWS[t]
                    v = j * NT + t
                    act.wait_ge(e["full"], v + (2 * NT * i + 1))
                    act.wait_ge(e["added"], v + 2 * NT * i if t < 2 else v + (2 * NT * i - 1))
                    act.activation(gs[0:r, t % 2, :], bank[0:r, 2 * (t % 3), :], ACT.Sigmoid).then_inc(e["gate_ready"], 1)

        def ple_gpsimd(pool, i, k):
            meet(pool, 1 if i == 0 else 5)
            norm_gpsimd(pool, k)

        def ple_vector(dve, i, k):
            meet(dve, 1 if i == 0 else 5)
            norm_vector(dve, k)
            with dve.Fori(0, 2) as j:
                for t in range(NT):
                    r = ROWS[t]
                    v = j * NT + t
                    g_ = gs[0:r, t % 2, :]
                    dve.wait_ge(e["gate_ready"], v + (2 * NT * i + 1))
                    dve.tensor_tensor(g_, g_, bank[0:r, 2 * (t % 3) + 1, :], ALU.mult).then_inc(e["gated"], 1)
                    dve.wait_ge(e["gated"], v + (2 * NT * i + 1))
                    hv = h[0:r, t, bass.ds(j * 512, 512)]
                    dve.tensor_tensor(hv, hv, g_, ALU.add).then_inc(e["added"], 1)

        def ple_tensor(pe, i, k):
            meet(pe, 1 if i == 0 else 5)
            pe.wait_ge(e["p_landed"], 32 * (i + 1))
            for t in range(NT):
                r = ROWS[t]
                if t > 1:
                    pe.wait_ge(e["pT_ready"], NT * i + t - 1)
                for f in range(PLE // P):
                    last = pe.transpose(bank[:, 4 + t % 2, f * P:f * P + r], pin[0:r, t, f * P:(f + 1) * P], ident[0:r, 0:r])
                last.then_inc(e["pT_full"], 1)
            norm_tensor(pe, k)
            pe.wait_ge(e["pT_ready"], NT * (i + 1))
            pe.wait_ge(e["w_landed"], 48 * (i + 1))
            pe.wait_ge(uT_ready, 2 * NT * (k + 1))
            with pe.Fori(0, 2) as j:
                for t in range(NT):
                    r = ROWS[t]
                    v = j * NT + t
                    pe.wait_ge(e["gated"], v + 2 * NT * i if t < 3 else v + (2 * NT * i - 2))
                    alone(pe)
                    for kk in range(KT):
                        pe.matmul(bank[0:r, 2 * (t % 3), :], uT[:, kk, cols(t)],
                                  wg[:, bass.ds(j, 1), kk, :].rearrange("p a n -> p (a n)"), start=(kk == 0), stop=(kk == KT - 1))
                    for kk in range(PLE // P):
                        last = pe.matmul(bank[0:r, 2 * (t % 3) + 1, :], pT[:, kk, cols(t)], wp[:, kk, bass.ds(j * 512, 512)],
                                         start=(kk == 0), stop=(kk == PLE // P - 1))
                    last.then_inc(e["full"], 1)

        s3 = ExitStack()
        sb = sb_in(s3)
        same = ExitStack()
        wr = sb_in(same)("wr", [P, 2, KT, 512])
        same.close()
        wl = sb("wl", [P, 2, KT, 512], FR)
        wh = sb("wh", [P, 2, KT, 512], FR)
        uL = sb("uL", [P, KT, TOK], FR)
        rope = sb("rope", [P, 2, NT, HD])
        tab = sb("tab", [P, 4, NT, HD])
        nw = sb("nw", [P, 2, HD])
        raws = sb("raws", [P, 2, 512])
        sqr = square[:, :].rearrange("p (a n) -> p a n", a=2)
        rot = u[:, :, 0:512]
        swp = u[:, 0, 512:D]
        hs3 = sb("hs3", [P, 3, 8])
        s3.close()
        j3 = {n: sem("proj_" + n) for n in """full raw_ready ms_ready r_ready rot_ready t_landed tab_ready
            kv_out wh_ready wl_ready""".split()}
        w3_landed = [sem(f"w3_landed{i}") for i in range(2)]
        stored3 = [sem(f"stored3_{i}") for i in range(2)]
        KVB, QB, GB = 3, 6, 2
        UNITS3 = (KVB + QB + GB) * NT
        kv_flat = s["kv"].rearrange("t c g n -> t (c g n)")
        q_flat = s["q"].rearrange("t g n -> t (g n)")
        kw_src = a["kv_w"].rearrange("(k p) n -> p k n", p=P)
        qw_src = a["a_in_w"][0].rearrange("(k p) n -> p k n", p=P)

        def turn_of(i, times, const):
            return const if i is None else i * times + const

        def blocks3(eng, body, between=lambda: None):
            for b in range(KVB):
                body(None, b, (8, 4, 0)[b], 0)
            between()
            with eng.Fori(0, QB // 2) as i:
                for d in range(2):
                    body(i, KVB + d, 8, 2)
            for b in range(KVB + QB, KVB + QB + GB):
                body(None, b, 0, None)

        SPLIT_AT = 5

        def split_weights(eng, i, nb, scalar):
            sl = nb % 2
            if scalar:
                eng.wait_ge(w3_landed[sl], turn_of(i, 16, 16 * (nb // 2 + 1)))
                eng.copy(wh[:, sl, :, :], wr[:, sl, :, :]).then_inc(j3["wh_ready"], 1)
            else:
                eng.wait_ge(j3["wh_ready"], turn_of(i, 2, nb + 1))
                eng.tensor_tensor(wl[:, sl, :, :], wr[:, sl, :, :], wh[:, sl, :, :].bitcast(F32), ALU.subtract).then_inc(j3["wl_ready"], 1)

        def section3_sync(sp):
            meet(sp, 2)
            load_gain(sp, 2, a["kv_norm_w"].unsqueeze(0))
            for j, n in enumerate(("cos", "sin")):
                at, w = LAYOUT[n]
                sp.dma_start(rope[:, j, :, :], a["consts"][:, at:at + w].rearrange("p (t d) -> p t d", t=NT)).then_inc(j3["t_landed"], 16)
            sp.dma_start(nw[:, 0, :], a["k_norm_w"].unsqueeze(0).broadcast_to([P, HD])).then_inc(j3["t_landed"], 16)
            sp.dma_start(nw[:, 1, :], a["a_q_norm_w"].broadcast_to([P, HD])).then_inc(j3["t_landed"], 16)
            sp.dma_start(wr[:, 0, :, :], kw_src[:, :, 0:512]).then_inc(w3_landed[0], 16)

            def body(i, b, m, tb):
                nb = b + 1
                if nb < KVB + QB + GB:
                    if b:
                        sp.wait_ge(j3["full"], turn_of(i, 2 * NT, b * NT))
                        alone(sp)
                    src = kw_src[:, :, 512 * nb:512 * (nb + 1)] if nb < KVB else \
                        qw_src[:, :, bass.ds(turn_of(i, 1024, 512 * (nb - KVB)), 512)]
                    sp.dma_start(wr[:, nb % 2, :, :], src).then_inc(w3_landed[nb % 2], 16)
                for t in range(NT):
                    r = ROWS[t]
                    par = (b * NT + t) % 2
                    sp.wait_ge(j3["rot_ready"], turn_of(i, 2 * NT, b * NT + t + 1))
                    alone(sp)
                    if b < KVB:
                        dst = kv_flat[cols(t), 512 * b:512 * (b + 1)]
                    elif i is None:
                        dst = s["gate"][cols(t), 512 * (b - KVB - QB):512 * (b - KVB - QB + 1)]
                    else:
                        dst = q_flat[cols(t), bass.ds(turn_of(i, 1024, 512 * (b - KVB)), 512)]
                    sp.dma_start(dst, rot[0:r, par, :]).then_inc(stored3[par], 16)

            def between():
                kvn = KVB * NT
                sp.wait_ge(stored3[0], 16 * ((kvn + 1) // 2))
                sp.wait_ge(stored3[1], 16 * (kvn // 2))
                for g in range(NGR):
                    w = min((128, 512, 2048)[g], SEQ)
                    sp.dma_start(o[f"kv_prompt_g{g + 1}"][0].rearrange("t c h d -> t c (h d)"), s["kv"][SEQ - w:SEQ, :, g, :]).then_inc(j3["kv_out"], 16)
                    sp.dma_start(o[f"kv_sample_g{g + 1}"].rearrange("b t c h d -> (b t) c (h d)"), s["kv"][SEQ:TOK, :, g, :]).then_inc(j3["kv_out"], 16)
                load_gain(sp, 3, a["norm_w"][1:2, :])

            blocks3(sp, body, between)
            sp.wait_ge(stored3[0], 16 * ((UNITS3 + 1) // 2))
            sp.wait_ge(stored3[1], 16 * (UNITS3 // 2))
            sp.wait_ge(j3["kv_out"], 16 * 2 * NGR)

        def section3_tensor(pe):
            meet(pe, 2)
            norm_tensor(pe, 2, split=True)
            pe.wait_ge(uT_ready, 2 * NT * 3)
            pe.wait_ge(uL_ready, NT)

            def body(i, b, m, tb):
                pe.wait_ge(j3["wl_ready"], turn_of(i, 2, b + 1))
                for t in range(NT):
                    cs = slice(min(t * P, TOK - P), min(t * P, TOK - P) + P)
                    if b or t > 2:
                        pe.wait_ge(j3["raw_ready"], turn_of(i, 2 * NT, b * NT + t - 2))
                    alone(pe)
                    for k in range(KT):
                        high, low = (x[:, k, cs] for x in (uH, uL))
                        whigh, wlow = (x[:, b % 2, k, :] for x in (wh, wl))
                        pe.matmul(bank[:, 4 + t % 3, :], high, whigh, start=(k == 0), stop=False)
                        pe.matmul(bank[:, 4 + t % 3, :], high, wlow, start=False, stop=False)
                        last = pe.matmul(bank[:, 4 + t % 3, :], low, whigh, start=False, stop=(k == KT - 1))
                    last.then_inc(j3["full"], 1)

            def between():
                norm_tensor(pe, 3, split=True)
                pe.wait_ge(uT_ready, 2 * NT * 4)
                pe.wait_ge(uL_ready, 2 * NT)

            blocks3(pe, body, between)

        def section3_scalar(act):
            meet(act, 2)
            norm_scalar(act, 2, split=True)
            split_weights(act, None, 0, True)

            def body(i, b, m, tb):
                for t in range(NT):
                    r = ROWS[t]
                    tok = bank[P - r:P, 4 + t % 3, :]
                    if t == SPLIT_AT and b + 1 < KVB + QB + GB:
                        split_weights(act, i, b + 1, True)
                    par = (b * NT + t) % 2
                    act.wait_ge(j3["full"], turn_of(i, 2 * NT, b * NT + t + 1))
                    if b or t > 1:
                        act.wait_ge(j3["rot_ready"], turn_of(i, 2 * NT, b * NT + t - 1))
                    if tb is None:
                        ins = act.activation(raws[0:r, par, :], tok, ACT.Silu)
                    elif tb == 2:
                        v = tok.rearrange("p (a r d) -> p a r d", a=2, d=HD)
                        act.copy(raws[0:r, par, :].rearrange("p (r a d) -> p a r d", a=2, d=HD), v)
                        ins = act.activation(sqr[0:r, par, :].rearrange("p (r a d) -> p a r d", a=2, d=HD), v, ACT.Square)
                    else:
                        ins = act.copy(raws[0:r, par, :], tok)
                        if m:
                            ins = act.activation(sqr[0:r, par, 0:m * HD], tok[:, 0:m * HD], ACT.Square)
                    ins.then_inc(j3["raw_ready"], 1)

            blocks3(act, body, lambda: norm_scalar(act, 3, squares=False, split=True))

        def section3_gpsimd(pool):
            meet(pool, 2)
            norm_gpsimd(pool, 2)
            count = 0
            for b, m in ((0, 8), (1, 4)):
                for t in range(NT):
                    count += 1
                    pool.wait_ge(j3["ms_ready"], count)
                    pool.tensor_tensor(hs3[0:ROWS[t], 2, 0:m], hs3[0:ROWS[t], 1, 0:m], mhalf[0:ROWS[t], 0:m], ALU.pow).then_inc(j3["r_ready"], 1)
            with pool.Fori(0, QB) as i:
                for t in range(NT):
                    pool.wait_ge(j3["ms_ready"], i * NT + (2 * NT + t + 1))
                    pool.tensor_tensor(hs3[0:ROWS[t], 2, :], hs3[0:ROWS[t], 1, :], mhalf[0:ROWS[t], 0:8], ALU.pow).then_inc(j3["r_ready"], 1)

        def section3_vector(dve, chain):
            meet(dve, 2)
            dve.wait_ge(j3["t_landed"], 64)
            half = HD // 2
            chain(dve.tensor_scalar(nw[:, 1, :], nw[:, 1, :], HD ** -0.5, None, ALU.mult))
            for tb in range(2):
                dve.tensor_tensor(tab[:, 2 * tb, :, :], rope[:, 0, :, :], over(nw[:, tb, :], P, NT, HD), ALU.mult)
                for x in range(2):
                    o_ = slice(x * half, (x + 1) * half)
                    i_ = slice((1 - x) * half, (2 - x) * half)
                    last = dve.tensor_tensor(tab[:, 2 * tb + 1, :, o_], rope[:, 1, :, o_], over(nw[:, tb, i_], P, NT, half), ALU.mult)
            last.then_inc(j3["tab_ready"], 1)
            dve.wait_ge(j3["tab_ready"], 1)
            norm_vector(dve, 2, split=True)
            split_weights(dve, None, 0, False)

            def body(i, b, m, tb):
                for t in range(NT):
                    r = ROWS[t]
                    if t == SPLIT_AT + 1 and b + 1 < KVB + QB + GB:
                        split_weights(dve, i, b + 1, False)
                    v0 = b * NT + t
                    par = v0 % 2
                    dve.wait_ge(j3["raw_ready"], turn_of(i, 2 * NT, v0 + 1))
                    if v0 > 1:
                        dve.wait_ge(stored3[par], turn_of(i, 16 * NT, 16 * (v0 // 2)))
                    if m:
                        hv = lambda x: x[0:r, 0:m * HD].rearrange("p (m d) -> p m d", m=m)
                        x, out, sw = hv(raws[:, par, :]), hv(rot[:, par, :]), hv(swp)
                        chain(dve.tensor_reduce(hs3[0:r, 0, 0:m], hv(sqr[:, par, :]), AX_X, ALU.add))
                        dve.tensor_scalar(hs3[0:r, 1, 0:m], hs3[0:r, 0, 0:m], 1.0 / HD, EPS, ALU.mult, ALU.add).then_inc(j3["ms_ready"], 1)
                        dve.tensor_tensor(out, x, over(tab[0:r, tb, t, :], r, m, HD), ALU.mult)
                        dve.tensor_tensor(sw[:, :, 0:half], x[:, :, half:], over(tab[0:r, tb + 1, t, 0:half], r, m, half), ALU.mult)
                        chain(dve.tensor_tensor(sw[:, :, half:], x[:, :, 0:half], over(tab[0:r, tb + 1, t, half:], r, m, half), ALU.mult))
                        chain(dve.tensor_tensor(out, out, sw, ALU.add))
                        nm = v0 if b < 2 else turn_of(i, 2 * NT, v0 - NT)
                        dve.wait_ge(j3["r_ready"], nm + 1)
                        ins = dve.tensor_tensor(out, out, bc(hs3[0:r, 2, 0:m], r, m, HD), ALU.mult)
                    if m < 8:
                        ins = dve.tensor_copy(rot[0:r, par, m * HD:], raws[0:r, par, m * HD:])
                    ins.then_inc(j3["rot_ready"], 1)
                    if m:
                        dve.wait_ge(j3["rot_ready"], turn_of(i, 2 * NT, v0 + 1))

            def between():
                kvn = KVB * NT
                dve.wait_ge(stored3[0], 16 * ((kvn + 1) // 2))
                dve.wait_ge(stored3[1], 16 * (kvn // 2))
                norm_vector(dve, 3, squares=False, split=True)

            for b in range(KVB):
                body(None, b, (8, 4, 0)[b], 0)
            between()
            with dve.Fori(0, QB // 2) as i:
                chain.enter(i, 3 * 2 * NT)
                for d in range(2):
                    body(i, KVB + d, 8, 2)
                chain.leave(QB // 2)
            for b in range(KVB + QB, KVB + QB + GB):
                body(None, b, 0, None)

        s4 = ExitStack()
        sb = sb_in(s4)
        HP = AH // 2
        UN = NGR * PT
        win = sb("win", [P, 2 * P])
        pair = sb("pair", [P, P])
        qn = sb("qn", [P, 2, D])
        kn = sb("kn", [P, 2, KVH * HD])
        vv = sb("vv", [P, 2, 2, KVH * HD])
        kT = sb("kT", [P, 2, KVH // 2, 2, P])
        qT = sb("qT", [P, 2, HP, 2, P])
        sc = sb("sc", [P, 4, 512])
        pT4 = sb("pT4", [P, 2, 512])
        mxs = sb("mxs", [P, 2, 2 * AH])
        nmx = sb("nmx", [P, 2, AH])
        ub = sb("ub", [P, 2, D])
        NTILE = 10
        NEW = NGR * DSEQ
        SW = P + NEW + 8 * P
        smask = sb("smask", [P, SW])
        ck = sb("ck", [P, 2, 9, 2 * KVH * HD])
        nk = sb("nk", [NEW, 2, 2 * KVH * HD])
        ssc = sb("ssc", [P, SW])
        pTs = sb("pTs", [P, NTILE, P])
        qTs = sb("qTs", [P, NGR, 2, P])
        osb = sb("osb", [P, 2, HD])
        st4 = sb("st4", [P, 8])
        qz = uT[:, :, :].rearrange("p k t -> p (k t)")[:, 0:NSEQ * NGR * 2 * P].rearrange("p (s g a d) -> p s g a d", s=NSEQ, g=NGR, a=2)
        qzs = sc[:, :, :].rearrange("p a n -> p (a n)")[:, 0:2 * NGR * 2 * P].rearrange("p (s g a d) -> p s g a d", s=2, g=NGR, a=2)
        kTs = uT[:, :, :].rearrange("p k t -> p (k t)")[:, NSEQ * NGR * 2 * P:NSEQ * NGR * 2 * P + 2 * SW].rearrange("p (a n) -> p a n", a=2)
        s4.close()
        f4 = {n: sem("att_" + n) for n in """m_landed s_full masked p_ready t_full pt_ready pv_done u_taken tr_full
            tr_ready kp_ready zeroed qz_landed os_stored qzs_ready
            ktr_full ktr_ready ss_full ss_masked se_ready rd_ready st_full spt_ready so_full so_ready schain""".split()}
        qk_landed = [sem(f"qk_landed{i}") for i in range(2)]
        v_landed = [sem(f"v_landed{i}") for i in range(2)]
        vp_landed = [sem(f"vp_landed{i}") for i in range(2)]
        ub_stored = [sem(f"ub_stored{i}") for i in range(2)]
        ck_landed = [sem(f"ck_landed{i}") for i in range(2)]

        OWN, FULL = 1, 2

        def head(j, x):
            return 2 * REP * (j // REP) + REP * x + j % REP

        def units4(eng, body):
            body(None, 0, OWN, None, 0)
            body(None, 1, FULL, OWN, 1)
            with eng.Fori(0, 3) as i:
                body(i, 2, FULL, FULL, 1)
                body(i, 3, FULL, FULL, 2)
            body(None, 8, OWN, FULL, 0)
            body(None, 9, FULL, OWN, 5)
            with eng.Fori(0, 3) as i:
                body(i, 10, OWN, FULL, 0)
                body(i, 11, FULL, OWN, 6)
            body(None, 16, OWN, FULL, 0)
            body(None, 17, OWN, OWN, 0)
            with eng.Fori(0, 2) as i:
                body(i, 18, OWN, OWN, 0)
                body(i, 19, OWN, OWN, 0)
            body(None, 22, OWN, OWN, 0)
            body(None, 23, OWN, OWN, 0)

        def sequences(eng, body):
            with eng.Fori(0, NSEQ // 2 - 1) as i:
                for d in range(2):
                    body(i, d)
            for d in (NSEQ - 2, NSEQ - 1):
                body(None, d)

        def rows4(table, i, un, hi):
            g = un // PT
            if g == 0:
                return table[bass.ds(turn_of(i, 2 * P, un * P + 64 * hi), 64), :]
            j = un - g * PT
            if g == 1:
                x = table[0:SEQ, :].rearrange("(p r) n -> r p n", r=4)
                res, at = turn_of(i, 1, j // 2), (j % 2) * P + 64 * hi
            else:
                x = table[0:SEQ, :].rearrange("(p r) n -> r p n", r=16)
                res, at = turn_of(i, 4, 2 * j + hi), 0
            return x[bass.ds(res, 1), at:at + 64, :].rearrange("r p n -> (r p) n")

        def section4_sync(sp):
            meet(sp, 3)
            for tile, name in ((win, "win"), (pair, "pair"), (smask, "smask")):
                at, w = LAYOUT[name]
                sp.dma_start(tile[:, :], a["consts"][:, at:at + w]).then_inc(f4["m_landed"], 16)

            def store(i, un):
                g, sl = un // PT, un % 2
                sp.wait_ge(f4["u_taken"], turn_of(i, 4, 2 * un + 2))
                alone(sp)
                for hi in range(2):
                    ps = slice(64 * hi, 64 * hi + 64)
                    sp.dma_start(rows4(s["u"][g], i, un, hi), ub[ps, sl, :]).then_inc(ub_stored[sl], 16)
                    sp.dma_start(rows4(s["ms"][g], i, un, hi), mxs[ps, sl, :]).then_inc(ub_stored[sl], 16)

            def body(i, un, kind, before, nth):
                g, sl = un // PT, un % 2
                if un > 1:
                    sp.wait_ge(f4["tr_full"], turn_of(i, 6, 3 * (un - 1)))
                alone(sp)
                for hi in range(2):
                    ps = slice(64 * hi, 64 * hi + 64)
                    sp.dma_start(qn[ps, sl, :], rows4(s["q"][:, g, :], i, un, hi)).then_inc(qk_landed[sl], 16)
                    sp.dma_start(kn[ps, sl, :], rows4(s["kv"][:, 0, g, :], i, un, hi)).then_inc(qk_landed[sl], 16)
                if un > 1:
                    sp.wait_ge(f4["pv_done"], turn_of(i, 16, 8 * (un - 1)))
                alone(sp)
                for hi in range(2):
                    ps = slice(64 * hi, 64 * hi + 64)
                    sp.dma_start(vv[ps, sl, 1, :], rows4(s["kv"][:, 1, g, :], i, un, hi)).then_inc(v_landed[sl], 16)
                    if kind == FULL:
                        sp.dma_start(vv[ps, sl, 0, :], rows4(s["kv"][:, 1, g, :], i, un - 1, hi)).then_inc(vp_landed[sl], 16)
                if un > 1:
                    store(i, un - 2)

            units4(sp, body)
            store(None, UN - 2)
            store(None, UN - 1)
            sp.wait_ge(f4["zeroed"], 3)
            for x in range(AH):
                kv = x // REP
                for g in range(NGR):
                    at = (x // (2 * REP) * 2 * REP + x % REP * 2 + kv % 2) * HD
                    src = s["q"][SEQ:TOK, g, at:at + HD].rearrange("(s t) d -> t s d", t=DSEQ)
                    sp.dma_start(qz[x * DSEQ:(x + 1) * DSEQ, :, g, kv // 2, (kv % 2) * HD:(kv % 2 + 1) * HD], src).then_inc(f4["qz_landed"], 16)
            caches = [a[f"cache_kv_g{g}"].rearrange("s t c h d -> s t (c h d)") for g in (1, 2, 3)]

            def load_sequence(i, d):
                sl, one = d % 2, bass.ds(turn_of(i, 2, d), 1)
                c1, c2, c3 = (c[one].rearrange("s t n -> (s t) n") for c in caches)
                sp.dma_start(ck[:, sl, 0, :], c1).then_inc(ck_landed[sl], 16)
                sp.dma_start(ck[:, sl, 1:5, :], c2.rearrange("(i r) n -> i r n", r=4)).then_inc(ck_landed[sl], 16)
                for hi in range(2):
                    sp.dma_start(ck[64 * hi:64 * hi + 64, sl, 5:9, :],
                                 c3.rearrange("(i r) n -> i r n", r=16)[:, hi:8:2, :]).then_inc(ck_landed[sl], 16)
                for g in range(NGR):
                    sp.dma_start(nk[g * DSEQ:(g + 1) * DSEQ, sl, :].rearrange("t (c n) -> t c n", c=2),
                                 s["kv"][bass.ds(turn_of(i, 2 * DSEQ, SEQ + d * DSEQ), DSEQ), :, g, :]).then_inc(ck_landed[sl], 16)

            load_sequence(None, 0)
            load_sequence(None, 1)

            def sample(i, d):
                if d < NSEQ - 2:
                    sp.wait_ge(f4["so_full"], turn_of(i, 2, d + 1))
                    alone(sp)
                    load_sequence(i, d + 2)
                sp.wait_ge(f4["so_ready"], turn_of(i, 2, d + 1))
                alone(sp)
                for x in range(AH):
                    sp.dma_start(s["os"][bass.ds(turn_of(i, 2 * DSEQ, d * DSEQ), DSEQ), x * HD:(x + 1) * HD],
                                 osb[x * DSEQ:(x + 1) * DSEQ, d % 2, :]).then_inc(f4["os_stored"], 16)

            sequences(sp, sample)
            sp.wait_ge(f4["os_stored"], 16 * AH * NSEQ)
            sp.wait_ge(ub_stored[0], 64 * (UN // 2))
            sp.wait_ge(ub_stored[1], 64 * (UN // 2))

        def section4_gpsimd(pool):
            meet(pool, 3)
            for x in range(2):
                other = slice(64 * (1 - x), 64 * (1 - x) + 64)
                pool.memset(qT[other, :, :, x, :], 0.0).then_inc(f4["zeroed"], 1)
                pool.wait_ge(f4["zeroed"], x + 1)
            pool.memset(qz, 0.0).then_inc(f4["zeroed"], 1)

            def body(i, un, kind, before, nth):
                if un < UN - 1:
                    nx = un + 1
                    pool.wait_ge(f4["tr_ready"], turn_of(i, 6, 3 * un + 1))
                    pool.wait_ge(f4["s_full"], turn_of(i, 32, 16 * un))
                    alone(pool)
                    pool.tensor_copy(kT[:, nx % 2, :, 0, :], kT[:, un % 2, :, 1, :]).then_inc(f4["kp_ready"], 1)

            units4(pool, body)
            pool.wait_ge(f4["qz_landed"], 16 * AH * NGR)
            pool.wait_ge(f4["t_full"], HP * UN)

            def pick(i, d):
                if d > 1 or i is not None:
                    pool.wait_ge(f4["ktr_full"], turn_of(i, 14, 7 * max(0, d - 1)))
                alone(pool)
                pool.tensor_copy(qzs[:, d % 2, :, :, :], qz[:, bass.ds(turn_of(i, 2, d), 1), :, :, :].rearrange("p s g a d -> p (s g) a d")).then_inc(f4["qzs_ready"], 1)

            sequences(pool, pick)

        def section4_scalar(act):
            meet(act, 3)

            def take(i, un, part):
                sl = un % 2
                act.wait_ge(f4["tr_full"], turn_of(i, 6, 3 * un + part + 1))
                if part == 0:
                    if un:
                        act.wait_ge(f4["kp_ready"], turn_of(i, 2, un - 1))
                    act.copy(kT[:, sl, :, 1, :], bank[:, 7, 0:2 * P].rearrange("p (h n) -> p h n", h=2)).then_inc(f4["tr_ready"], 1)
                else:
                    for x in range(2):
                        hs_ = slice(64 * x, 64 * x + 64)
                        last = act.copy(qT[hs_, sl, 4 * (part - 1):4 * part, x, :], bank[hs_, 7, :].rearrange("p (h n) -> p h n", h=4))
                    last.then_inc(f4["tr_ready"], 1)

            def hand_out(i, un, part):
                sl = un % 2
                act.wait_ge(f4["pv_done"], turn_of(i, 16, 8 * un + 4 * (part + 1)))
                if un > 1 and part == 0:
                    act.wait_ge(ub_stored[sl], turn_of(i, 64, 64 * (un // 2)))
                act.copy(ub[:, sl, part * 512:(part + 1) * 512], bank[:, 4 + part, :]).then_inc(f4["u_taken"], 1)

            act.wait_ge(f4["zeroed"], 2)
            for part in range(3):
                take(None, 0, part)

            def body(i, un, kind, before, nth):
                sl = un % 2
                n = kind * P
                for j in range(HP):
                    st0 = HP * un + j
                    if j in (2, 4, 6) and un < UN - 1:
                        take(i, un + 1, j // 2 - 1)
                    if j == 3 and un:
                        hand_out(i, un - 1, 1)
                    if j == 7:
                        hand_out(i, un, 0)
                    act.wait_ge(f4["masked"], turn_of(i, 16, st0 + 1))
                    if j == 0 and un > 1:
                        act.wait_ge(ub_stored[sl], turn_of(i, 64, 64 * (un // 2)))
                    for x in range(2):
                        v = sc[:, st0 % 4, 256 * x:256 * x + n]
                        last = act.activation(v, v, ACT.Exp, bias=nmx[:, sl, head(j, x):head(j, x) + 1],
                                              accum_out=mxs[:, sl, AH + head(j, x):AH + head(j, x) + 1])
                    last.then_inc(f4["p_ready"], 1)

            units4(act, body)
            hand_out(None, UN - 1, 1)

            def turned(i, d, k):
                act.wait_ge(f4["ktr_full"], turn_of(i, 14, 7 * d + k + 1))
                b = bank[:, 6 + (7 * d + k) % 2, :]
                if k < 5:
                    kTs_copy(act, k, b)
                elif k == 5:
                    act.copy(qTs[:, 0:2, :, :].rearrange("p g a n -> p (g a) n"), b.rearrange("p (x n) -> p x n", x=4)).then_inc(f4["ktr_ready"], 1)
                else:
                    act.copy(qTs[:, 2, :, :], b[:, 0:2 * P].rearrange("p (x n) -> p x n", x=2)).then_inc(f4["ktr_ready"], 1)

            def kTs_copy(act, k, b):
                if k < 4:
                    at = P + NEW + 2 * k * P
                    act.copy(kTs[:, :, at:at + 2 * P], b.rearrange("p (a n) -> p a n", a=2)).then_inc(f4["ktr_ready"], 1)
                else:
                    act.copy(kTs[:, :, 0:P + NEW], b.rearrange("p (a n) -> p a n", a=2)[:, :, 0:P + NEW]).then_inc(f4["ktr_ready"], 1)

            for k in range(7):
                turned(None, 0, k)

            def sample(i, d):
                act.wait_ge(f4["ss_masked"], turn_of(i, 2, d + 1))
                act.activation(ssc[:, :], ssc[:, :], ACT.Exp, bias=st4[:, 4:5], accum_out=st4[:, 5:6]).then_inc(f4["se_ready"], 1)
                if d < NSEQ - 1:
                    for k in range(7):
                        turned(i, d + 1, k)
                act.wait_ge(f4["rd_ready"], turn_of(i, 2, d + 1))
                act.wait_ge(f4["so_full"], turn_of(i, 2, d + 1))
                act.wait_ge(f4["os_stored"], turn_of(i, 32 * AH, 16 * AH * d))
                for kv in range(KVH):
                    ps = slice(32 * kv, 32 * kv + 32)
                    last = act.activation(osb[ps, d % 2, :], bank[ps, 0, kv * HD:(kv + 1) * HD], ACT.Copy, scale=st4[ps, 6:7])
                last.then_inc(f4["so_ready"], 1)

            sequences(act, sample)

        def section4_vector(dve, chain):
            meet(dve, 3)
            dve.wait_ge(f4["m_landed"], 48)

            def evacuate(i, st0, kind):
                dve.wait_ge(f4["t_full"], turn_of(i, 16, st0 + 1))
                if st0 > 1:
                    dve.wait_ge(f4["pv_done"], turn_of(i, 16, st0 - 1))
                dve.tensor_copy(pT4[:, st0 % 2, 0:2 * kind * P], bank[:, 6, 0:2 * kind * P]).then_inc(f4["pt_ready"], 1)

            state = {}

            def body(i, un, kind, before, nth):
                sl, n = un % 2, kind * P
                mask = pair[:, :] if un >= 2 * PT else win[:, 2 * P - n:2 * P]
                if i is not None and un % 2 == 0:
                    chain.enter(i, 2 * HP)
                for j in range(HP):
                    st0 = HP * un + j
                    dve.wait_ge(f4["s_full"], turn_of(i, 32, 2 * (st0 + 1)))
                    if st0 > 3:
                        dve.wait_ge(f4["t_full"], turn_of(i, 16, st0 - 3))
                    if j == 0 and un > 1:
                        dve.wait_ge(ub_stored[sl], turn_of(i, 64, 64 * (un // 2)))
                    alone(dve)
                    for x in range(2):
                        last = dve.tensor_tensor_reduce(sc[:, st0 % 4, 256 * x:256 * x + n], bank[:, 2 * (st0 % 2) + x, 0:n], mask,
                                                        1.0, -3e38, ALU.add, ALU.max, mxs[:, sl, head(j, x):head(j, x) + 1])
                    chain(last)
                    two = slice(head(j, 0), head(j, 1) + 1, REP)
                    dve.tensor_scalar(nmx[:, sl, two], mxs[:, sl, two], -1.0, None, ALU.mult).then_inc(f4["masked"], 1)
                    if st0 > 1:
                        evacuate(i, st0 - 2, kind if j > 1 else before)
                if i is not None and un % 2 == 1:
                    chain.leave({3: 3, 11: 3, 19: 2}[un])

            units4(dve, body)
            evacuate(None, HP * UN - 2, OWN)
            evacuate(None, HP * UN - 1, OWN)

            def sample(i, d):
                dve.wait_ge(f4["ss_full"], turn_of(i, 2, d + 1))
                dve.wait_ge(f4["st_full"], turn_of(i, 6, 3 * d))
                dve.wait_ge(f4["so_ready"], turn_of(i, 2, d))
                alone(dve)
                for b, (c0, c1) in enumerate(((0, P + NEW), (P + NEW, P + NEW + 512), (P + NEW + 512, SW))):
                    last = dve.tensor_tensor_reduce(ssc[:, c0:c1], bank[:, b, 0:c1 - c0], smask[:, c0:c1], 1.0, -3e38,
                                                    ALU.add, ALU.max, st4[:, b:b + 1])
                last.then_inc(f4["schain"], 1)
                dve.wait_ge(f4["schain"], turn_of(i, 4, 2 * d + 1))
                dve.tensor_reduce(st4[:, 3:4], st4[:, 0:3], AX_X, ALU.max).then_inc(f4["schain"], 1)
                dve.wait_ge(f4["schain"], turn_of(i, 4, 2 * d + 2))
                dve.tensor_scalar(st4[:, 4:5], st4[:, 3:4], -1.0, None, ALU.mult).then_inc(f4["ss_masked"], 1)
                dve.wait_ge(f4["se_ready"], turn_of(i, 2, d + 1))
                dve.reciprocal(st4[:, 6:7], st4[:, 5:6]).then_inc(f4["rd_ready"], 1)
                for b in range(3):
                    dve.wait_ge(f4["st_full"], turn_of(i, 6, 3 * d + b + 1))
                    dve.wait_ge(f4["so_full"], turn_of(i, 2, d))
                    if b < 2:
                        ins = dve.tensor_copy(pTs[:, 2 + 4 * b:6 + 4 * b, :].rearrange("p x n -> p (x n)"), bank[:, 3 + b, :])
                    else:
                        dve.tensor_copy(pTs[:, 0, :], bank[:, 5, 0:P])
                        ins = dve.tensor_copy(pTs[0:NEW, 1, :], bank[0:NEW, 5, P:2 * P])
                    ins.then_inc(f4["spt_ready"], 1)

            sequences(dve, sample)

        def section4_tensor(pe):
            meet(pe, 3)

            def turn(i, un, part):
                sl = un % 2
                if part == 0:
                    pe.wait_ge(qk_landed[sl], turn_of(i, 64, 64 * (un // 2 + 1)))
                if un or part:
                    pe.wait_ge(f4["tr_ready"], turn_of(i, 6, 3 * un + part))
                if part == 0:
                    for x in range(KVH // 2):
                        last = pe.transpose(bank[:, 7, x * P:(x + 1) * P], kn[:, sl, x * P:(x + 1) * P], ident)
                else:
                    for x in range(REP):
                        f = REP * (part - 1) + x
                        last = pe.transpose(bank[:, 7, x * P:(x + 1) * P], qn[:, sl, f * P:(f + 1) * P], ident)
                last.then_inc(f4["tr_full"], 1)

            def turn_scores(i, st0, kind):
                pe.wait_ge(f4["p_ready"], turn_of(i, 16, st0 + 1))
                if st0 > 0:
                    pe.wait_ge(f4["pt_ready"], turn_of(i, 16, st0))
                for x in range(2):
                    for k in range(kind):
                        last = pe.transpose(bank[:, 6, (x * kind + k) * P:(x * kind + k + 1) * P],
                                            sc[:, st0 % 4, 256 * x + k * P:256 * x + (k + 1) * P], ident)
                last.then_inc(f4["t_full"], 1)

            def values(i, un, j, kind, nth):
                st0 = HP * un + j
                sl = un % 2
                pe.wait_ge(f4["pt_ready"], turn_of(i, 16, st0 + 1))
                if j == 0:
                    pe.wait_ge(v_landed[sl], turn_of(i, 32, 32 * (un // 2 + 1)))
                    if kind == FULL:
                        pe.wait_ge(vp_landed[sl], turn_of(i, 32, 32 * nth))
                if j in (0, 4) and un:
                    pe.wait_ge(f4["u_taken"], turn_of(i, 4, 2 * un - 1 + j // 4))
                for x in range(2):
                    hd = head(j, x)
                    for k in range(kind):
                        last = pe.matmul(bank[:, 4 + hd // 8, (hd % 8) * HD:(hd % 8 + 1) * HD],
                                         pT4[:, st0 % 2, (x * kind + k) * P:(x * kind + k + 1) * P],
                                         vv[:, sl, k + 2 - kind, (hd // REP) * HD:(hd // REP + 1) * HD], start=(k == 0), stop=(k == kind - 1))
                last.then_inc(f4["pv_done"], 1)

            for part in range(3):
                turn(None, 0, part)

            def body(i, un, kind, before, nth):
                sl, n = un % 2, kind * P
                pe.wait_ge(f4["tr_ready"], turn_of(i, 6, 3 * (un + 1)))
                if un:
                    pe.wait_ge(f4["kp_ready"], turn_of(i, 2, un))
                for j in range(HP):
                    st0 = HP * un + j
                    if st0 > 1:
                        pe.wait_ge(f4["masked"], turn_of(i, 16, st0 - 1))
                    for x in range(2):
                        pe.matmul(bank[:, 2 * (st0 % 2) + x, 0:n], qT[:, sl, j, x, :],
                                  kT[:, sl, j // REP, 2 - kind:2, :].rearrange("p a n -> p (a n)"), start=True, stop=True).then_inc(f4["s_full"], 1)
                    if st0 > 1:
                        turn_scores(i, st0 - 2, kind if j > 1 else before)
                    if st0 > 2:
                        if j > 2:
                            values(i, un, j - 3, kind, nth)
                        else:
                            values(i, un - 1, j + HP - 3, before, 0)
                    if j in (1, 3, 5) and un < UN - 1:
                        turn(i, un + 1, j // 2)

            units4(pe, body)
            turn_scores(None, HP * UN - 2, OWN)
            values(None, UN - 1, HP - 3, OWN, 0)
            turn_scores(None, HP * UN - 1, OWN)
            values(None, UN - 1, HP - 2, OWN, 0)
            values(None, UN - 1, HP - 1, OWN, 0)

            def turn_keys(i, d):
                sl = d % 2
                pe.wait_ge(ck_landed[sl], turn_of(i, 112, 112 * (d // 2 + 1)))
                for k in range(7):
                    n0 = 7 * d + k
                    if n0 > 1:
                        pe.wait_ge(f4["ktr_ready"], turn_of(i, 14, n0 - 1))
                    b = bank[:, 6 + n0 % 2, :]
                    if k < 4:
                        for x in range(2):
                            for pr in range(2):
                                last = pe.transpose(b[:, (2 * pr + x) * P:(2 * pr + x + 1) * P], ck[:, sl, 1 + 2 * k + x, pr * P:(pr + 1) * P], ident)
                    elif k == 4:
                        for pr in range(2):
                            pe.transpose(b[:, 2 * pr * P:(2 * pr + 1) * P], ck[:, sl, 0, pr * P:(pr + 1) * P], ident)
                            last = pe.transpose(b[:, (2 * pr + 1) * P:(2 * pr + 1) * P + NEW], nk[:, sl, pr * P:(pr + 1) * P], ident[0:NEW, 0:NEW])
                    else:
                        if k == 5:
                            pe.wait_ge(f4["qzs_ready"], turn_of(i, 2, d + 1))
                        for x in range(4 if k == 5 else 2):
                            g = 2 * (k - 5) + x // 2
                            last = pe.transpose(b[:, x * P:(x + 1) * P], qzs[:, sl, g, x % 2, :], ident)
                    last.then_inc(f4["ktr_full"], 1)

            def sample(i, d):
                sl = d % 2
                pe.wait_ge(f4["ktr_ready"], turn_of(i, 14, 7 * (d + 1)))
                pe.wait_ge(f4["so_ready"], turn_of(i, 2, d))
                pe.wait_ge(f4["ss_masked"], turn_of(i, 2, d))
                new = [(g, 0, P + g * DSEQ, P + (g + 1) * DSEQ, P + g * DSEQ) for g in range(NGR)]
                for g, b, c0, c1, at in [(0, 0, 0, P, 0)] + new + [(1, 1, P + NEW, P + NEW + 512, 0), (2, 2, P + NEW + 512, SW, 0)]:
                    for pr in range(2):
                        last = pe.matmul(bank[:, b, at:at + c1 - c0], qTs[:, g, pr, :], kTs[:, pr, c0:c1], start=(pr == 0), stop=(pr == 1))
                last.then_inc(f4["ss_full"], 1)
                if d < NSEQ - 1:
                    turn_keys(i, d + 1)
                pe.wait_ge(f4["se_ready"], turn_of(i, 2, d + 1))
                pe.wait_ge(f4["spt_ready"], turn_of(i, 6, 3 * d))
                for b in range(2):
                    for x in range(4):
                        at = P + NEW + (4 * b + x) * P
                        last = pe.transpose(bank[:, 3 + b, x * P:(x + 1) * P], ssc[:, at:at + P], ident)
                    last.then_inc(f4["st_full"], 1)
                pe.transpose(bank[:, 5, 0:P], ssc[:, 0:P], ident)
                pe.transpose(bank[0:NEW, 5, P:2 * P], ssc[:, P:P + NEW], ident).then_inc(f4["st_full"], 1)
                pe.wait_ge(f4["spt_ready"], turn_of(i, 6, 3 * (d + 1)))
                vals = [ck[:, sl, 0, KVH * HD:]] + [nk[:, sl, KVH * HD:]] + [ck[:, sl, 1 + x, KVH * HD:] for x in range(8)]
                for x, v in enumerate(vals):
                    r = NEW if x == 1 else P
                    last = pe.matmul(bank[:, 0, 0:KVH * HD], pTs[0:r, x, :], v, start=(x == 0), stop=(x == NTILE - 1))
                last.then_inc(f4["so_full"], 1)

            turn_keys(None, 0)
            sequences(pe, sample)

        s5 = ExitStack()
        sb = sb_in(s5)
        same = ExitStack()
        wo5 = sb_in(same)("wo5", [P, KT, D])
        same.close()
        wl5 = sb("wl5", [P, KT, D], FR)
        wh5 = uH[:, :, 0:D]
        u3 = sb("u3", [P, 2, NGR, D])
        m3 = sb("m3", [P, 2, NGR, 2 * AH])
        gate = sb("gate", [P, 2, D])
        wts = sb("wts", [P, 5, NGR, AH])
        y5 = sb("y5", [P, 2, D])
        yT5 = sb("yT5", [P, 2, 2, KT, P], FR)
        s5.close()
        f5 = {n: sem("last_" + n) for n in """w_landed e_in e_ready w_ready third y_ready t_full t_ready
            full added wh_ready wl_ready low_ready""".split()}
        in5 = [sem(f"in5_{i}") for i in range(2)]

        def tiles5(eng, body):
            with eng.Fori(0, PT // 2) as i:
                for t in range(2):
                    body(i, t)
            body(None, PT)

        def section5_sync(sp):
            meet(sp, 4)
            ow = a["a_out_w"][0].rearrange("(k p) n -> p k n", p=P)
            sp.dma_start(wo5[:, :, :], ow).then_inc(f5["w_landed"], 16)

            def body(i, t):
                sl, r = t % 2, ROWS[t]
                rows = bass.ds(turn_of(i, 2 * P, t * P), r)
                sp.wait_ge(f5["y_ready"], turn_of(i, 2, t + 1))
                alone(sp)
                sp.dma_start(gate[0:r, sl, :], s["gate"][rows, :]).then_inc(in5[sl], 16)
                if t < PT:
                    for g in range(NGR):
                        sp.dma_start(u3[:, sl, g, :], s["u"][g][rows, :]).then_inc(in5[sl], 16)
                        sp.dma_start(m3[:, sl, g, :], s["ms"][g][rows, :]).then_inc(in5[sl], 16)
                else:
                    sp.wait_ge(f5["t_full"], PT - 1)
                    sp.dma_start(y5[0:r, sl, :], s["os"]).then_inc(in5[sl], 16)

            tiles5(sp, body)

        def section5_gpsimd(pool):
            meet(pool, 4)

            def body(i, t):
                if t == PT:
                    return
                pool.wait_ge(f5["w_ready"], turn_of(i, 2, t + 1))
                v = u3[:, t % 2, 2, :].rearrange("p (h d) -> p h d", h=AH)
                pool.tensor_tensor(v, v, bc(wts[:, 4, 2, :], P, AH, HD), ALU.mult).then_inc(f5["third"], 1)

            tiles5(pool, body)

        def section5_scalar(act):
            meet(act, 4)

            act.wait_ge(f5["w_landed"], 16)
            act.copy(wh5, wo5[:, :, :]).then_inc(f5["wh_ready"], 1)

            def body(i, t):
                sl, r = t % 2, ROWS[t]
                if t < PT:
                    act.wait_ge(f5["e_in"], turn_of(i, 2, t + 1))
                    act.activation(wts[:, 1, :, :], wts[:, 0, :, :], ACT.Exp).then_inc(f5["e_ready"], 1)
                act.wait_ge(f5["t_full"], turn_of(i, 2, t + 1))
                for half in range(2):
                    b = bank[:, 2 * sl + half, :].rearrange("p (k n) -> p k n", k=4)[:, :, 0:r]
                    last = act.copy(yT5[:, sl, 0, 4 * half:4 * half + 4, 0:r], b)
                last.then_inc(f5["t_ready"], 1)

            tiles5(act, body)

        def section5_vector(dve, chain):
            meet(dve, 4)

            def low_part(i, t):
                sl, r = t % 2, ROWS[t]
                dve.wait_ge(f5["t_ready"], turn_of(i, 2, t + 1))
                for half in range(2):
                    b = bank[:, 2 * sl + half, :].rearrange("p (k n) -> p k n", k=4)[:, :, 0:r]
                    part = slice(4 * half, 4 * half + 4)
                    last = dve.tensor_tensor(yT5[:, sl, 1, part, 0:r], b, yT5[:, sl, 0, part, 0:r].bitcast(F32), ALU.subtract)
                last.then_inc(f5["low_ready"], 1)

            def finish(i, t):
                sl, r = t % 2, ROWS[t]
                dve.wait_ge(f5["full"], turn_of(i, 2, t + 1))
                for half in range(2):
                    hv = h[0:r, bass.ds(turn_of(i, 2, t), 1), 512 * half:512 * (half + 1)].rearrange("p t n -> p (t n)")
                    last = dve.tensor_tensor(hv, hv, bank[0:r, 4 + 2 * sl + half, :], ALU.add)
                last.then_inc(f5["added"], 1)

            def body(i, t):
                sl, r = t % 2, ROWS[t]
                if t == PT:
                    dve.wait_ge(in5[0], 16 * 7 * (PT // 2) + 32)
                    dve.tensor_tensor(y5[0:r, sl, :], y5[0:r, sl, :], gate[0:r, sl, :], ALU.mult).then_inc(f5["y_ready"], 1)
                else:
                    dve.wait_ge(in5[sl], turn_of(i, 112, 112 * (t // 2 + 1)))
                    mx = lambda g: m3[:, sl, g, 0:AH]
                    top = wts[:, 2, 0, :]
                    chain(dve.tensor_tensor(top, mx(0), mx(1), ALU.max))
                    chain(dve.tensor_tensor(top, top, mx(2), ALU.max))
                    dve.tensor_tensor(wts[:, 0, :, :], m3[:, sl, :, 0:AH], over(top, P, NGR, AH), ALU.subtract).then_inc(f5["e_in"], 1)
                    dve.wait_ge(f5["e_ready"], turn_of(i, 2, t + 1))
                    chain(dve.tensor_tensor(wts[:, 3, :, :], wts[:, 1, :, :], m3[:, sl, :, AH:], ALU.mult))
                    chain(dve.tensor_tensor(top, wts[:, 3, 0, :], wts[:, 3, 1, :], ALU.add))
                    chain(dve.tensor_tensor(top, top, wts[:, 3, 2, :], ALU.add))
                    chain(dve.reciprocal(top, top))
                    dve.wait_ge(f5["third"], turn_of(i, 2, t))
                    dve.tensor_tensor(wts[:, 4, :, :], wts[:, 1, :, :], over(top, P, NGR, AH), ALU.mult).then_inc(f5["w_ready"], 1)
                    dve.wait_ge(f5["w_ready"], turn_of(i, 2, t + 1))
                    uv = lambda g: u3[:, sl, g, :].rearrange("p (h d) -> p h d", h=AH)
                    yv = y5[:, sl, :]
                    if t > 1 or i is not None:
                        dve.wait_ge(f5["t_full"], turn_of(i, 2, t - 1))
                    dve.tensor_tensor(yv.rearrange("p (h d) -> p h d", h=AH), uv(0), bc(wts[:, 4, 0, :], P, AH, HD), ALU.mult)
                    chain(dve.tensor_tensor(uv(1), uv(1), bc(wts[:, 4, 1, :], P, AH, HD), ALU.mult))
                    chain(dve.tensor_tensor(yv, yv, u3[:, sl, 1, :], ALU.add))
                    dve.wait_ge(f5["third"], turn_of(i, 2, t + 1))
                    chain(dve.tensor_tensor(yv, yv, u3[:, sl, 2, :], ALU.add))
                    dve.tensor_tensor(yv, yv, gate[:, sl, :], ALU.mult).then_inc(f5["y_ready"], 1)

            def step(i, t):
                low_part(i, t)
                if t < PT:
                    body(i, t + 1)
                finish(i, t)

            dve.sem_inc(f5["y_ready"], 2)
            body(None, 0)
            dve.wait_ge(f5["wh_ready"], 1)
            dve.tensor_tensor(wl5[:, :, :], wo5[:, :, :], wh5.bitcast(F32), ALU.subtract).then_inc(f5["wl_ready"], 1)
            with dve.Fori(0, PT // 2 - 1) as i:
                chain.enter(i, 18)
                step(i, 0)
                step(i, 1)
                chain.leave(PT // 2 - 1)
            for t in range(PT - 2, NT):
                step(None, t)

        def section5_tensor(pe):
            meet(pe, 4)

            def body(i, t):
                sl, r = t % 2, ROWS[t]
                pe.wait_ge(f5["y_ready"], turn_of(i, 2, t + 3))
                pe.wait_ge(f5["t_ready"], turn_of(i, 2, max(0, t - 1)))
                for f in range(KT):
                    last = pe.transpose(bank[:, 2 * sl + f // 4, (f % 4) * P:(f % 4) * P + r], y5[0:r, sl, f * P:(f + 1) * P], ident[0:r, 0:r])
                last.then_inc(f5["t_full"], 1)
                pe.wait_ge(f5["low_ready"], turn_of(i, 2, t + 1))
                if t == 0:
                    pe.wait_ge(f5["wl_ready"], 1)
                pe.wait_ge(f5["added"], turn_of(i, 2, 0) if t < 2 else PT)
                for half in range(2):
                    for k in range(KT):
                        high, low = (yT5[:, sl, x, k, :] for x in range(2))
                        whigh, wlow = (x[:, k, 512 * half:512 * (half + 1)] for x in (wh5, wl5))
                        pe.matmul(bank[:, 4 + 2 * sl + half, :], high, whigh, start=(k == 0), stop=False)
                        pe.matmul(bank[:, 4 + 2 * sl + half, :], high, wlow, start=False, stop=False)
                        last = pe.matmul(bank[:, 4 + 2 * sl + half, :], low, whigh, start=False, stop=(k == KT - 1))
                last.then_inc(f5["full"], 1)

            tiles5(pe, body)


        @block.sync
        def _(sp):
            sp.dma_start(h[:, 0:PT, :], a["x_prompt"][0].rearrange("(t p) d -> p t d", p=P)).then_inc(q["res_loaded"], 16)
            sp.dma_start(h[0:SAMP, PT, :], a["x_sample"].rearrange("b t d -> (b t) d")).then_inc(q["res_loaded"], 16)
            load_gain(sp, 0, a["norm_w"][0:1, :])
            sp.dma_start(cst[:, :], a["consts"][:, 0:NMASK]).then_inc(q["const_loaded"], 16)
            sp.dma_start(wdt[:, :, :], in_w[:, :, DTCOL:DTCOL + NH]).then_inc(q["wdt_loaded"], 16)
            for j, n in enumerate(("m_dt_bias", "m_A_log", "m_D")):
                sp.dma_start(vec[:, j * NH:(j + 1) * NH], a[n].broadcast_to([P, NH])).then_inc(q["vec_loaded"], 16)
            sp.dma_start(cw_rows[0:CK * CONVF, :], a["m_conv_w"][0].rearrange("k (f p) -> (k f) p", p=P)).then_inc(q["cw_loaded"], 16)
            sp.dma_start(cw_rows[CK * CONVF:(CK + 1) * CONVF, :], a["m_conv_b"][0].rearrange("(f p) -> f p", p=P)).then_inc(q["cw_loaded"], 16)
            sp.dma_start(sc_rows, a["state_conv"].rearrange("x s k (c n) -> (x s k) c n", c=3)).then_inc(q["cw_loaded"], 16)
            with sp.Fori(0, NG) as g:
                for f in range(CF):
                    col = [g * GW + XCOL + f * P, g * DS + BCOL, g * DS + CCOL][max(0, f - XF + 1)]
                    sp.wait_ge(q["xg_full"], g * CF + max(0, f - 1))
                    alone(sp)
                    sp.dma_start(wx[:, f % 2, :, :], in_w[:, :, bass.ds(col, P)]).then_inc(wx_landed[f % 2], 16)
                    if f == 2:
                        sp.wait_ge(q["z_full"], g * NT)
                        alone(sp)
                        sp.dma_start(wz[:, :, :], in_w[:, :, bass.ds(g * GW, GW)]).then_inc(q["wz_landed"], 16)
                        sp.wait_ge(q["out_full"], g * 2 * NT)
                        alone(sp)
                        sp.dma_start(wo[:, :, :], out_w[:, bass.ds(g * XF, XF), :]).then_inc(q["wo_landed"], 16)
                        sp.wait_ge(q["yn_ready"], g * NT)
                        alone(sp)
                        sp.dma_start(nwg[:, :], a["m_norm_w"][:, bass.ds(g * GW, GW)].broadcast_to([P, GW])).then_inc(q["nw_landed"], 16)

                def load_state(n):
                    sp.dma_start(st[:, n % 4, :, :],
                                 st_in[bass.ds(g * GW, GW), n, :].rearrange("(f p) n -> p f n", p=P)).then_inc(st_landed[n % 4], 16)

                for n in range(4):
                    load_state(n)
                for n in range(NSEQ):
                    sp.wait_ge(q["snew_ready"], g * NSEQ + n + 1)
                    alone(sp)
                    sp.dma_start(st_out[bass.ds(g * GW, GW), n, :].rearrange("(f p) n -> p f n", p=P),
                                 st[:, n % 4, :, :]).then_inc(q["state_stored"], 16)
                    if n + 4 < NSEQ:
                        sp.wait_ge(q["state_stored"], g * (16 * NSEQ) + 16 * (n + 1))
                        alone(sp)
                        load_state(n + 4)
                sp.wait_ge(q["fin_ready"], g + 1)
                alone(sp)
                sp.wait_ge(q["state_stored"], g * (16 * NSEQ) + 16 * NSEQ)
                alone(sp)
                sp.dma_start(st_prompt[bass.ds(g * GW, GW), :].rearrange("(f p) n -> p f n", p=P),
                             h0T[:, 0, :].rearrange("p (f n) -> p f n", f=XF)).then_inc(q["fin_stored"], 16)
            sp.wait_ge(q["fin_stored"], 16 * NG)
            sp.wait_ge(q["tail_ready"], CONVF // 4)
            sp.dma_start(o["conv_prompt"].rearrange("x b k (c n) -> (x b k) c n", c=3), tail_rows[0:CK - 1, :, :]).then_inc(q["fin_stored"], 16)
            sp.dma_start(o["conv_sample"].rearrange("x s k (c n) -> (x s k) c n", c=3), tail_rows[CK - 1:TAIL, :, :]).then_inc(q["fin_stored"], 16)
            sp.wait_ge(q["fin_stored"], 16 * NG + 32)
            ple_sync(sp, 0, 1, False)
            section3_sync(sp)
            section4_sync(sp)
            section5_sync(sp)
            ple_sync(sp, 1, 4, True)

        @block.gpsimd
        def _(pool):
            pool.memset(mhalf[:, :], -0.5).then_inc(q["memset_done"], 1)
            pool.memset(ss[:, :], 1.0).then_inc(q["memset_done"], 1)
            pool.memset(ones[:, :], 1.0).then_inc(q["memset_done"], 1)
            pool.memset(raw[:, :, 0:CK - 1], 0.0).then_inc(q["memset_done"], 1)
            pool.wait_ge(q["memset_done"], 4)
            norm_gpsimd(pool, 0)
            pool.wait_ge(q["dt_ready"], 2)
            pool.wait_ge(q["const_loaded"], 16)
            pool.wait_ge(q["vec_loaded"], 48)

            def decay_sums(g, c, n):
                r = ROWS[c]
                alone(pool)
                tri = con("tri" if c < LC else "tri8", r)[:, 0:r]
                out = mix[0:r, c % 2, 0:HG * r].rearrange("p (h l) -> p h l", h=HG)
                pool.tensor_tensor(out, over(tri, r, HG, r), bc(dta[0:r, c, bass.ds(g * HG, HG)], r, HG, r),
                                   ALU.mult).then_inc(q["sum_ready"], 1)

            with pool.Fori(0, NG) as g:
                for c in range(NT):
                    n = g * NT + c
                    r = ROWS[c]
                    if c == 0:
                        pool.wait_ge(q["yd_full"], n)
                        decay_sums(g, 0, n)
                    v = xt[0:r, :].rearrange("p (h d) -> p h d", h=HG)
                    pool.wait_ge(q["xdt_ready"], n + 1)
                    alone(pool)
                    pool.tensor_tensor(v, v,
                                       bc(vec[0:r, bass.ds(g * HG + 2 * NH, HG)], r, HG, HD), ALU.mult).then_inc(q["skip_ready"], 1)
                    if c:
                        pool.wait_ge(q["st_full"], g * LC + c)
                    else:
                        pool.wait_ge(q["snew_full"], g * NSEQ)
                    alone(pool)
                    pool.tensor_tensor(xdtd[0:r, :].rearrange("p (h d) -> p h d", h=HG),
                                       xdt[0:r, :].rearrange("p (h d) -> p h d", h=HG),
                                       bc(dend[0:r, c, bass.ds(g * HG, HG)], r, HG, HD), ALU.mult).then_inc(q["xdtd_ready"], 1)
                    if c + 1 < NT:
                        if c:
                            pool.wait_ge(q["yd_full"], n)
                        decay_sums(g, c + 1, n + 1)
                    pool.wait_ge(q["msy_ready"], n + 1)
                    pool.tensor_tensor(ybuf[0:r, 2:3], ybuf[0:r, 1:2], mhalf[0:r, 0:1], ALU.pow).then_inc(q["ry_ready"], 1)
            ple_gpsimd(pool, 0, 1)
            section3_gpsimd(pool)
            section4_gpsimd(pool)
            section5_gpsimd(pool)
            ple_gpsimd(pool, 1, 4)

        @block.scalar
        def _(act):
            act.wait_ge(q["memset_done"], 4)
            act.wait_ge(q["res_loaded"], 32)
            norm_scalar(act, 0)
            act.wait_ge(q["cwT_full"], 1)
            act.copy(cw[:, :], bank[:, 4, 0:(CK + 1) * CONVF]).then_inc(q["cwT_ready"], 1)
            for j in range(2):
                act.wait_ge(q["scT_full"], j + 1)
                w = NSEQ * (CK - 1)
                act.copy(sct[:, 12 * j:12 * j + 12, :].rearrange("p f w -> p (f w)"), bank[:, 5 + j, 0:12 * w]).then_inc(q["scT_ready"], 1)
            chain = Chain(act, q["achain"])
            act.wait_ge(q["dt_ready"], 1)
            chain(act.activation(tiny[:, 1, :], tiny[:, 0, :], ACT.Abs))
            chain(act.activation(tiny[:, 2, :], tiny[:, 1, :], ACT.Exp, scale=-1.0))
            act.activation(tiny[:, 3, :], tiny[:, 2, :], ACT.Ln, bias=1.0).then_inc(q["acum_ready"], 1)
            act.activation(vec[:, NH:2 * NH], vec[:, NH:2 * NH], ACT.Exp).then_inc(q["acum_ready"], 1)
            act.wait_ge(q["acum_full"], 2)
            for b, dst in ((5, ea), (6, dec)):
                act.activation(dst[:, 0:PT, :], bank[:, b, 0:PT * NH].rearrange("p (t h) -> p t h", t=PT), ACT.Exp)
                act.activation(dst[0:SAMP, PT, :], bank[0:SAMP, b, PT * NH:NT * NH], ACT.Exp).then_inc(q["acum_ready"], 1)
            act.wait_ge(q["dt_ready"], 3)
            act.activation(dend[:, :, :].rearrange("p t h -> p (t h)"), tiny[:, 4, :], ACT.Exp).then_inc(q["acum_ready"], 1)
            act.wait_ge(q["memset_done"], 4)
            act.wait_ge(q["scT_ready"], 2)
            W = CK + 1
            with act.Fori(0, NG) as g:
                cwv = cw[:, :].rearrange("p (k f) -> p f k", k=W)
                act.wait_ge(q["conv_done"], g * CF)
                act.copy(cwg[:, 0:XF, :], cwv[:, bass.ds(g * XF, XF), :])
                act.copy(cwg[:, XF, :], cwv[:, bass.ds(g + NG * XF, 1), :].rearrange("p f k -> p (f k)"))
                act.copy(cwg[:, XF + 1, :], cwv[:, bass.ds(g + NG * XF + NG, 1), :].rearrange("p f k -> p (f k)")).then_inc(q["cwg_ready"], 1)
                for f in range(CF + 1):
                    if f < CF:
                        ft = [g * XF + f, g + NG * XF, g + NG * XF + NG][max(0, f - XF + 1)]
                        act.wait_ge(q["conv_done"], g * CF + max(0, f - 1))
                        rs = raw[:, f % 2, SOFF:RAWW].rearrange("p (s w) -> p s w", s=NSEQ)
                        act.copy(rs[:, :, 0:CK - 1], sct[:, bass.ds(ft, 1), :].rearrange("p f (s w) -> p (f s) w", s=NSEQ))
                        act.wait_ge(q["xg_full"], g * CF + f + 1)
                        b = 3 * (f % 2)
                        act.copy(raw[:, f % 2, CK - 1:CK - 1 + 512], bank[:, b, :])
                        act.copy(raw[:, f % 2, CK - 1 + 512:SOFF], bank[:, b + 1, :])
                        act.copy(rs[:, :, CK - 1:], bank[:, b + 2, 0:SAMP].rearrange("p (s w) -> p s w", s=NSEQ)).then_inc(q["raw_ready"], 1)
                    if f:
                        act.wait_ge(q["conv_done"], g * CF + f)
                        act.activation(xbc[:, f - 1, :], xbc[:, f - 1, :], ACT.Silu).then_inc(q["conv_ready"], 1)

                def turn(c, n):
                    r = ROWS[c]
                    act.wait_ge(q["yT_full"], n + 1)
                    act.wait_ge(q["out_full"], n * 2)
                    act.copy(yT[:, :, 0:r], bank[:, 0, :].rearrange("p (f r) -> p f r", f=XF)[:, :, 0:r]).then_inc(q["yT_ready"], 1)

                for c in range(NT):
                    n = g * NT + c
                    r = ROWS[c]
                    act.wait_ge(q["x_full"], n + 1)
                    act.wait_ge(q["gated"], n)
                    act.copy(xt[0:r, :], bank[0:r, 0, :]).then_inc(q["xt_ready"], 1)
                    act.wait_ge(q["bc_full"], n + 1)
                    if c:
                        act.wait_ge(q["st_full"], g * LC + c)
                    else:
                        act.wait_ge(q["bseq_ready"], g)
                    act.copy(btok[0:r, :], bank[0:r, 1, 0:DS]).then_inc(q["btok_ready"], 1)
                    act.wait_ge(q["seg_full"], n + 1)
                    if c < LC:
                        act.activation(mix[:, c % 2, :], bank[:, 2:4, :].rearrange("p b n -> p (b n)"), ACT.Exp).then_inc(q["e_ready"], 1)
                    else:
                        act.activation(mix[0:r, c % 2, 0:HG * r], bank[0:r, 2, :], ACT.Exp).then_inc(q["e_ready"], 1)
                    act.wait_ge(q["z_full"], n + 1)
                    act.activation(zs[0:r, :], bank[0:r, 4, :], ACT.Silu).then_inc(q["z_ready"], 1)
                    if c:
                        turn(c - 1, n - 1)
                    if c == LC:
                        for sq in range(NSEQ):
                            act.wait_ge(q["h0_full"], g * NSEQ + sq + 1)
                            if sq == 0:
                                act.wait_ge(q["fin_stored"], g * 16)
                            else:
                                if sq >= 2:
                                    act.wait_ge(q["yo_used"], g * NSEQ + sq - 1)
                            act.copy(h0T[:, sq % 2, :], bank[:, 7, :]).then_inc(q["h0_ready"], 1)
                    act.wait_ge(q["gated"], n + 1)
                    act.wait_ge(q["ssy_ready"], n)
                    act.activation(square[0:r, 0:GW], y[0:r, :], ACT.Square, accum_out=ybuf[0:r, 0:1]).then_inc(q["ssy_ready"], 1)
                act.wait_ge(q["fin_full"], g + 1)
                act.wait_ge(q["yo_used"], g * NSEQ + NSEQ)
                act.copy(h0T[:, 0, :], bank[:, 7, :]).then_inc(q["fin_ready"], 1)
                turn(NT - 1, g * NT + NT - 1)
            act.wait_ge(q["out_full"], 2 * NT * NG)
            for j in range(CONVF // 4):
                act.wait_ge(q["tail_full"], j + 1)
                act.copy(tail_rows[:, j // 2, 512 * (j % 2):512 * (j % 2) + 512], bank[0:TAIL, 4 + j % 2, :]).then_inc(q["tail_ready"], 1)
            ple_scalar(act, 0, 1)
            section3_scalar(act)
            section4_scalar(act)
            section5_scalar(act)
            ple_scalar(act, 1, 4)

        @block.vector
        def _(dve):
            chain = Chain(dve, q["vchain"])
            norm_vector(dve, 0)
            n = NT * NH
            dve.wait_ge(q["dt_full"], 1)
            dve.wait_ge(q["vec_loaded"], 48)
            chain(dve.memset(tiny[:, :, :], 0.0))
            for t in range(NT):
                r = ROWS[t]
                last = dve.tensor_tensor(tiny[0:r, 0, t * NH:(t + 1) * NH], bank[0:r, 7, t * NH:(t + 1) * NH], vec[0:r, 0:NH], ALU.add)
            last.then_inc(q["dt_ready"], 1)
            dve.wait_ge(q["dt_ready"], 1)
            dve.wait_ge(q["acum_ready"], 2)
            w, e, x = tiny[:, 1, :], tiny[:, 2, :], tiny[:, 0, :]
            chain(dve.tensor_scalar(w, e, 1.0, None, ALU.add))
            chain(dve.tensor_scalar(tiny[:, 4, :], w, -1.0, None, ALU.add))
            chain(dve.tensor_tensor(tiny[:, 4, :], e, tiny[:, 4, :], ALU.subtract))
            chain(dve.reciprocal(w, w))
            chain(dve.tensor_tensor(w, w, tiny[:, 4, :], ALU.mult))
            chain(dve.tensor_tensor(w, w, tiny[:, 3, :], ALU.add))
            flat = dtv[:, :, :].rearrange("p t h -> p (t h)")
            chain(dve.scalar_tensor_tensor(flat, x, 0.0, w, ALU.max, ALU.add))
            chain(dve.tensor_scalar(vec[:, NH:2 * NH], vec[:, NH:2 * NH], -1.0, None, ALU.mult))
            dve.tensor_tensor(dta[:, :, :], dtv[:, :, :], over(vec[:, NH:2 * NH], P, NT, NH), ALU.mult).then_inc(q["dt_ready"], 1)
            dve.wait_ge(q["acum_full"], 2)
            dve.wait_ge(q["acum_ready"], 4)
            for r, c0, c1 in ((P, 0, PT * NH), (SAMP, PT * NH, n)):
                chain(dve.tensor_copy(tiny[0:r, 4, c0:c1], bank[0:r, 6, c0:c1]))
                last = dve.tensor_tensor(tiny[0:r, 4, c0:c1], tiny[0:r, 4, c0:c1], bank[0:r, 5, c0:c1], ALU.subtract)
            last.then_inc(q["dt_ready"], 1)
            dve.wait_ge(q["scT_ready"], 2)
            with dve.Fori(0, NG) as g:
                chain.enter(g, VSTEPS)
                dve.wait_ge(q["cwg_ready"], g + 1)
                dve.wait_ge(q["fin_full"], g)
                chain(dve.memset(hT[:, :], 0.0))
                for f in range(CF):
                    ft = [g * XF + f, g + NG * XF, g + NG * XF + NG][max(0, f - XF + 1)]
                    dve.wait_ge(q["raw_ready"], g * CF + f + 1)
                    rs = raw[:, f % 2, SOFF:RAWW].rearrange("p (s w) -> p s w", s=NSEQ)
                    dst = xbc[:, f, SEQ:TOK].rearrange("p (s w) -> p s w", s=NSEQ)
                    dve.tensor_copy(tail[:, bass.ds(ft, 1), 0:CK - 1], raw[:, f % 2, SOFF - (CK - 1):SOFF].unsqueeze(1))
                    dve.tensor_copy(tail[:, bass.ds(ft, 1), CK - 1:].rearrange("p f (s w) -> p (f s) w", s=NSEQ), rs[:, :, DSEQ:])
                    for k in range(CK):
                        wk = cwg[:, f, k:k + 1]
                        parts = ((xbc[:, f, 0:SEQ], raw[:, f % 2, k:k + SEQ]), (dst, rs[:, :, k:k + DSEQ]))
                        for m, (d, src) in enumerate(parts):
                            if k == 0:
                                ins = dve.tensor_scalar(d, src, wk, cwg[:, f, CK:CK + 1], ALU.mult, ALU.add)
                            else:
                                ins = dve.scalar_tensor_tensor(d, src, wk, d, ALU.mult, ALU.add)
                        if k < CK - 1:
                            chain(ins)
                    ins.then_inc(q["conv_done"], 1)
                dve.wait_ge(q["nw_landed"], g * 16 + 16)
                for c in range(NT):
                    m = g * NT + c
                    r = ROWS[c]
                    hv = lambda t: t.rearrange("p (h d) -> p h d", h=HG)
                    hs = bass.ds(g * HG, HG)
                    dve.wait_ge(q["btok_ready"], m + 1)
                    dve.tensor_tensor(cbm[0:r, 0:r], bank[0:r, 1, DS:DS + r], con("tri" if c < LC else "tri8", r)[:, 0:r], ALU.mult).then_inc(q["cbm_ready"], 1)
                    dve.wait_ge(q["xt_ready"], m + 1)
                    dve.wait_ge(q["yd_full"], m)
                    dve.wait_ge(q["xdtd_ready"], m)
                    dve.tensor_tensor(hv(xdt[0:r, :]), hv(xt[0:r, :]), bc(dtv[0:r, c, hs], r, HG, HD), ALU.mult).then_inc(q["xdt_ready"], 1)
                    dve.wait_ge(q["e_ready"], m + 1)
                    dve.wait_ge(q["cbm_ready"], m + 1)
                    mv = mix[0:r, c % 2, 0:HG * r].rearrange("p (h l) -> p h l", h=HG)
                    dve.tensor_tensor(mv, mv, over(cbm[0:r, 0:r], r, HG, r), ALU.mult).then_inc(q["m_ready"], 1)
                    if c == LC:
                        dve.wait_ge(q["btok_ready"], m + 1)
                        dve.tensor_tensor(bseq[:, :, :], over(btok[0:r, :], r, NSEQ, DS), bc(con("inseq", r), r, NSEQ, DS), ALU.mult).then_inc(q["bseq_ready"], 1)
                        chain(dve.memset(cseq[:, :, :], 0.0))
                        diag = cseq[:, :, :].rearrange("p s t -> p (s t)")
                        for sq in range(NSEQ):
                            ins = dve.tensor_copy(cseq[:, sq, sq * DSEQ:(sq + 1) * DSEQ], xbc[:, XF + 1, SEQ + sq * DSEQ:SEQ + (sq + 1) * DSEQ])
                        ins.then_inc(q["cseq_ready"], 1)
                        dve.tensor_copy(hv(dexp[:, :]), bc(dec[0:r, c, hs], r, HG, HD)).then_inc(q["dexp_ready"], 1)
                        dve.wait_ge(q["sdec_full"], g + 1)
                        chain(dve.tensor_copy(sdec[:, :, :], bank[:, 6, 0:XF * NSEQ].rearrange("p (f s) -> p f s", f=XF)))
                        for sq in range(NSEQ):
                            dve.wait_ge(q["snew_full"], g * NSEQ + sq + 1)
                            sv = st[:, sq % 4, :, :]
                            chain(dve.tensor_tensor(sv, sv, bc(sdec[:, :, sq], P, XF, DS), ALU.mult))
                            dve.tensor_tensor(sv, sv, bank[:, 1 + 2 * (sq % 2), :].rearrange("p (f n) -> p f n", f=XF), ALU.add).then_inc(q["snew_ready"], 1)
                    dve.wait_ge(q["yd_full"], m + 1)
                    dve.wait_ge(q["yn_ready"], m)
                    dve.wait_ge(q["yT_full"], m)
                    chain(dve.tensor_tensor(hv(y[0:r, :]), hv(bank[0:r, 5, :]), bc(ea[0:r, c, hs], r, HG, HD), ALU.mult))
                    chain(dve.tensor_tensor(y[0:r, :], y[0:r, :], bank[0:r, 6, :], ALU.add))
                    dve.wait_ge(q["skip_ready"], m + 1)
                    chain(dve.tensor_tensor(y[0:r, :], y[0:r, :], xt[0:r, :], ALU.add))
                    dve.wait_ge(q["z_ready"], m + 1)
                    dve.tensor_tensor(y[0:r, :], y[0:r, :], zs[0:r, :], ALU.mult).then_inc(q["gated"], 1)
                    if c < LC:
                        dve.wait_ge(q["st_full"], g * LC + c + 1)
                        chain(dve.tensor_tensor(hv(hT[:, :]), hv(hT[:, :]), bc(dec[:, c, hs], P, HG, HD), ALU.mult))
                        dve.tensor_tensor(hT[:, :], hT[:, :], bank[:, 7, :], ALU.add).then_inc(q["hT_ready"], 1)
                    if c:
                        add_out(dve, c - 1, m - 1)
                    dve.wait_ge(q["ssy_ready"], m + 1)
                    dve.tensor_scalar(ybuf[0:r, 1:2], ybuf[0:r, 0:1], 1.0 / GW, EPS, ALU.mult, ALU.add).then_inc(q["msy_ready"], 1)
                    dve.wait_ge(q["ry_ready"], m + 1)
                    dve.scalar_tensor_tensor(y[0:r, :], y[0:r, :], ybuf[0:r, 2:3], nwg[0:r, :], ALU.mult, ALU.mult).then_inc(q["yn_ready"], 1)
                add_out(dve, NT - 1, g * NT + NT - 1)
                chain.leave(NG)
            ple_vector(dve, 0, 1)
            section3_vector(dve, chain)
            section4_vector(dve, chain)
            section5_vector(dve, chain)
            ple_vector(dve, 1, 4)

        @block.tensor
        def _(pe):
            pe.wait_ge(q["const_loaded"], 16)
            norm_tensor(pe, 0)
            pe.wait_ge(q["cw_loaded"], 48)
            pe.transpose(bank[:, 4, 0:(CK + 1) * CONVF], cw_rows, ident[0:(CK + 1) * CONVF, 0:(CK + 1) * CONVF]).then_inc(q["cwT_full"], 1)
            w = NSEQ * (CK - 1)
            for f in range(CONVF):
                last = pe.transpose(bank[:, 5 + f // 12, (f % 12) * w:(f % 12 + 1) * w], sc_rows[:, f // 8, (f % 8) * P:(f % 8 + 1) * P], ident[0:w, 0:w])
                if f % 12 == 11:
                    last.then_inc(q["scT_full"], 1)
            pe.wait_ge(uT_ready, 2 * NT)
            pe.wait_ge(q["wdt_loaded"], 16)
            for t in range(NT):
                r = ROWS[t]
                for k in range(KT):
                    last = pe.matmul(bank[0:r, 7, t * NH:(t + 1) * NH], uT[:, k, cols(t)], wdt[:, k, :], start=(k == 0), stop=(k == KT - 1))
            last.then_inc(q["dt_full"], 1)
            pe.wait_ge(q["dt_ready"], 2)
            pe.wait_ge(q["scT_ready"], 2)
            pe.wait_ge(q["memset_done"], 4)
            for b, full, part in ((5, "tri", "tri8"), (6, None, "same8")):
                for t in range(NT):
                    r = ROWS[t]
                    m = (con(full) if full else ones[:, :]) if t < PT else con(part, r)[:, 0:r]
                    last = pe.matmul(bank[0:r, b, t * NH:(t + 1) * NH], m, dta[0:r, t, :], start=True, stop=True)
                last.then_inc(q["acum_full"], 1)
            pe.wait_ge(q["acum_ready"], 5)
            pe.wait_ge(q["cwT_ready"], 1)
            with pe.Fori(0, NG) as g:
                pe.wait_ge(q["out_added"], g * (2 * NT))
                pe.wait_ge(q["fin_ready"], g)
                for f in range(CF):
                    pe.wait_ge(wx_landed[f % 2], g * 48 + 16 * (f // 2 + 1))
                    if f > 1:
                        pe.wait_ge(q["raw_ready"], g * CF + f - 1)
                    for j, (c0, c1) in enumerate(((0, 512), (512, 1024), (SEQ, TOK))):
                        for k in range(KT):
                            last = pe.matmul(bank[:, 3 * (f % 2) + j, 0:c1 - c0], wx[:, f % 2, k, :], uT[:, k, c0:c1],
                                             start=(k == 0), stop=(k == KT - 1))
                    last.then_inc(q["xg_full"], 1)
                pe.wait_ge(q["conv_ready"], g * CF + CF)
                pe.wait_ge(q["raw_ready"], g * CF + CF)

                def turn_y(c, n):
                    r = ROWS[c]
                    pe.wait_ge(q["yn_ready"], n + 1)
                    alone(pe)
                    for f in range(XF):
                        last = pe.transpose(bank[:, 0, f * P:f * P + r], y[0:r, f * P:(f + 1) * P], ident[0:r, 0:r])
                    last.then_inc(q["yT_full"], 1)

                def multiply_out(c, n):
                    r = ROWS[c]
                    pe.wait_ge(q["yT_ready"], n + 1)
                    if c == 0:
                        pe.wait_ge(q["wo_landed"], g * 16 + 16)
                    alone(pe)
                    for half in range(2):
                        for k in range(XF):
                            last = pe.matmul(bank[0:r, 2 + half, :], yT[:, k, 0:r], wo[:, k, 512 * half:512 * (half + 1)],
                                             start=(k == 0), stop=(k == XF - 1))
                        last.then_inc(q["out_full"], 1)

                for c in range(NT):
                    n = g * NT + c
                    r = ROWS[c]
                    cs = cols(c)
                    if c > 1:
                        pe.wait_ge(q["yT_ready"], n - 1)
                    if c == LC:
                        alone(pe)
                    for f in range(XF):
                        last = pe.transpose(bank[0:r, 0, f * P:(f + 1) * P], xbc[:, f, cs], ident)
                    last.then_inc(q["x_full"], 1)
                    pe.wait_ge(q["btok_ready"], n)
                    pe.wait_ge(q["cbm_ready"], n)
                    if c == LC:
                        alone(pe)
                    pe.transpose(bank[0:r, 1, 0:DS], xbc[:, XF, cs], ident)
                    pe.matmul(bank[0:r, 1, DS:DS + r], xbc[:, XF, cs], xbc[:, XF + 1, cs], start=True, stop=True).then_inc(q["bc_full"], 1)
                    pe.wait_ge(q["sum_ready"], n + 1)
                    if c > 1:
                        pe.wait_ge(q["out_added"], n * 2 - 2)
                    if c == LC:
                        alone(pe)
                    if c < LC:
                        for half in range(2):
                            last = pe.matmul(bank[:, 2 + half, :], con("after"), mix[:, c % 2, 512 * half:512 * (half + 1)], start=True, stop=True)
                    else:
                        last = pe.matmul(bank[0:r, 2, :], con("after8", r)[:, 0:r], mix[0:r, c % 2, 0:HG * r], start=True, stop=True)
                    last.then_inc(q["seg_full"], 1)
                    if c == 0:
                        pe.wait_ge(q["wz_landed"], g * 16 + 16)
                    pe.wait_ge(q["z_ready"], n)
                    if c == LC:
                        alone(pe)
                    for k in range(KT):
                        last = pe.matmul(bank[0:r, 4, :], uT[:, k, cs], wz[:, k, :], start=(k == 0), stop=(k == KT - 1))
                    last.then_inc(q["z_full"], 1)
                    if c:
                        pe.wait_ge(q["xt_ready"], n + 1)
                        turn_y(c - 1, n - 1)
                    pe.wait_ge(q["gated"], n)
                    pe.wait_ge(q["m_ready"], n + 1)
                    pe.wait_ge(q["xdt_ready"], n + 1)
                    if c == LC:
                        pe.wait_ge(q["hT_ready"], g * LC + LC)
                        pe.wait_ge(q["dexp_ready"], g + 1)
                        alone(pe)
                        for f in range(XF):
                            last = pe.matmul(bank[:, 6, f * NSEQ:(f + 1) * NSEQ], dexp[:, f * P:(f + 1) * P], con("first", r), start=True, stop=True)
                        last.then_inc(q["sdec_full"], 1)
                        pe.wait_ge(q["cseq_ready"], g + 1)
                        pe.wait_ge(q["bseq_ready"], g + 1)
                        pe.wait_ge(q["xdtd_ready"], n + 1)
                        pe.wait_ge(q["btok_ready"], n + 1)
                        pe.wait_ge(q["cbm_ready"], n + 1)
                        pe.wait_ge(q["e_ready"], n + 1)

                        def turn_state(sq):
                            pe.wait_ge(st_landed[sq % 4], g * 32 + 16 * (sq // 4 + 1))
                            if sq:
                                pe.wait_ge(q["h0_ready"], g * NSEQ + sq)
                            for f in range(XF):
                                last = pe.transpose(bank[:, 7, f * P:(f + 1) * P], st[:, sq % 4, f, :], ident)
                            last.then_inc(q["h0_full"], 1)

                        turn_state(0)
                        for sq in range(NSEQ):
                            if sq > 1:
                                pe.wait_ge(q["snew_ready"], g * NSEQ + sq - 1)
                            alone(pe)
                            for f in range(XF):
                                last = pe.matmul(bank[:, 1 + 2 * (sq % 2), f * P:(f + 1) * P], xdtd[0:r, f * P:(f + 1) * P], bseq[:, sq, :], start=True, stop=True)
                            last.then_inc(q["snew_full"], 1)
                            if sq + 1 < NSEQ:
                                turn_state(sq + 1)
                            pe.wait_ge(q["h0_ready"], g * NSEQ + sq + 1)
                            alone(pe)
                            pe.matmul(bank[0:r, 5, :], cseq[:, sq, :], h0T[:, sq % 2, :], start=(sq == 0), stop=(sq == NSEQ - 1)).then_inc(q["yo_used"], 1)
                        pe.wait_ge(q["snew_ready"], g * NSEQ + NSEQ)
                    else:
                        if c:
                            pe.wait_ge(q["hT_ready"], g * LC + c)
                        else:
                            pe.wait_ge(q["raw_ready"], g * CF + CF)
                        pe.matmul(bank[:, 5, :], xbc[:, XF + 1, cs], hT[:, :], start=True, stop=True)
                    if c == LC:
                        alone(pe)
                    for hh in range(HG):
                        last = pe.matmul(bank[0:r, 6, hh * HD:(hh + 1) * HD], mix[0:r, c % 2, hh * r:(hh + 1) * r],
                                         xdt[0:r, hh * HD:(hh + 1) * HD], start=True, stop=True)
                    last.then_inc(q["yd_full"], 1)
                    if c < LC:
                        pe.wait_ge(q["xdtd_ready"], n + 1)
                        pe.wait_ge(q["btok_ready"], n + 1)
                        pe.matmul(bank[:, 7, :], btok[:, :], xdtd[:, :], start=True, stop=True).then_inc(q["st_full"], 1)
                    if c:
                        multiply_out(c - 1, n - 1)
                pe.wait_ge(q["h0_ready"], g * NSEQ + NSEQ)
                for f in range(XF):
                    last = pe.transpose(bank[:, 7, f * P:(f + 1) * P], hT[:, f * P:(f + 1) * P], ident)
                last.then_inc(q["fin_full"], 1)
                turn_y(NT - 1, g * NT + NT - 1)
                multiply_out(NT - 1, g * NT + NT - 1)
            for j in range(CONVF // 4):
                if j > 1:
                    pe.wait_ge(q["tail_ready"], j - 1)
                for i in range(4):
                    last = pe.transpose(bank[0:TAIL, 4 + j % 2, i * P:(i + 1) * P], tail[:, 4 * j + i, :], ident)
                last.then_inc(q["tail_full"], 1)
            ple_tensor(pe, 0, 1)
            section3_tensor(pe)
            section4_tensor(pe)
            section5_tensor(pe)
            ple_tensor(pe, 1, 4)


_INS = ["x_prompt", "x_sample", "state_ssm", "state_conv", "cache_kv_g1", "cache_kv_g2", "cache_kv_g3",
        "p_prompt", "p_sample", "norm_w", "m_in_w", "m_conv_w", "m_conv_b", "m_dt_bias", "m_A_log", "m_D",
        "m_norm_w", "m_out_w", "kv_norm_w", "kv_w", "k_norm_w", "a_in_w", "a_q_norm_w", "a_out_w",
        "ple_w", "ple_gate_w", "ple_norm_w"]
KV = (2, KVH, HD)
_OUTS = {"y_prompt": (1, SEQ, D), "y_sample": (NSEQ, DSEQ, D), "ssm_prompt": (1, 1, NH, HD, DS),
         "conv_prompt": (1, 1, CK - 1, CONVF * P), "ssm_sample": (1, NSEQ, NH, HD, DS),
         "conv_sample": (1, NSEQ, CK - 1, CONVF * P),
         "kv_prompt_g1": (1, 128) + KV, "kv_prompt_g2": (1, 512) + KV, "kv_prompt_g3": (1, 1024) + KV,
         "kv_sample_g1": (NSEQ, DSEQ) + KV, "kv_sample_g2": (NSEQ, DSEQ) + KV, "kv_sample_g3": (NSEQ, DSEQ) + KV}
_SCRATCH = {"kv": (TOK, 2, NGR, KVH * HD), "q": (TOK, NGR, D), "gate": (TOK, D), "u": (NGR, SEQ, D), "ms": (NGR, SEQ, 2 * AH),
            "os": (SAMP, D)}


def kernel(**inputs):
    import concourse.bacc as bacc
    from concourse.bass_utils import run_bass_kernel_spmd

    nc = bacc.Bacc("TRN2", target_bir_lowering=False, num_devices=1)
    arrays, a = {}, {}
    for name in _INS:
        x = np.ascontiguousarray(inputs[name])
        arrays[f"in_{name}"] = x
        a[name] = nc.dram_tensor(f"in_{name}", x.shape, mybir.dt.from_np(x.dtype), kind="ExternalInput").ap()
    table = np.concatenate([v for v in shape_constants().values()], 1)
    arrays["in_consts"] = table
    a["consts"] = nc.dram_tensor("in_consts", table.shape, F32, kind="ExternalInput").ap()
    o = {n: nc.dram_tensor(f"out_{n}", shape, F32, kind="ExternalOutput").ap() for n, shape in _OUTS.items()}
    s = {n: nc.dram_tensor(f"scratch_{n}", shape, F32).ap() for n, shape in _SCRATCH.items()}
    trunk_kernel(nc, a, o, s)
    r = run_bass_kernel_spmd(nc, [arrays], core_ids=[0])
    return tuple(r.results[0][f"out_{n}"] for n in _OUTS)
```

```python
from contextlib import ExitStack

import numpy as np

import concourse.bass as bass
from concourse import mybir

F32 = mybir.dt.float32
ALU = mybir.AluOpType
ACT = mybir.ActivationFunctionType
AX_X = mybir.AxisListType.X
P = 128
EPS = 1e-6
FR = mybir.dt.float32r
NEG = -1e30

D = 1024
KT = D // P
SEQ, NSEQ, DSEQ, PAST = 1024, 8, 8, 1024
PT = SEQ // P
NT = PT + 1
SAMP = NSEQ * DSEQ
TOK = SEQ + SAMP
ROWS = [P] * PT + [SAMP]
DI, HD, NH, NG, DS = 2048, 64, 32, 4, 128
HG = NH // NG
GW = HG * HD
XF = GW // P
CF = XF + 2
CONVF = (DI + 2 * NG * DS) // P
CK = 4
LC = SEQ // P
RAWW = CK - 1 + SEQ + NSEQ * (CK - 1 + DSEQ)
SOFF = CK - 1 + SEQ
TAIL = (CK - 1) * (1 + NSEQ)
_third = -(-TOK // 3) + (-(-TOK // 3)) % 2
CUTS = (0, _third, 2 * _third, TOK)
AH, KVH, REP = 16, 4, 4
NGR = 3
DIL = (1, 4, 16)
PLE = 256


def shape_constants():
    i = np.arange(P)
    seq = i // DSEQ
    same = seq[:, None] == seq[None, :]
    c = {}
    c["ident"] = np.eye(P)
    c["tri"] = (i[:, None] <= i[None, :])
    c["after"] = (i[:, None] > i[None, :])
    c["tri8"] = (i[:, None] <= i[None, :]) & same
    c["after8"] = (i[:, None] > i[None, :]) & same
    c["same8"] = same
    s = np.arange(NSEQ)
    c["inseq"] = seq[:, None] == s[None, :]
    c["first"] = i[:, None] == DSEQ * s[None, :]
    half = HD // 2
    inv = 1.0 / (10000.0 ** (np.arange(half, dtype=np.float32) / np.float32(half)))
    pos = np.concatenate([np.arange(SEQ), PAST + np.arange(P) % DSEQ]).astype(np.float32)
    ang = pos[:, None] * inv[None, :].astype(np.float32)
    cos = np.cos(ang).reshape(NT, P, half).transpose(1, 0, 2)
    sin = np.sin(ang).reshape(NT, P, half).transpose(1, 0, 2)
    c["cos"] = np.concatenate([cos, cos], -1).reshape(P, -1)
    c["sin"] = np.concatenate([-sin, sin], -1).reshape(P, -1)
    q, k = i[:, None], i[None, :]
    c["win"] = np.concatenate([np.where(k >= q, 0, NEG), np.where(k <= q, 0, NEG)], 1)
    c["pair"] = np.where((k <= q) & (k // 64 == q // 64), 0, NEG)
    t = (i % DSEQ)[:, None]
    new = np.arange(DSEQ)[None, :]
    parts = [np.where(k >= t, 0, NEG)]
    for dil in DIL:
        parts.append(np.where((new <= t) & ((t - new) % dil == 0), 0, NEG))
    for r in range(4):
        parts.append(np.where(((t % 4) == r) & (4 * k + r >= t), 0, NEG))
    for a in range(4):
        parts.append(np.where((2 * a + k // 64) == t, 0, NEG) + 0.0 * k)
    c["smask"] = np.concatenate([p + np.zeros((P, p.shape[1])) for p in parts], 1)
    return {n: np.ascontiguousarray(v, np.float32) for n, v in c.items()}


LAYOUT, _at = {}, 0
for _n, _w in (("ident", P), ("tri", P), ("after", P), ("tri8", P), ("after8", P), ("same8", P),
               ("inseq", NSEQ), ("first", NSEQ), ("cos", NT * HD), ("sin", NT * HD),
               ("win", 2 * P), ("pair", P), ("smask", P + 3 * DSEQ + 8 * P)):
    LAYOUT[_n] = (_at, _w)
    _at += _w
NMASK = LAYOUT["cos"][0]


class Chain:

    def __init__(self, eng, sem):
        self.eng, self.sem, self.n, self.i, self.start, self.stride = eng, sem, 0, None, 0, 0

    def enter(self, i, stride):
        self.i, self.start, self.stride = i, self.n, stride

    def leave(self, times):
        assert self.n - self.start == self.stride, (self.n - self.start, self.stride)
        self.n = self.start + times * self.stride
        self.i = None

    def __call__(self, ins):
        ins.then_inc(self.sem, 1)
        self.n += 1
        if self.i is None:
            self.eng.wait_ge(self.sem, self.n)
        else:
            self.eng.wait_ge(self.sem, self.i * self.stride + self.n)


def trunk_kernel(nc, a, o, s):
    outer = ExitStack()
    with outer:
        def sem(name):
            return outer.enter_context(nc.semaphore(name))

        def sb_in(ctx):
            def sb(name, shape, dt=F32):
                return ctx.enter_context(nc.sbuf_tensor(name, shape, dt))
            return sb

        keep = sb_in(outer)
        bank = outer.enter_context(nc.psum_tensor("bank", [P, 8, 512], F32))
        same = ExitStack()
        wz = sb_in(same)("wz", [P, KT, GW])
        same.close()
        same = ExitStack()
        wzl = sb_in(same)("wzl", [P, KT, GW], FR)
        wzh = sb_in(same)("wzh", [P, KT, GW], FR)
        h0T = sb_in(same)("h0T", [P, 2, GW])
        same.close()
        h = keep("h", [P, NT, D])
        cst = keep("cst", [P, NMASK])
        same = ExitStack()
        yh = sb_in(same)("yh", [P, 2, DI // P, P], FR)
        same.close()
        gain = keep("gain", [P, D])
        u = keep("u", [P, 2, D])
        square = keep("square", [P, D])
        ss = keep("ss", [P, 16])
        ms = keep("ms", [P, 16])
        rstd = keep("rstd", [P, 16])
        mhalf = keep("mhalf", [P, 16])
        same = ExitStack()
        uT = sb_in(same)("uT", [P, KT, TOK])
        same.close()
        uH = keep("uH", [P, KT, TOK], FR)

        def con(name, rows=P):
            at, w = LAYOUT[name]
            return cst[0:rows, at:at + w]

        ident = con("ident")

        s1 = ExitStack()
        sb = sb_in(s1)
        same = ExitStack()
        wx = sb_in(same)("wx", [P, 2, KT, P])
        same.close()
        wxl = sb("wxl", [P, 2, KT, P], FR)
        wxh = sb("wxh", [P, 2, KT, P], FR)
        uL1 = sb("uL1", [P, KT, TOK], FR)
        raw = sb("raw", [P, 2, RAWW])
        xbc = sb("xbc", [P, CF, TOK])
        sct = sb("sct", [P, CONVF, NSEQ * (CK - 1)])
        tail = sb("tail", [P, CONVF, TAIL])
        cw = sb("cw", [P, (CK + 1) * CONVF])
        cwg = sb("cwg", [P, CF, CK + 1])
        vec = sb("vec", [P, 3 * NH])
        dtv = sb("dtv", [P, NT, NH])
        dta = sb("dta", [P, NT, NH])
        ea = sb("ea", [P, NT, NH])
        dend = sb("dend", [P, NT, NH])
        dec = sb("dec", [P, NT, NH])
        nwg = gain[:, 0:GW]
        ones = sb("ones", [P, P])
        xt = sb("xt", [P, GW])
        btok = sb("btok", [P, DS])
        cbm = sb("cbm", [P, P])
        same = ExitStack()
        wdt = sb_in(same)("wdt", [P, KT, P])
        same.close()
        same = ExitStack()
        wdtl = sb_in(same)("wdtl", [P, KT, P], FR)
        wdth = sb_in(same)("wdth", [P, KT, P], FR)
        same.close()
        mix = sb("mix", [P, 2, HG * P])
        xdt = sb("xdt", [P, GW])
        xdtd = sb("xdtd", [P, GW])
        y = square[:, GW:2 * GW]
        zs = sb("zs", [P, GW])
        yT = sb("yT", [P, XF, P])
        hT = gain[:, GW:2 * GW]
        ybuf = sb("ybuf", [P, 4])
        bseq = u[0:SAMP, 0, :].rearrange("p (s n) -> p s n", s=NSEQ)
        cseq = u[:, 1, 0:GW].rearrange("p (s t) -> p s t", s=NSEQ)
        dexp = u[0:SAMP, 1, GW:2 * GW]
        st = raw[:, :, :].rearrange("p a w -> p (a w)")[:, 0:4 * XF * DS].rearrange("p (s f n) -> p s f n", s=4, f=XF)
        sdec = sb("sdec", [P, XF, NSEQ])
        tiny = xbc[:, 3:5, :].rearrange("p a b -> p (a b)")[:, 0:5 * NT * NH].rearrange("p (a b) -> p a b", a=5)
        dtT = xbc[:, CF - 1, :]
        cw_rows = xdt[0:(CK + 1) * CONVF, 0:P]
        sc_rows = xbc[0:NSEQ * (CK - 1), 0:3, 0:D]
        tail_rows = xbc[0:TAIL, 0:3, 0:D]
        s1.close()

        ss_ready = sem("ss_ready")
        ms_ready = sem("ms_ready")
        rstd_ready = sem("rstd_ready")
        gain_landed = sem("gain_landed")
        u_ready = sem("u_ready")
        uT_full = sem("uT_full")
        uT_ready = sem("uT_ready")
        uL_ready = sem("uL_ready")
        wh_ready = sem("wh_ready")
        wl_ready = sem("wl_ready")
        IN_SPLITS = CF + 1
        _n = 2 + NG * IN_SPLITS
        SPLIT_BEFORE = {1.5: _n, 2: _n + 8, 3: _n + 10, 5: _n + 21, 6: _n + 25}
        section = sem("section")
        names = """res_loaded const_loaded vec_loaded cw_loaded memset_done
            turned_full turned_ready dt_full dt_ready acum_full acum_ready
            wz_landed wo_landed nw_landed xg_full raw_ready conv_done conv_ready
            x_full xt_ready bc_full btok_ready cbm_ready sum_ready seg_full e_ready m_ready z_full z_ready
            xdt_ready xdtd_ready skip_ready yd_full st_full hT_ready gated ssy_ready msy_ready ry_ready yn_ready
            yT_full yT_ready out_full out_added cwg_ready dexp_ready sdec_full bseq_ready yT_stored
            h0_full h0_ready snew_full snew_ready yo_used fin_full fin_ready fin_stored state_stored tail_full
            tail_ready vchain achain waits_passed"""
        q = {n: sem(n) for n in names.split()}
        wx_landed = [sem(f"wx_landed{i}") for i in range(2)]
        st_landed = [sem(f"st_landed{i}") for i in range(4)]

        in_w = a["m_in_w"][0].rearrange("(k p) n -> p k n", p=P)
        st_in = a["state_ssm"].rearrange("x s h p n -> (x h p) s n")
        st_out = o["ssm_sample"].rearrange("x s h p n -> (x h p) s n")
        st_prompt = o["ssm_prompt"].rearrange("x b h p n -> (x b h p) n")
        XCOL, BCOL, CCOL, DTCOL = DI, 2 * DI, 2 * DI + NG * DS, 2 * DI + 2 * NG * DS

        DTBANK = (3, 7, 0)
        VSTEPS = 2 + CF * (CK - 1) + 2 + NSEQ + 3 * NT + LC
        block = outer.enter_context(nc.Block())

        def cols(t):
            return slice(t * P, t * P + ROWS[t])

        def bc(ap, rows, n, m):
            return ap.unsqueeze(2).broadcast_to([rows, n, m])

        def over(ap, rows, n, m):
            return ap.unsqueeze(1).broadcast_to([rows, n, m])

        def alone(eng):
            eng.sem_inc(q["waits_passed"], 1)

        def norm_scalar(act, k, squares=True, low=None, amid=lambda: None):
            if squares:
                for t in range(NT):
                    r = ROWS[t]
                    act.wait_ge(ss_ready, NT * (rstd_count[k] - 1) + t)
                    act.activation(square[0:r, :], h[0:r, t, :], ACT.Square,
                                   accum_out=ss[0:r, t:t + 1]).then_inc(ss_ready, 1)
            amid()
            for t in range(NT):
                r = ROWS[t]
                act.wait_ge(uT_full, NT * k + t + 1)
                for half in range(2):
                    b = bank[:, 2 * (t % 2) + half, :].rearrange("p (k r) -> p k r", k=4)[:, :, 0:r]
                    act.copy((uT if low is None else uH)[:, 4 * half:4 * half + 4, cols(t)], b).then_inc(uT_ready, 1)

        rstd_count = {0: 1, 1: 2, 2: 3, 3: 3, 4: 4}

        def low_part(dve, k, t, low):
            dve.wait_ge(uT_ready, 2 * (NT * k + t + 1))
            for half in range(2):
                part = (slice(None), slice(4 * half, 4 * half + 4), cols(t))
                b = bank[:, 2 * (t % 2) + half, :].rearrange("p (k r) -> p k r", k=4)[:, :, 0:ROWS[t]]
                last = dve.tensor_tensor(low[part], b, uH[part].bitcast(F32), ALU.subtract)
            last.then_inc(uL_ready, 1)

        def norm_vector(dve, k, squares=True, low=None):
            if squares:
                dve.wait_ge(ss_ready, NT * rstd_count[k])
                dve.tensor_scalar(ms[:, 0:NT], ss[:, 0:NT], 1.0 / D, EPS, ALU.mult,
                                  ALU.add).then_inc(ms_ready, 1)
            dve.wait_ge(rstd_ready, rstd_count[k])
            dve.wait_ge(gain_landed, 16 * (k + 1))
            for t in range(NT):
                r = ROWS[t]
                if NT * k + t >= 2:
                    dve.wait_ge(uT_full, NT * k + t - 1)
                dve.scalar_tensor_tensor(u[0:r, t % 2, :], h[0:r, t, :], rstd[0:r, t:t + 1], gain[0:r, :],
                                         ALU.mult, ALU.mult).then_inc(u_ready, 1)
                if low is not None and t:
                    low_part(dve, k, t - 1, low)
            if low is not None:
                low_part(dve, k, NT - 1, low)

        def norm_gpsimd(pool, k):
            pool.wait_ge(ms_ready, rstd_count[k])
            if k:
                pool.wait_ge(u_ready, NT * k)
            pool.tensor_tensor(rstd[:, 0:NT], ms[:, 0:NT], mhalf[:, 0:NT], ALU.pow).then_inc(rstd_ready, 1)

        def norm_tensor(pe, k, low=None):
            for t in range(NT):
                r = ROWS[t]
                pe.wait_ge(u_ready, NT * k + t + 1)
                if t >= 2:
                    pe.wait_ge(uT_ready, 2 * (NT * k + t - 1))
                    if low is not None:
                        pe.wait_ge(uL_ready, NT * k + t - 1)
                for f in range(KT):
                    last = pe.transpose(bank[:, 2 * (t % 2) + f // 4, (f % 4) * P:(f % 4) * P + r],
                                        u[0:r, t % 2, f * P:(f + 1) * P], ident[0:r, 0:r])
                last.then_inc(uT_full, 1)

        def load_gain(sp, k, row):
            if k:
                sp.wait_ge(u_ready, NT * k)
            sp.dma_start(gain[:, :], row.broadcast_to([P, D])).then_inc(gain_landed, 16)

        def meet(eng, k):
            eng.drain().then_inc(section, 1)
            eng.wait_ge(section, 5 * k)

        DIT = DI // P
        sout = ExitStack()
        sb = sb_in(sout)
        same = ExitStack()
        wo = sb_in(same)("wo", [P, 2, DIT, 512])
        same.close()
        wol = sb("wol", [P, 2, DIT, 512], FR)
        woh1 = sb("woh1", [P, DIT, 512], FR)
        same = ExitStack()
        yin = sb_in(same)("yin", [P, 2, DIT, P])
        same.close()
        yl = sb("yl", [P, 2, DIT, P], FR)
        sout.close()
        woh = [uH[:, :, :].rearrange("p k t -> p (k t)")[:, 0:DIT * 512].rearrange("p (k n) -> p k n", k=DIT), woh1[:, :, :]]
        tile_landed = [sem(f"tile_landed{x}") for x in range(2)]
        yh_ready = sem("yh_ready")
        yl_ready = sem("yl_ready")

        def out_steps():
            return [(j * NT + t, j, t) for j in range(2) for t in range(NT)]

        def out_sync(sp):
            meet(sp, 1)
            src = a["m_out_w"][0].rearrange("(k p) n -> p k n", p=P)
            yT_src = s["yT"].rearrange("(k p) t -> p k t", p=P)
            for v, j, t in out_steps():
                if v > 1:
                    sp.wait_ge(q["out_full"], v - 1)
                at = min(t * P, TOK - P)
                sp.dma_start(yin[:, v % 2, :, :], yT_src[:, :, at:at + P]).then_inc(tile_landed[v % 2], 16)
                if v == 0:
                    sp.dma_start(wo[:, 0, :, :], src[:, :, 0:512]).then_inc(q["wo_landed"], 16)
                    sp.dma_start(h[:, 0:PT, :], a["x_prompt"][0].rearrange("(t p) d -> p t d", p=P)).then_inc(q["res_loaded"], 16)
                    sp.dma_start(h[0:SAMP, PT, :], a["x_sample"].rearrange("b t d -> (b t) d")).then_inc(q["res_loaded"], 16)
                if v == 1:
                    sp.wait_ge(wh_ready, SPLIT_BEFORE[1.5] + 1)
                    sp.dma_start(wo[:, 1, :, :], src[:, :, 512:D]).then_inc(q["wo_landed"], 16)

        def out_scalar(act):
            meet(act, 1)
            for v, j, t in out_steps():
                act.wait_ge(tile_landed[v % 2], 16 * (v // 2 + 1))
                act.copy(yh[:, v % 2, :, :], yin[:, v % 2, :, :]).then_inc(yh_ready, 1)
                if t == 0:
                    act.wait_ge(q["wo_landed"], 16 * (j + 1))
                    for x in range(4):
                        ks = slice(4 * x, 4 * x + 4)
                        act.copy(woh[j][:, ks, :], wo[:, j, ks, :]).then_inc(wh_ready, 1)

        def out_vector(dve):
            meet(dve, 1)
            def add(v, j, t):
                r = ROWS[t]
                if v == 0:
                    dve.wait_ge(q["res_loaded"], 64)
                dve.wait_ge(q["out_full"], v + 1)
                d = h[0:r, t, 512 * j:512 * (j + 1)]
                dve.tensor_tensor(d, d, bank[P - r:P, v % 2, :], ALU.add).then_inc(q["out_added"], 1)

            for v, j, t in out_steps():
                dve.wait_ge(yh_ready, v + 1)
                dve.tensor_tensor(yl[:, v % 2, :, :], yin[:, v % 2, :, :], yh[:, v % 2, :, :].bitcast(F32), ALU.subtract).then_inc(yl_ready, 1)
                if t == 0:
                    for x in range(4):
                        ks = slice(4 * x, 4 * x + 4)
                        dve.wait_ge(wh_ready, SPLIT_BEFORE[1.5] + 4 * j + x + 1)
                        dve.tensor_tensor(wol[:, j, ks, :], wo[:, j, ks, :], woh[j][:, ks, :].bitcast(F32), ALU.subtract).then_inc(wl_ready, 1)
                if v:
                    add(*out_steps()[v - 1])
            add(*out_steps()[-1])

        def out_tensor(pe):
            meet(pe, 1)
            for v, j, t in out_steps():
                pe.wait_ge(yl_ready, v + 1)
                if v > 1:
                    pe.wait_ge(q["out_added"], v - 1)
                for k in range(DIT):
                    to = bank[:, v % 2, :]
                    if t == 0 and k % 4 == 0:
                        pe.wait_ge(wl_ready, SPLIT_BEFORE[1.5] + 4 * j + k // 4 + 1)
                    pe.matmul(to, yh[:, v % 2, k, :], woh[j][:, k, :], start=(k == 0), stop=False)
                    pe.matmul(to, yh[:, v % 2, k, :], wol[:, j, k, :], start=False, stop=False)
                    last = pe.matmul(to, yl[:, v % 2, k, :], woh[j][:, k, :], start=False, stop=(k == DIT - 1))
                last.then_inc(q["out_full"], 1)

        def out_gpsimd(pool):
            meet(pool, 1)

        s2 = ExitStack()
        sb = sb_in(s2)
        same = ExitStack()
        wg = sb_in(same)("wg", [P, 2, KT, 512])
        same.close()
        wgl = sb("wgl", [P, 2, KT, 512], FR)
        wgh = sb("wgh", [P, 2, KT, 512], FR)
        same = ExitStack()
        pin = sb_in(same)("pin", [P, NT, PLE])
        same.close()
        uL2 = sb("uL2", [P, KT, TOK], FR)
        wp = sb("wp", [P, PLE // P, D])
        pT = sb("pT", [P, PLE // P, TOK])
        gs = square[:, :].rearrange("p (a n) -> p a n", a=2)
        s2.close()
        e = {n: sem("ple_" + n) for n in """p_landed pT_full pT_ready full gate_ready gated
            added stored""".split()}

        wg_landed = [sem(f"wg_landed{j}") for j in range(2)]

        def ple_sync(sp, i, k, last):
            meet(sp, 2 if i == 0 else 6)
            load_gain(sp, k, a["ple_norm_w"][i:i + 1, :])
            sp.dma_start(pin[:, 0:PT, :], a["p_prompt"][i, 0].rearrange("(t p) d -> p t d", p=P)).then_inc(e["p_landed"], 16)
            sp.dma_start(pin[0:SAMP, PT, :], a["p_sample"][i].rearrange("b t d -> (b t) d")).then_inc(e["p_landed"], 16)
            for j in range(2):
                sp.dma_start(wg[:, j, :, :], a["ple_gate_w"][i].rearrange("(k p) n -> p k n", p=P)[:, :, 512 * j:512 * (j + 1)]).then_inc(wg_landed[j], 16)
                if j == 0:
                    sp.dma_start(wp[:, :, :], a["ple_w"][i].rearrange("(k p) n -> p k n", p=P)).then_inc(e["p_landed"], 16)
            if last:
                for t in range(NT):
                    sp.wait_ge(e["added"], 2 * NT * i + NT + t + 1)
                    dst = o["y_prompt"][0, t * P:(t + 1) * P, :] if t < PT else o["y_sample"].rearrange("b t d -> (b t) d")
                    sp.dma_start(dst, h[0:ROWS[t], t, :]).then_inc(e["stored"], 16)
                sp.wait_ge(e["stored"], 16 * NT)

        def ple_scalar(act, i, k):
            meet(act, 2 if i == 0 else 6)

            def high_gate(j):
                act.wait_ge(wg_landed[j], 16 * (i + 1))
                act.copy(wgh[:, j, :, :], wg[:, j, :, :]).then_inc(wh_ready, 1)

            def turned():
                for t in range(NT):
                    r = ROWS[t]
                    act.wait_ge(e["pT_full"], NT * i + t + 1)
                    act.copy(pT[:, :, cols(t)], bank[:, 4 + t % 2, 0:PLE].rearrange("p (k r) -> p k r", k=2)[:, :, 0:r]).then_inc(e["pT_ready"], 1)
                high_gate(0)

            norm_scalar(act, k, low=uL2, amid=turned)
            high_gate(1)
            with act.Fori(0, 2) as j:
                for t in range(NT):
                    r = ROWS[t]
                    v = j * NT + t
                    act.wait_ge(e["full"], v + (2 * NT * i + 1))
                    act.wait_ge(e["added"], v + 2 * NT * i if t < 2 else v + (2 * NT * i - 1))
                    act.activation(gs[0:r, t % 2, :], bank[P - r:P, 2 * (t % 3), :], ACT.Sigmoid).then_inc(e["gate_ready"], 1)

        def ple_gpsimd(pool, i, k):
            meet(pool, 2 if i == 0 else 6)
            norm_gpsimd(pool, k)

        def ple_vector(dve, i, k):
            meet(dve, 2 if i == 0 else 6)
            norm_vector(dve, k, low=uL2)
            for j in range(2):
                dve.wait_ge(wh_ready, SPLIT_BEFORE[2 + 4 * i] + j + 1)
                dve.tensor_tensor(wgl[:, j, :, :], wg[:, j, :, :], wgh[:, j, :, :].bitcast(F32), ALU.subtract).then_inc(wl_ready, 1)
            with dve.Fori(0, 2) as j:
                for t in range(NT):
                    r = ROWS[t]
                    v = j * NT + t
                    g_ = gs[0:r, t % 2, :]
                    dve.wait_ge(e["gate_ready"], v + (2 * NT * i + 1))
                    dve.tensor_tensor(g_, g_, bank[0:r, 2 * (t % 3) + 1, :], ALU.mult).then_inc(e["gated"], 1)
                    dve.wait_ge(e["gated"], v + (2 * NT * i + 1))
                    hv = h[0:r, t, bass.ds(j * 512, 512)]
                    dve.tensor_tensor(hv, hv, g_, ALU.add).then_inc(e["added"], 1)

        def ple_tensor(pe, i, k):
            meet(pe, 2 if i == 0 else 6)
            pe.wait_ge(e["p_landed"], 48 * (i + 1))
            for t in range(NT):
                r = ROWS[t]
                if t > 1:
                    pe.wait_ge(e["pT_ready"], NT * i + t - 1)
                for f in range(PLE // P):
                    last = pe.transpose(bank[:, 4 + t % 2, f * P:f * P + r], pin[0:r, t, f * P:(f + 1) * P], ident[0:r, 0:r])
                last.then_inc(e["pT_full"], 1)
            norm_tensor(pe, k, low=uL2)
            pe.wait_ge(e["pT_ready"], NT * (i + 1))
            pe.wait_ge(uL_ready, NT * (k + 1))
            pe.wait_ge(uT_ready, 2 * NT * (k + 1))
            with pe.Fori(0, 2) as j:
                pe.wait_ge(wl_ready, j + (SPLIT_BEFORE[2 + 4 * i] + 1))
                for t in range(NT):
                    r = ROWS[t]
                    cs = slice(min(t * P, TOK - P), min(t * P, TOK - P) + P)
                    v = j * NT + t
                    pe.wait_ge(e["gated"], v + 2 * NT * i if t < 3 else v + (2 * NT * i - 2))
                    alone(pe)
                    for kk in range(KT):
                        gate_bank = bank[:, 2 * (t % 3), :]
                        whigh, wlow = (x[:, bass.ds(j, 1), kk, :].rearrange("p a n -> p (a n)") for x in (wgh, wgl))
                        pe.matmul(gate_bank, uH[:, kk, cs], whigh, start=(kk == 0), stop=False)
                        pe.matmul(gate_bank, uH[:, kk, cs], wlow, start=False, stop=False)
                        pe.matmul(gate_bank, uL2[:, kk, cs], whigh, start=False, stop=(kk == KT - 1))
                    for kk in range(PLE // P):
                        last = pe.matmul(bank[0:r, 2 * (t % 3) + 1, :], pT[:, kk, cols(t)], wp[:, kk, bass.ds(j * 512, 512)],
                                         start=(kk == 0), stop=(kk == PLE // P - 1))
                    last.then_inc(e["full"], 1)

        s3 = ExitStack()
        sb = sb_in(s3)
        same = ExitStack()
        wr = sb_in(same)("wr", [P, 2, KT, 512])
        same.close()
        wl = sb("wl", [P, 2, KT, 512], FR)
        wh = sb("wh", [P, 2, KT, 512], FR)
        uL = sb("uL", [P, KT, TOK], FR)
        rope = sb("rope", [P, 2, NT, HD])
        tab = sb("tab", [P, 4, NT, HD])
        nw = sb("nw", [P, 2, HD])
        raws = sb("raws", [P, 2, 512])
        sqr = square[:, :].rearrange("p (a n) -> p a n", a=2)
        rot = u[:, :, 0:512]
        swp = u[:, 0, 512:D]
        hs3 = sb("hs3", [P, 3, 8])
        s3.close()
        j3 = {n: sem("proj_" + n) for n in """full raw_ready ms_ready r_ready rot_ready t_landed tab_ready
            kv_out""".split()}
        w3_landed = [sem(f"w3_landed{i}") for i in range(2)]
        stored3 = [sem(f"stored3_{i}") for i in range(2)]
        KVB, QB, GB = 3, 6, 2
        UNITS3 = (KVB + QB + GB) * NT
        kv_flat = s["kv"].rearrange("t c g n -> t (c g n)")
        q_flat = s["q"].rearrange("t g n -> t (g n)")
        kw_src = a["kv_w"].rearrange("(k p) n -> p k n", p=P)
        qw_src = a["a_in_w"][0].rearrange("(k p) n -> p k n", p=P)

        def turn_of(i, times, const):
            return const if i is None else i * times + const

        def blocks3(eng, body, between=lambda: None):
            for b in range(KVB):
                body(None, b, (8, 4, 0)[b], 0)
            between()
            with eng.Fori(0, QB // 2) as i:
                for d in range(2):
                    body(i, KVB + d, 8, 2)
            for b in range(KVB + QB, KVB + QB + GB):
                body(None, b, 0, None)

        SPLIT_AT = 5

        def split_weights(eng, i, nb, scalar):
            sl = nb % 2
            if scalar:
                eng.wait_ge(w3_landed[sl], turn_of(i, 16, 16 * (nb // 2 + 1)))
                eng.copy(wh[:, sl, :, :], wr[:, sl, :, :]).then_inc(wh_ready, 1)
            else:
                eng.wait_ge(wh_ready, turn_of(i, 2, SPLIT_BEFORE[3] + nb + 1))
                eng.tensor_tensor(wl[:, sl, :, :], wr[:, sl, :, :], wh[:, sl, :, :].bitcast(F32), ALU.subtract).then_inc(wl_ready, 1)

        def section3_sync(sp):
            meet(sp, 3)
            load_gain(sp, 2, a["kv_norm_w"].unsqueeze(0))
            for j, n in enumerate(("cos", "sin")):
                at, w = LAYOUT[n]
                sp.dma_start(rope[:, j, :, :], a["consts"][:, at:at + w].rearrange("p (t d) -> p t d", t=NT)).then_inc(j3["t_landed"], 16)
            sp.dma_start(nw[:, 0, :], a["k_norm_w"].unsqueeze(0).broadcast_to([P, HD])).then_inc(j3["t_landed"], 16)
            sp.dma_start(nw[:, 1, :], a["a_q_norm_w"].broadcast_to([P, HD])).then_inc(j3["t_landed"], 16)
            sp.dma_start(wr[:, 0, :, :], kw_src[:, :, 0:512]).then_inc(w3_landed[0], 16)

            def body(i, b, m, tb):
                nb = b + 1
                if nb < KVB + QB + GB:
                    if b:
                        sp.wait_ge(j3["full"], turn_of(i, 2 * NT, b * NT))
                        alone(sp)
                    src = kw_src[:, :, 512 * nb:512 * (nb + 1)] if nb < KVB else \
                        qw_src[:, :, bass.ds(turn_of(i, 1024, 512 * (nb - KVB)), 512)]
                    sp.dma_start(wr[:, nb % 2, :, :], src).then_inc(w3_landed[nb % 2], 16)
                for t in range(NT):
                    r = ROWS[t]
                    par = (b * NT + t) % 2
                    sp.wait_ge(j3["rot_ready"], turn_of(i, 2 * NT, b * NT + t + 1))
                    alone(sp)
                    if b < KVB:
                        dst = kv_flat[cols(t), 512 * b:512 * (b + 1)]
                    elif i is None:
                        dst = s["gate"][cols(t), 512 * (b - KVB - QB):512 * (b - KVB - QB + 1)]
                    else:
                        dst = q_flat[cols(t), bass.ds(turn_of(i, 1024, 512 * (b - KVB)), 512)]
                    sp.dma_start(dst, rot[0:r, par, :]).then_inc(stored3[par], 16)

            def between():
                kvn = KVB * NT
                sp.wait_ge(stored3[0], 16 * ((kvn + 1) // 2))
                sp.wait_ge(stored3[1], 16 * (kvn // 2))
                for g in range(NGR):
                    w = min((128, 512, 2048)[g], SEQ)
                    sp.dma_start(o[f"kv_prompt_g{g + 1}"][0].rearrange("t c h d -> t c (h d)"), s["kv"][SEQ - w:SEQ, :, g, :]).then_inc(j3["kv_out"], 16)
                    sp.dma_start(o[f"kv_sample_g{g + 1}"].rearrange("b t c h d -> (b t) c (h d)"), s["kv"][SEQ:TOK, :, g, :]).then_inc(j3["kv_out"], 16)
                load_gain(sp, 3, a["norm_w"][1:2, :])

            blocks3(sp, body, between)
            sp.wait_ge(stored3[0], 16 * ((UNITS3 + 1) // 2))
            sp.wait_ge(stored3[1], 16 * (UNITS3 // 2))
            sp.wait_ge(j3["kv_out"], 16 * 2 * NGR)

        def section3_tensor(pe):
            meet(pe, 3)
            norm_tensor(pe, 2, low=uL)
            pe.wait_ge(uT_ready, 2 * NT * 3)
            pe.wait_ge(uL_ready, 3 * NT)

            def body(i, b, m, tb):
                pe.wait_ge(wl_ready, turn_of(i, 2, SPLIT_BEFORE[3] + b + 1))
                for t in range(NT):
                    cs = slice(min(t * P, TOK - P), min(t * P, TOK - P) + P)
                    if b or t > 2:
                        pe.wait_ge(j3["raw_ready"], turn_of(i, 2 * NT, b * NT + t - 2))
                    alone(pe)
                    for k in range(KT):
                        high, low = (x[:, k, cs] for x in (uH, uL))
                        whigh, wlow = (x[:, b % 2, k, :] for x in (wh, wl))
                        pe.matmul(bank[:, 4 + t % 3, :], high, whigh, start=(k == 0), stop=False)
                        pe.matmul(bank[:, 4 + t % 3, :], high, wlow, start=False, stop=False)
                        last = pe.matmul(bank[:, 4 + t % 3, :], low, whigh, start=False, stop=(k == KT - 1))
                    last.then_inc(j3["full"], 1)

            def between():
                norm_tensor(pe, 3, low=uL)
                pe.wait_ge(uT_ready, 2 * NT * 4)
                pe.wait_ge(uL_ready, 4 * NT)

            blocks3(pe, body, between)

        def section3_scalar(act):
            meet(act, 3)
            norm_scalar(act, 2, low=uL)
            split_weights(act, None, 0, True)

            def body(i, b, m, tb):
                for t in range(NT):
                    r = ROWS[t]
                    tok = bank[P - r:P, 4 + t % 3, :]
                    if t == SPLIT_AT and b + 1 < KVB + QB + GB:
                        split_weights(act, i, b + 1, True)
                    par = (b * NT + t) % 2
                    act.wait_ge(j3["full"], turn_of(i, 2 * NT, b * NT + t + 1))
                    if b or t > 1:
                        act.wait_ge(j3["rot_ready"], turn_of(i, 2 * NT, b * NT + t - 1))
                    if tb is None:
                        ins = act.activation(raws[0:r, par, :], tok, ACT.Silu)
                    elif tb == 2:
                        v = tok.rearrange("p (a r d) -> p a r d", a=2, d=HD)
                        act.copy(raws[0:r, par, :].rearrange("p (r a d) -> p a r d", a=2, d=HD), v)
                        ins = act.activation(sqr[0:r, par, :].rearrange("p (r a d) -> p a r d", a=2, d=HD), v, ACT.Square)
                    else:
                        ins = act.copy(raws[0:r, par, :], tok)
                        if m:
                            ins = act.activation(sqr[0:r, par, 0:m * HD], tok[:, 0:m * HD], ACT.Square)
                    ins.then_inc(j3["raw_ready"], 1)

            blocks3(act, body, lambda: norm_scalar(act, 3, squares=False, low=uL))

        def section3_gpsimd(pool):
            meet(pool, 3)
            norm_gpsimd(pool, 2)
            count = 0
            for b, m in ((0, 8), (1, 4)):
                for t in range(NT):
                    count += 1
                    pool.wait_ge(j3["ms_ready"], count)
                    pool.tensor_tensor(hs3[0:ROWS[t], 2, 0:m], hs3[0:ROWS[t], 1, 0:m], mhalf[0:ROWS[t], 0:m], ALU.pow).then_inc(j3["r_ready"], 1)
            with pool.Fori(0, QB) as i:
                for t in range(NT):
                    pool.wait_ge(j3["ms_ready"], i * NT + (2 * NT + t + 1))
                    pool.tensor_tensor(hs3[0:ROWS[t], 2, :], hs3[0:ROWS[t], 1, :], mhalf[0:ROWS[t], 0:8], ALU.pow).then_inc(j3["r_ready"], 1)

        def section3_vector(dve, chain):
            meet(dve, 3)
            dve.wait_ge(j3["t_landed"], 64)
            half = HD // 2
            chain(dve.tensor_scalar(nw[:, 1, :], nw[:, 1, :], HD ** -0.5, None, ALU.mult))
            for tb in range(2):
                dve.tensor_tensor(tab[:, 2 * tb, :, :], rope[:, 0, :, :], over(nw[:, tb, :], P, NT, HD), ALU.mult)
                for x in range(2):
                    o_ = slice(x * half, (x + 1) * half)
                    i_ = slice((1 - x) * half, (2 - x) * half)
                    last = dve.tensor_tensor(tab[:, 2 * tb + 1, :, o_], rope[:, 1, :, o_], over(nw[:, tb, i_], P, NT, half), ALU.mult)
            last.then_inc(j3["tab_ready"], 1)
            dve.wait_ge(j3["tab_ready"], 1)
            norm_vector(dve, 2, low=uL)
            split_weights(dve, None, 0, False)

            def body(i, b, m, tb):
                for t in range(NT):
                    r = ROWS[t]
                    if t == SPLIT_AT + 1 and b + 1 < KVB + QB + GB:
                        split_weights(dve, i, b + 1, False)
                    v0 = b * NT + t
                    par = v0 % 2
                    dve.wait_ge(j3["raw_ready"], turn_of(i, 2 * NT, v0 + 1))
                    if v0 > 1:
                        dve.wait_ge(stored3[par], turn_of(i, 16 * NT, 16 * (v0 // 2)))
                    if m:
                        hv = lambda x: x[0:r, 0:m * HD].rearrange("p (m d) -> p m d", m=m)
                        x, out, sw = hv(raws[:, par, :]), hv(rot[:, par, :]), hv(swp)
                        chain(dve.tensor_reduce(hs3[0:r, 0, 0:m], hv(sqr[:, par, :]), AX_X, ALU.add))
                        dve.tensor_scalar(hs3[0:r, 1, 0:m], hs3[0:r, 0, 0:m], 1.0 / HD, EPS, ALU.mult, ALU.add).then_inc(j3["ms_ready"], 1)
                        dve.tensor_tensor(out, x, over(tab[0:r, tb, t, :], r, m, HD), ALU.mult)
                        dve.tensor_tensor(sw[:, :, 0:half], x[:, :, half:], over(tab[0:r, tb + 1, t, 0:half], r, m, half), ALU.mult)
                        chain(dve.tensor_tensor(sw[:, :, half:], x[:, :, 0:half], over(tab[0:r, tb + 1, t, half:], r, m, half), ALU.mult))
                        chain(dve.tensor_tensor(out, out, sw, ALU.add))
                        nm = v0 if b < 2 else turn_of(i, 2 * NT, v0 - NT)
                        dve.wait_ge(j3["r_ready"], nm + 1)
                        ins = dve.tensor_tensor(out, out, bc(hs3[0:r, 2, 0:m], r, m, HD), ALU.mult)
                    if m < 8:
                        ins = dve.tensor_copy(rot[0:r, par, m * HD:], raws[0:r, par, m * HD:])
                    ins.then_inc(j3["rot_ready"], 1)
                    if m:
                        dve.wait_ge(j3["rot_ready"], turn_of(i, 2 * NT, v0 + 1))

            def between():
                kvn = KVB * NT
                dve.wait_ge(stored3[0], 16 * ((kvn + 1) // 2))
                dve.wait_ge(stored3[1], 16 * (kvn // 2))
                norm_vector(dve, 3, squares=False, low=uL)

            for b in range(KVB):
                body(None, b, (8, 4, 0)[b], 0)
            between()
            with dve.Fori(0, QB // 2) as i:
                chain.enter(i, 3 * 2 * NT)
                for d in range(2):
                    body(i, KVB + d, 8, 2)
                chain.leave(QB // 2)
            for b in range(KVB + QB, KVB + QB + GB):
                body(None, b, 0, None)

        s4 = ExitStack()
        sb = sb_in(s4)
        HP = AH // 2
        UN = NGR * PT
        qn = sb("qn", [P, 2, D])
        kn = sb("kn", [P, 2, KVH * HD])
        vv = sb("vv", [P, 2, 2, KVH * HD])
        kT = sb("kT", [P, 2, KVH // 2, 2, P])
        qT = sb("qT", [P, 2, HP, 2, P])
        win = sb("win", [P, 2 * P])
        pair = sb("pair", [P, P])
        sc = sb("sc", [P, 4, 512])
        pT4 = sb("pT4", [P, 2, 512])
        mxs = sb("mxs", [P, 2, 2 * AH])
        nmx = sb("nmx", [P, 2, AH])
        ub = sb("ub", [P, 2, D])
        NTILE = 10
        NEW = NGR * DSEQ
        SW = P + NEW + 8 * P
        smask = sb("smask", [P, SW])
        ck = sb("ck", [P, 2, 9, 2 * KVH * HD])
        nk = sb("nk", [NEW, 2, 2 * KVH * HD])
        ssc = sb("ssc", [P, SW])
        pTs = sb("pTs", [P, NTILE, P])
        qTs = sb("qTs", [P, NGR, 2, P])
        osb = sb("osb", [P, 2, HD])
        st4 = sb("st4", [P, 8])
        qz = uT[:, :, :].rearrange("p k t -> p (k t)")[:, 0:NSEQ * NGR * 2 * P].rearrange("p (s g a d) -> p s g a d", s=NSEQ, g=NGR, a=2)
        qzs = sc[:, :, :].rearrange("p a n -> p (a n)")[:, 0:2 * NGR * 2 * P].rearrange("p (s g a d) -> p s g a d", s=2, g=NGR, a=2)
        kTs = uT[:, :, :].rearrange("p k t -> p (k t)")[:, NSEQ * NGR * 2 * P:NSEQ * NGR * 2 * P + 2 * SW].rearrange("p (a n) -> p a n", a=2)
        s4.close()
        f4 = {n: sem("att_" + n) for n in """m_landed s_full masked p_ready t_full pt_ready pv_done u_taken tr_full
            tr_ready kp_ready zeroed qz_landed os_stored qzs_ready
            ktr_full ktr_ready ss_full ss_masked se_ready rd_ready st_full spt_ready so_full so_ready schain""".split()}
        qk_landed = [sem(f"qk_landed{i}") for i in range(2)]
        v_landed = [sem(f"v_landed{i}") for i in range(2)]
        vp_landed = [sem(f"vp_landed{i}") for i in range(2)]
        ub_stored = [sem(f"ub_stored{i}") for i in range(2)]
        ck_landed = [sem(f"ck_landed{i}") for i in range(2)]

        OWN, FULL = 1, 2

        def head(j, x):
            return 2 * REP * (j // REP) + REP * x + j % REP

        def units4(eng, body):
            body(None, 0, OWN, None, 0)
            body(None, 1, FULL, OWN, 1)
            with eng.Fori(0, 3) as i:
                body(i, 2, FULL, FULL, 1)
                body(i, 3, FULL, FULL, 2)
            body(None, 8, OWN, FULL, 0)
            body(None, 9, FULL, OWN, 5)
            with eng.Fori(0, 3) as i:
                body(i, 10, OWN, FULL, 0)
                body(i, 11, FULL, OWN, 6)
            body(None, 16, OWN, FULL, 0)
            body(None, 17, OWN, OWN, 0)
            with eng.Fori(0, 2) as i:
                body(i, 18, OWN, OWN, 0)
                body(i, 19, OWN, OWN, 0)
            body(None, 22, OWN, OWN, 0)
            body(None, 23, OWN, OWN, 0)

        def sequences(eng, body):
            with eng.Fori(0, NSEQ // 2 - 1) as i:
                for d in range(2):
                    body(i, d)
            for d in (NSEQ - 2, NSEQ - 1):
                body(None, d)

        def rows4(table, i, un, hi):
            g = un // PT
            if g == 0:
                return table[bass.ds(turn_of(i, 2 * P, un * P + 64 * hi), 64), :]
            j = un - g * PT
            if g == 1:
                x = table[0:SEQ, :].rearrange("(p r) n -> r p n", r=4)
                res, at = turn_of(i, 1, j // 2), (j % 2) * P + 64 * hi
            else:
                x = table[0:SEQ, :].rearrange("(p r) n -> r p n", r=16)
                res, at = turn_of(i, 4, 2 * j + hi), 0
            return x[bass.ds(res, 1), at:at + 64, :].rearrange("r p n -> (r p) n")

        def section4_sync(sp):
            meet(sp, 4)
            for tile, name in ((win, "win"), (pair, "pair"), (smask, "smask")):
                at, w = LAYOUT[name]
                sp.dma_start(tile[:, :], a["consts"][:, at:at + w]).then_inc(f4["m_landed"], 16)

            def store(i, un):
                g, sl = un // PT, un % 2
                sp.wait_ge(f4["u_taken"], turn_of(i, 4, 2 * un + 2))
                alone(sp)
                for hi in range(2):
                    ps = slice(64 * hi, 64 * hi + 64)
                    sp.dma_start(rows4(s["u"][g], i, un, hi), ub[ps, sl, :]).then_inc(ub_stored[sl], 16)
                    sp.dma_start(rows4(s["ms"][g], i, un, hi), mxs[ps, sl, :]).then_inc(ub_stored[sl], 16)

            EARLY = (PT, PT + 1, 2 * PT, 2 * PT + 1)

            def load_queries(kv):
                sp.wait_ge(f4["zeroed"], 3)
                for x in range(kv * REP, (kv + 1) * REP):
                    for g in range(NGR):
                        at = (x // (2 * REP) * 2 * REP + x % REP * 2 + kv % 2) * HD
                        src = s["q"][SEQ:TOK, g, at:at + HD].rearrange("(s t) d -> t s d", t=DSEQ)
                        sp.dma_start(qz[x * DSEQ:(x + 1) * DSEQ, :, g, kv // 2, (kv % 2) * HD:(kv % 2 + 1) * HD], src).then_inc(f4["qz_landed"], 16)

            caches = [a[f"cache_kv_g{g}"].rearrange("s t c h d -> s t (c h d)") for g in (1, 2, 3)]

            def load_sequence(i, d):
                sl, one = d % 2, bass.ds(turn_of(i, 2, d), 1)
                c1, c2, c3 = (c[one].rearrange("s t n -> (s t) n") for c in caches)
                sp.dma_start(ck[:, sl, 0, :], c1).then_inc(ck_landed[sl], 16)
                sp.dma_start(ck[:, sl, 1:5, :], c2.rearrange("(i r) n -> i r n", r=4)).then_inc(ck_landed[sl], 16)
                for hi in range(2):
                    sp.dma_start(ck[64 * hi:64 * hi + 64, sl, 5:9, :],
                                 c3.rearrange("(i r) n -> i r n", r=16)[:, hi:8:2, :]).then_inc(ck_landed[sl], 16)
                for g in range(NGR):
                    sp.dma_start(nk[g * DSEQ:(g + 1) * DSEQ, sl, :].rearrange("t (c n) -> t c n", c=2),
                                 s["kv"][bass.ds(turn_of(i, 2 * DSEQ, SEQ + d * DSEQ), DSEQ), :, g, :]).then_inc(ck_landed[sl], 16)

            def body(i, un, kind, before, nth):
                g, sl = un // PT, un % 2
                if un > 1:
                    sp.wait_ge(f4["tr_full"], turn_of(i, 6, 3 * (un - 1)))
                alone(sp)
                for hi in range(2):
                    ps = slice(64 * hi, 64 * hi + 64)
                    sp.dma_start(qn[ps, sl, :], rows4(s["q"][:, g, :], i, un, hi)).then_inc(qk_landed[sl], 16)
                    sp.dma_start(kn[ps, sl, :], rows4(s["kv"][:, 0, g, :], i, un, hi)).then_inc(qk_landed[sl], 16)
                if un > 1:
                    sp.wait_ge(f4["pv_done"], turn_of(i, 16, 8 * (un - 1)))
                alone(sp)
                for hi in range(2):
                    ps = slice(64 * hi, 64 * hi + 64)
                    sp.dma_start(vv[ps, sl, 1, :], rows4(s["kv"][:, 1, g, :], i, un, hi)).then_inc(v_landed[sl], 16)
                    if kind == FULL:
                        sp.dma_start(vv[ps, sl, 0, :], rows4(s["kv"][:, 1, g, :], i, un - 1, hi)).then_inc(vp_landed[sl], 16)
                if un > 1:
                    store(i, un - 2)
                if un in EARLY:
                    load_queries(EARLY.index(un))
                if un >= UN - 2:
                    load_sequence(None, un - (UN - 2))

            units4(sp, body)
            store(None, UN - 2)
            store(None, UN - 1)
            def sample(i, d):
                if d < NSEQ - 2:
                    sp.wait_ge(f4["so_full"], turn_of(i, 2, d + 1))
                    alone(sp)
                    load_sequence(i, d + 2)
                sp.wait_ge(f4["so_ready"], turn_of(i, 2, d + 1))
                alone(sp)
                for x in range(AH):
                    sp.dma_start(s["os"][bass.ds(turn_of(i, 2 * DSEQ, d * DSEQ), DSEQ), x * HD:(x + 1) * HD],
                                 osb[x * DSEQ:(x + 1) * DSEQ, d % 2, :]).then_inc(f4["os_stored"], 16)

            sp.wait_ge(f4["pv_done"], HP * UN)
            sp.dma_start(wo5[:, :, :], a["a_out_w"][0].rearrange("(k p) n -> p k n", p=P)).then_inc(f5["w_landed"], 16)
            sequences(sp, sample)
            sp.wait_ge(f4["os_stored"], 16 * AH * NSEQ)
            sp.wait_ge(ub_stored[0], 64 * (UN // 2))
            sp.wait_ge(ub_stored[1], 64 * (UN // 2))

        def section4_gpsimd(pool):
            meet(pool, 4)
            for x in range(2):
                other = slice(64 * (1 - x), 64 * (1 - x) + 64)
                pool.memset(qT[other, :, :, x, :], 0.0).then_inc(f4["zeroed"], 1)
                pool.wait_ge(f4["zeroed"], x + 1)
            pool.memset(qz, 0.0).then_inc(f4["zeroed"], 1)

            def body(i, un, kind, before, nth):
                if un < UN - 1:
                    nx = un + 1
                    pool.wait_ge(f4["tr_ready"], turn_of(i, 6, 3 * un + 1))
                    pool.wait_ge(f4["s_full"], turn_of(i, 32, 16 * un))
                    alone(pool)
                    pool.tensor_copy(kT[:, nx % 2, :, 0, :], kT[:, un % 2, :, 1, :]).then_inc(f4["kp_ready"], 1)

            units4(pool, body)
            pool.wait_ge(f4["qz_landed"], 16 * AH * NGR)
            pool.wait_ge(f4["t_full"], HP * UN)

            def pick(i, d):
                if d > 1 or i is not None:
                    pool.wait_ge(f4["ktr_full"], turn_of(i, 14, 7 * max(0, d - 1)))
                alone(pool)
                pool.tensor_copy(qzs[:, d % 2, :, :, :], qz[:, bass.ds(turn_of(i, 2, d), 1), :, :, :].rearrange("p s g a d -> p (s g) a d")).then_inc(f4["qzs_ready"], 1)

            sequences(pool, pick)

        def section4_scalar(act):
            meet(act, 4)

            def take(i, un, part):
                sl = un % 2
                act.wait_ge(f4["tr_full"], turn_of(i, 6, 3 * un + part + 1))
                if part == 0:
                    if un:
                        act.wait_ge(f4["kp_ready"], turn_of(i, 2, un - 1))
                    act.copy(kT[:, sl, :, 1, :], bank[:, 7, 0:2 * P].rearrange("p (h n) -> p h n", h=2)).then_inc(f4["tr_ready"], 1)
                else:
                    for x in range(2):
                        hs_ = slice(64 * x, 64 * x + 64)
                        last = act.copy(qT[hs_, sl, 4 * (part - 1):4 * part, x, :], bank[hs_, 7, :].rearrange("p (h n) -> p h n", h=4))
                    last.then_inc(f4["tr_ready"], 1)

            def hand_out(i, un, part):
                sl = un % 2
                act.wait_ge(f4["pv_done"], turn_of(i, 16, 8 * un + 4 * (part + 1)))
                if un > 1 and part == 0:
                    act.wait_ge(ub_stored[sl], turn_of(i, 64, 64 * (un // 2)))
                act.copy(ub[:, sl, part * 512:(part + 1) * 512], bank[:, 4 + part, :]).then_inc(f4["u_taken"], 1)

            act.wait_ge(f4["zeroed"], 2)
            for part in range(3):
                take(None, 0, part)

            def body(i, un, kind, before, nth):
                sl = un % 2
                n = kind * P
                for j in range(HP):
                    st0 = HP * un + j
                    if j in (2, 4, 6) and un < UN - 1:
                        take(i, un + 1, j // 2 - 1)
                    if j == 3 and un:
                        hand_out(i, un - 1, 1)
                    if j == 7:
                        hand_out(i, un, 0)
                    act.wait_ge(f4["masked"], turn_of(i, 16, st0 + 1))
                    if j == 0 and un > 1:
                        act.wait_ge(ub_stored[sl], turn_of(i, 64, 64 * (un // 2)))
                    for x in range(2):
                        v = sc[:, st0 % 4, 256 * x:256 * x + n]
                        last = act.activation(v, v, ACT.Exp, bias=nmx[:, sl, head(j, x):head(j, x) + 1],
                                              accum_out=mxs[:, sl, AH + head(j, x):AH + head(j, x) + 1])
                    last.then_inc(f4["p_ready"], 1)

            units4(act, body)
            hand_out(None, UN - 1, 1)

            def turned(i, d, k):
                act.wait_ge(f4["ktr_full"], turn_of(i, 14, 7 * d + k + 1))
                b = bank[:, 6 + (7 * d + k) % 2, :]
                if k < 5:
                    kTs_copy(act, k, b)
                elif k == 5:
                    act.copy(qTs[:, 0:2, :, :].rearrange("p g a n -> p (g a) n"), b.rearrange("p (x n) -> p x n", x=4)).then_inc(f4["ktr_ready"], 1)
                else:
                    act.copy(qTs[:, 2, :, :], b[:, 0:2 * P].rearrange("p (x n) -> p x n", x=2)).then_inc(f4["ktr_ready"], 1)

            def kTs_copy(act, k, b):
                if k < 4:
                    at = P + NEW + 2 * k * P
                    act.copy(kTs[:, :, at:at + 2 * P], b.rearrange("p (a n) -> p a n", a=2)).then_inc(f4["ktr_ready"], 1)
                else:
                    act.copy(kTs[:, :, 0:P + NEW], b.rearrange("p (a n) -> p a n", a=2)[:, :, 0:P + NEW]).then_inc(f4["ktr_ready"], 1)

            for k in range(7):
                turned(None, 0, k)

            def sample(i, d):
                act.wait_ge(f4["ss_masked"], turn_of(i, 2, d + 1))
                act.activation(ssc[:, :], ssc[:, :], ACT.Exp, bias=st4[:, 4:5], accum_out=st4[:, 5:6]).then_inc(f4["se_ready"], 1)
                if d < NSEQ - 1:
                    for k in range(7):
                        turned(i, d + 1, k)
                act.wait_ge(f4["rd_ready"], turn_of(i, 2, d + 1))
                act.wait_ge(f4["so_full"], turn_of(i, 2, d + 1))
                act.wait_ge(f4["os_stored"], turn_of(i, 32 * AH, 16 * AH * d))
                for kv in range(KVH):
                    ps = slice(32 * kv, 32 * kv + 32)
                    last = act.activation(osb[ps, d % 2, :], bank[ps, 0, kv * HD:(kv + 1) * HD], ACT.Copy, scale=st4[ps, 6:7])
                last.then_inc(f4["so_ready"], 1)

            sequences(act, sample)

        def section4_vector(dve, chain):
            meet(dve, 4)
            dve.wait_ge(f4["m_landed"], 48)

            def evacuate(i, st0, kind):
                dve.wait_ge(f4["t_full"], turn_of(i, 16, st0 + 1))
                if st0 > 1:
                    dve.wait_ge(f4["pv_done"], turn_of(i, 16, st0 - 1))
                dve.tensor_copy(pT4[:, st0 % 2, 0:2 * kind * P], bank[:, 6, 0:2 * kind * P]).then_inc(f4["pt_ready"], 1)

            def body(i, un, kind, before, nth):
                sl, n = un % 2, kind * P
                mask = pair[:, :] if un >= 2 * PT else win[:, 2 * P - n:2 * P]
                if i is not None and un % 2 == 0:
                    chain.enter(i, 2 * HP)
                for j in range(HP):
                    st0 = HP * un + j
                    dve.wait_ge(f4["s_full"], turn_of(i, 32, 2 * (st0 + 1)))
                    if st0 > 3:
                        dve.wait_ge(f4["t_full"], turn_of(i, 16, st0 - 3))
                    if j == 0 and un > 1:
                        dve.wait_ge(ub_stored[sl], turn_of(i, 64, 64 * (un // 2)))
                    alone(dve)
                    for x in range(2):
                        last = dve.tensor_tensor_reduce(sc[:, st0 % 4, 256 * x:256 * x + n], bank[:, 2 * (st0 % 2) + x, 0:n], mask,
                                                        1.0, -3e38, ALU.add, ALU.max, mxs[:, sl, head(j, x):head(j, x) + 1])
                    chain(last)
                    two = slice(head(j, 0), head(j, 1) + 1, REP)
                    dve.tensor_scalar(nmx[:, sl, two], mxs[:, sl, two], -1.0, None, ALU.mult).then_inc(f4["masked"], 1)
                    if st0 > 1:
                        evacuate(i, st0 - 2, kind if j > 1 else before)
                if i is not None and un % 2 == 1:
                    chain.leave({3: 3, 11: 3, 19: 2}[un])

            units4(dve, body)
            evacuate(None, HP * UN - 2, OWN)
            evacuate(None, HP * UN - 1, OWN)

            def sample(i, d):
                dve.wait_ge(f4["ss_full"], turn_of(i, 2, d + 1))
                dve.wait_ge(f4["st_full"], turn_of(i, 6, 3 * d))
                dve.wait_ge(f4["so_ready"], turn_of(i, 2, d))
                alone(dve)
                for b, (c0, c1) in enumerate(((0, P + NEW), (P + NEW, P + NEW + 512), (P + NEW + 512, SW))):
                    last = dve.tensor_tensor_reduce(ssc[:, c0:c1], bank[:, b, 0:c1 - c0], smask[:, c0:c1], 1.0, -3e38,
                                                    ALU.add, ALU.max, st4[:, b:b + 1])
                last.then_inc(f4["schain"], 1)
                dve.wait_ge(f4["schain"], turn_of(i, 4, 2 * d + 1))
                dve.tensor_reduce(st4[:, 3:4], st4[:, 0:3], AX_X, ALU.max).then_inc(f4["schain"], 1)
                dve.wait_ge(f4["schain"], turn_of(i, 4, 2 * d + 2))
                dve.tensor_scalar(st4[:, 4:5], st4[:, 3:4], -1.0, None, ALU.mult).then_inc(f4["ss_masked"], 1)
                dve.wait_ge(f4["se_ready"], turn_of(i, 2, d + 1))
                dve.reciprocal(st4[:, 6:7], st4[:, 5:6]).then_inc(f4["rd_ready"], 1)
                for b in range(3):
                    dve.wait_ge(f4["st_full"], turn_of(i, 6, 3 * d + b + 1))
                    dve.wait_ge(f4["so_full"], turn_of(i, 2, d))
                    if b < 2:
                        ins = dve.tensor_copy(pTs[:, 2 + 4 * b:6 + 4 * b, :].rearrange("p x n -> p (x n)"), bank[:, 3 + b, :])
                    else:
                        dve.tensor_copy(pTs[:, 0, :], bank[:, 5, 0:P])
                        ins = dve.tensor_copy(pTs[0:NEW, 1, :], bank[0:NEW, 5, P:2 * P])
                    ins.then_inc(f4["spt_ready"], 1)

            sequences(dve, sample)

        def section4_tensor(pe):
            meet(pe, 4)

            def turn(i, un, part):
                sl = un % 2
                if part == 0:
                    pe.wait_ge(qk_landed[sl], turn_of(i, 64, 64 * (un // 2 + 1)))
                if un or part:
                    pe.wait_ge(f4["tr_ready"], turn_of(i, 6, 3 * un + part))
                if part == 0:
                    for x in range(KVH // 2):
                        last = pe.transpose(bank[:, 7, x * P:(x + 1) * P], kn[:, sl, x * P:(x + 1) * P], ident)
                else:
                    for x in range(REP):
                        f = REP * (part - 1) + x
                        last = pe.transpose(bank[:, 7, x * P:(x + 1) * P], qn[:, sl, f * P:(f + 1) * P], ident)
                last.then_inc(f4["tr_full"], 1)

            def turn_scores(i, st0, kind):
                pe.wait_ge(f4["p_ready"], turn_of(i, 16, st0 + 1))
                if st0 > 0:
                    pe.wait_ge(f4["pt_ready"], turn_of(i, 16, st0))
                for x in range(2):
                    for k in range(kind):
                        last = pe.transpose(bank[:, 6, (x * kind + k) * P:(x * kind + k + 1) * P],
                                            sc[:, st0 % 4, 256 * x + k * P:256 * x + (k + 1) * P], ident)
                last.then_inc(f4["t_full"], 1)

            def values(i, un, j, kind, nth):
                st0 = HP * un + j
                sl = un % 2
                pe.wait_ge(f4["pt_ready"], turn_of(i, 16, st0 + 1))
                if j == 0:
                    pe.wait_ge(v_landed[sl], turn_of(i, 32, 32 * (un // 2 + 1)))
                    if kind == FULL:
                        pe.wait_ge(vp_landed[sl], turn_of(i, 32, 32 * nth))
                if j in (0, 4) and un:
                    pe.wait_ge(f4["u_taken"], turn_of(i, 4, 2 * un - 1 + j // 4))
                for x in range(2):
                    hd = head(j, x)
                    for k in range(kind):
                        last = pe.matmul(bank[:, 4 + hd // 8, (hd % 8) * HD:(hd % 8 + 1) * HD],
                                         pT4[:, st0 % 2, (x * kind + k) * P:(x * kind + k + 1) * P],
                                         vv[:, sl, k + 2 - kind, (hd // REP) * HD:(hd // REP + 1) * HD], start=(k == 0), stop=(k == kind - 1))
                last.then_inc(f4["pv_done"], 1)

            for part in range(3):
                turn(None, 0, part)

            def body(i, un, kind, before, nth):
                sl, n = un % 2, kind * P
                pe.wait_ge(f4["tr_ready"], turn_of(i, 6, 3 * (un + 1)))
                if un:
                    pe.wait_ge(f4["kp_ready"], turn_of(i, 2, un))
                for j in range(HP):
                    st0 = HP * un + j
                    if st0 > 1:
                        pe.wait_ge(f4["masked"], turn_of(i, 16, st0 - 1))
                    for x in range(2):
                        pe.matmul(bank[:, 2 * (st0 % 2) + x, 0:n], qT[:, sl, j, x, :],
                                  kT[:, sl, j // REP, 2 - kind:2, :].rearrange("p a n -> p (a n)"), start=True, stop=True).then_inc(f4["s_full"], 1)
                    if st0 > 1:
                        turn_scores(i, st0 - 2, kind if j > 1 else before)
                    if st0 > 2:
                        if j > 2:
                            values(i, un, j - 3, kind, nth)
                        else:
                            values(i, un - 1, j + HP - 3, before, 0)
                    if j in (1, 3, 5) and un < UN - 1:
                        turn(i, un + 1, j // 2)

            units4(pe, body)
            turn_scores(None, HP * UN - 2, OWN)
            values(None, UN - 1, HP - 3, OWN, 0)
            turn_scores(None, HP * UN - 1, OWN)
            values(None, UN - 1, HP - 2, OWN, 0)
            values(None, UN - 1, HP - 1, OWN, 0)

            def turn_keys(i, d, batches):
                sl = d % 2
                if 0 in batches:
                    pe.wait_ge(ck_landed[sl], turn_of(i, 112, 112 * (d // 2 + 1)))
                for k in batches:
                    n0 = 7 * d + k
                    if n0 > 1:
                        pe.wait_ge(f4["ktr_ready"], turn_of(i, 14, n0 - 1))
                    b = bank[:, 6 + n0 % 2, :]
                    if k < 4:
                        for x in range(2):
                            for pr in range(2):
                                last = pe.transpose(b[:, (2 * pr + x) * P:(2 * pr + x + 1) * P], ck[:, sl, 1 + 2 * k + x, pr * P:(pr + 1) * P], ident)
                    elif k == 4:
                        for pr in range(2):
                            pe.transpose(b[:, 2 * pr * P:(2 * pr + 1) * P], ck[:, sl, 0, pr * P:(pr + 1) * P], ident)
                            last = pe.transpose(b[:, (2 * pr + 1) * P:(2 * pr + 1) * P + NEW], nk[:, sl, pr * P:(pr + 1) * P], ident[0:NEW, 0:NEW])
                    else:
                        if k == 5:
                            pe.wait_ge(f4["qzs_ready"], turn_of(i, 2, d + 1))
                        for x in range(4 if k == 5 else 2):
                            g = 2 * (k - 5) + x // 2
                            last = pe.transpose(b[:, x * P:(x + 1) * P], qzs[:, sl, g, x % 2, :], ident)
                    last.then_inc(f4["ktr_full"], 1)

            def sample(i, d):
                sl = d % 2
                pe.wait_ge(f4["ktr_ready"], turn_of(i, 14, 7 * (d + 1)))
                pe.wait_ge(f4["so_ready"], turn_of(i, 2, d))
                pe.wait_ge(f4["ss_masked"], turn_of(i, 2, d))
                new = [(g, 0, P + g * DSEQ, P + (g + 1) * DSEQ, P + g * DSEQ) for g in range(NGR)]
                for g, b, c0, c1, at in [(0, 0, 0, P, 0)] + new + [(1, 1, P + NEW, P + NEW + 512, 0), (2, 2, P + NEW + 512, SW, 0)]:
                    for pr in range(2):
                        last = pe.matmul(bank[:, b, at:at + c1 - c0], qTs[:, g, pr, :], kTs[:, pr, c0:c1], start=(pr == 0), stop=(pr == 1))
                last.then_inc(f4["ss_full"], 1)
                if d < NSEQ - 1:
                    turn_keys(i, d + 1, range(0, 2))
                pe.wait_ge(f4["se_ready"], turn_of(i, 2, d + 1))
                pe.wait_ge(f4["spt_ready"], turn_of(i, 6, 3 * d))
                for b in range(2):
                    for x in range(4):
                        at = P + NEW + (4 * b + x) * P
                        last = pe.transpose(bank[:, 3 + b, x * P:(x + 1) * P], ssc[:, at:at + P], ident)
                    last.then_inc(f4["st_full"], 1)
                pe.transpose(bank[:, 5, 0:P], ssc[:, 0:P], ident)
                pe.transpose(bank[0:NEW, 5, P:2 * P], ssc[:, P:P + NEW], ident).then_inc(f4["st_full"], 1)
                if d < NSEQ - 1:
                    turn_keys(i, d + 1, range(2, 7))
                pe.wait_ge(f4["spt_ready"], turn_of(i, 6, 3 * (d + 1)))
                vals = [ck[:, sl, 0, KVH * HD:]] + [nk[:, sl, KVH * HD:]] + [ck[:, sl, 1 + x, KVH * HD:] for x in range(8)]
                for x, v in enumerate(vals):
                    r = NEW if x == 1 else P
                    last = pe.matmul(bank[:, 0, 0:KVH * HD], pTs[0:r, x, :], v, start=(x == 0), stop=(x == NTILE - 1))
                last.then_inc(f4["so_full"], 1)

            turn_keys(None, 0, range(7))
            sequences(pe, sample)

        s5 = ExitStack()
        sb = sb_in(s5)
        same = ExitStack()
        wo5 = sb_in(same)("wo5", [P, KT, D])
        same.close()
        wl5 = sb("wl5", [P, KT, D], FR)
        wh5 = uH[:, :, 0:D]
        u3 = sb("u3", [P, 2, NGR, D])
        m3 = sb("m3", [P, 2, NGR, 2 * AH])
        gate = sb("gate", [P, 2, D])
        wts = sb("wts", [P, 5, NGR, AH])
        y5 = sb("y5", [P, 2, D])
        yT5 = sb("yT5", [P, 2, 2, KT, P], FR)
        s5.close()
        f5 = {n: sem("last_" + n) for n in """w_landed e_in e_ready w_ready third y_ready t_full t_ready
            full added low_ready""".split()}
        in5 = tile_landed
        BEFORE5 = 16 * NT

        def tiles5(eng, body):
            with eng.Fori(0, PT // 2) as i:
                for t in range(2):
                    body(i, t)
            body(None, PT)

        def section5_sync(sp):
            meet(sp, 5)

            def body(i, t):
                sl, r = t % 2, ROWS[t]
                rows = bass.ds(turn_of(i, 2 * P, t * P), r)
                sp.wait_ge(f5["y_ready"], turn_of(i, 2, t + 1))
                alone(sp)
                sp.dma_start(gate[0:r, sl, :], s["gate"][rows, :]).then_inc(in5[sl], 16)
                if t < PT:
                    for g in range(NGR):
                        sp.dma_start(u3[:, sl, g, :], s["u"][g][rows, :]).then_inc(in5[sl], 16)
                        sp.dma_start(m3[:, sl, g, :], s["ms"][g][rows, :]).then_inc(in5[sl], 16)
                else:
                    sp.wait_ge(f5["t_full"], PT - 1)
                    sp.dma_start(y5[0:r, sl, :], s["os"]).then_inc(in5[sl], 16)

            tiles5(sp, body)

        def section5_gpsimd(pool):
            meet(pool, 5)

            def body(i, t):
                if t == PT:
                    return
                pool.wait_ge(f5["w_ready"], turn_of(i, 2, t + 1))
                v = u3[:, t % 2, 2, :].rearrange("p (h d) -> p h d", h=AH)
                pool.tensor_tensor(v, v, bc(wts[:, 4, 2, :], P, AH, HD), ALU.mult).then_inc(f5["third"], 1)

            tiles5(pool, body)

        def section5_scalar(act):
            meet(act, 5)

            act.wait_ge(f5["w_landed"], 16)
            for x in range(4):
                ks = slice(2 * x, 2 * x + 2)
                act.copy(wh5[:, ks, :], wo5[:, ks, :]).then_inc(wh_ready, 1)

            def body(i, t):
                sl, r = t % 2, ROWS[t]
                if t < PT:
                    act.wait_ge(f5["e_in"], turn_of(i, 2, t + 1))
                    act.activation(wts[:, 1, :, :], wts[:, 0, :, :], ACT.Exp).then_inc(f5["e_ready"], 1)
                act.wait_ge(f5["t_full"], turn_of(i, 2, t + 1))
                for half in range(2):
                    b = bank[:, 2 * sl + half, :].rearrange("p (k n) -> p k n", k=4)[:, :, 0:r]
                    last = act.copy(yT5[:, sl, 0, 4 * half:4 * half + 4, 0:r], b)
                last.then_inc(f5["t_ready"], 1)

            tiles5(act, body)

        def section5_vector(dve, chain):
            meet(dve, 5)

            def low_part(i, t):
                sl, r = t % 2, ROWS[t]
                dve.wait_ge(f5["t_ready"], turn_of(i, 2, t + 1))
                for half in range(2):
                    b = bank[:, 2 * sl + half, :].rearrange("p (k n) -> p k n", k=4)[:, :, 0:r]
                    part = slice(4 * half, 4 * half + 4)
                    last = dve.tensor_tensor(yT5[:, sl, 1, part, 0:r], b, yT5[:, sl, 0, part, 0:r].bitcast(F32), ALU.subtract)
                last.then_inc(f5["low_ready"], 1)

            def finish(i, t):
                sl, r = t % 2, ROWS[t]
                dve.wait_ge(f5["full"], turn_of(i, 2, t + 1))
                for half in range(2):
                    hv = h[0:r, bass.ds(turn_of(i, 2, t), 1), 512 * half:512 * (half + 1)].rearrange("p t n -> p (t n)")
                    last = dve.tensor_tensor(hv, hv, bank[0:r, 4 + 2 * sl + half, :], ALU.add)
                last.then_inc(f5["added"], 1)

            def body(i, t):
                sl, r = t % 2, ROWS[t]
                if t == PT:
                    dve.wait_ge(in5[0], BEFORE5 + 16 * 7 * (PT // 2) + 32)
                    dve.tensor_tensor(y5[0:r, sl, :], y5[0:r, sl, :], gate[0:r, sl, :], ALU.mult).then_inc(f5["y_ready"], 1)
                else:
                    dve.wait_ge(in5[sl], turn_of(i, 112, BEFORE5 + 112 * (t // 2 + 1)))
                    mx = lambda g: m3[:, sl, g, 0:AH]
                    top = wts[:, 2, 0, :]
                    chain(dve.tensor_tensor(top, mx(0), mx(1), ALU.max))
                    chain(dve.tensor_tensor(top, top, mx(2), ALU.max))
                    dve.tensor_tensor(wts[:, 0, :, :], m3[:, sl, :, 0:AH], over(top, P, NGR, AH), ALU.subtract).then_inc(f5["e_in"], 1)
                    dve.wait_ge(f5["e_ready"], turn_of(i, 2, t + 1))
                    chain(dve.tensor_tensor(wts[:, 3, :, :], wts[:, 1, :, :], m3[:, sl, :, AH:], ALU.mult))
                    chain(dve.tensor_tensor(top, wts[:, 3, 0, :], wts[:, 3, 1, :], ALU.add))
                    chain(dve.tensor_tensor(top, top, wts[:, 3, 2, :], ALU.add))
                    chain(dve.reciprocal(top, top))
                    dve.wait_ge(f5["third"], turn_of(i, 2, t))
                    dve.tensor_tensor(wts[:, 4, :, :], wts[:, 1, :, :], over(top, P, NGR, AH), ALU.mult).then_inc(f5["w_ready"], 1)
                    dve.wait_ge(f5["w_ready"], turn_of(i, 2, t + 1))
                    uv = lambda g: u3[:, sl, g, :].rearrange("p (h d) -> p h d", h=AH)
                    yv = y5[:, sl, :]
                    if t > 1 or i is not None:
                        dve.wait_ge(f5["t_full"], turn_of(i, 2, t - 1))
                    dve.tensor_tensor(yv.rearrange("p (h d) -> p h d", h=AH), uv(0), bc(wts[:, 4, 0, :], P, AH, HD), ALU.mult)
                    chain(dve.tensor_tensor(uv(1), uv(1), bc(wts[:, 4, 1, :], P, AH, HD), ALU.mult))
                    chain(dve.tensor_tensor(yv, yv, u3[:, sl, 1, :], ALU.add))
                    dve.wait_ge(f5["third"], turn_of(i, 2, t + 1))
                    chain(dve.tensor_tensor(yv, yv, u3[:, sl, 2, :], ALU.add))
                    dve.tensor_tensor(yv, yv, gate[:, sl, :], ALU.mult).then_inc(f5["y_ready"], 1)

            def step(i, t):
                low_part(i, t)
                if t < PT:
                    body(i, t + 1)
                finish(i, t)

            dve.sem_inc(f5["y_ready"], 2)
            for x in range(4):
                ks = slice(2 * x, 2 * x + 2)
                dve.wait_ge(wh_ready, SPLIT_BEFORE[5] + x + 1)
                dve.tensor_tensor(wl5[:, ks, :], wo5[:, ks, :], wh5[:, ks, :].bitcast(F32), ALU.subtract).then_inc(wl_ready, 1)
            body(None, 0)
            with dve.Fori(0, PT // 2 - 1) as i:
                chain.enter(i, 18)
                step(i, 0)
                step(i, 1)
                chain.leave(PT // 2 - 1)
            for t in range(PT - 2, NT):
                step(None, t)

        def section5_tensor(pe):
            meet(pe, 5)

            def body(i, t):
                sl, r = t % 2, ROWS[t]
                pe.wait_ge(f5["y_ready"], turn_of(i, 2, t + 3))
                pe.wait_ge(f5["t_ready"], turn_of(i, 2, max(0, t - 1)))
                for f in range(KT):
                    last = pe.transpose(bank[:, 2 * sl + f // 4, (f % 4) * P:(f % 4) * P + r], y5[0:r, sl, f * P:(f + 1) * P], ident[0:r, 0:r])
                last.then_inc(f5["t_full"], 1)
                pe.wait_ge(f5["low_ready"], turn_of(i, 2, t + 1))
                if t == 0:
                    pe.wait_ge(wl_ready, SPLIT_BEFORE[5] + 4)
                pe.wait_ge(f5["added"], turn_of(i, 2, 0) if t < 2 else PT)
                for half in range(2):
                    for k in range(KT):
                        high, low = (yT5[:, sl, x, k, :] for x in range(2))
                        whigh, wlow = (x[:, k, 512 * half:512 * (half + 1)] for x in (wh5, wl5))
                        pe.matmul(bank[:, 4 + 2 * sl + half, :], high, whigh, start=(k == 0), stop=False)
                        pe.matmul(bank[:, 4 + 2 * sl + half, :], high, wlow, start=False, stop=False)
                        last = pe.matmul(bank[:, 4 + 2 * sl + half, :], low, whigh, start=False, stop=(k == KT - 1))
                last.then_inc(f5["full"], 1)

            tiles5(pe, body)


        @block.sync
        def _(sp):
            sp.dma_start(h[:, 0:PT, :], a["x_prompt"][0].rearrange("(t p) d -> p t d", p=P)).then_inc(q["res_loaded"], 16)
            sp.dma_start(h[0:SAMP, PT, :], a["x_sample"].rearrange("b t d -> (b t) d")).then_inc(q["res_loaded"], 16)
            load_gain(sp, 0, a["norm_w"][0:1, :])
            sp.dma_start(cst[:, :], a["consts"][:, 0:NMASK]).then_inc(q["const_loaded"], 16)
            sp.dma_start(wdt[:, :, :], in_w[:, :, DTCOL + NH - P:DTCOL + NH]).then_inc(q["vec_loaded"], 16)
            for j, n in enumerate(("m_dt_bias", "m_A_log", "m_D")):
                sp.dma_start(vec[:, j * NH:(j + 1) * NH], a[n].broadcast_to([P, NH])).then_inc(q["vec_loaded"], 16)
            sp.dma_start(cw_rows[0:CK * CONVF, :], a["m_conv_w"][0].rearrange("k (f p) -> (k f) p", p=P)).then_inc(q["cw_loaded"], 16)
            sp.dma_start(cw_rows[CK * CONVF:(CK + 1) * CONVF, :], a["m_conv_b"][0].rearrange("(f p) -> f p", p=P)).then_inc(q["cw_loaded"], 16)
            sp.dma_start(sc_rows, a["state_conv"].rearrange("x s k (c n) -> (x s k) c n", c=3)).then_inc(q["cw_loaded"], 16)
            for f in range(2):
                sp.dma_start(wx[:, f, :, :], in_w[:, :, XCOL + f * P:XCOL + (f + 1) * P]).then_inc(wx_landed[f], 16)
            sp.wait_ge(u_ready, NT)
            with sp.Fori(0, NG) as g:
                for f in range(2, CF + 2):
                    n = f % CF
                    col = [(g + f // CF) * GW + XCOL + n * P, g * DS + BCOL, g * DS + CCOL][max(0, n - XF + 1)]
                    sp.wait_ge(q["xg_full"], g * CF + (f - 1))
                    alone(sp)
                    sp.dma_start(wx[:, f % 2, :, :], in_w[:, :, bass.ds(col, P)]).then_inc(wx_landed[f % 2], 16)
                    if f == 2:
                        sp.wait_ge(q["z_full"], g * NT)
                        alone(sp)
                        sp.dma_start(wz[:, :, :], in_w[:, :, bass.ds(g * GW, GW)]).then_inc(q["wz_landed"], 16)
                        sp.wait_ge(q["yn_ready"], g * NT)
                        alone(sp)
                        sp.dma_start(nwg[:, :], a["m_norm_w"][:, bass.ds(g * GW, GW)].broadcast_to([P, GW])).then_inc(q["nw_landed"], 16)

                def load_state(n):
                    sp.dma_start(st[:, n % 4, :, :],
                                 st_in[bass.ds(g * GW, GW), n, :].rearrange("(f p) n -> p f n", p=P)).then_inc(st_landed[n % 4], 16)

                sp.wait_ge(q["conv_done"], g * CF + CF)
                alone(sp)
                for n in range(4):
                    load_state(n)

                def store_y(c):
                    sp.wait_ge(q["yT_ready"], g * NT + c + 1)
                    alone(sp)
                    sp.dma_start(s["yT"][bass.ds(g * GW, GW), cols(c)].rearrange("(f p) t -> p f t", p=P),
                                 yT[:, :, 0:ROWS[c]]).then_inc(q["yT_stored"], 16)

                for c in range(LC):
                    store_y(c)
                for n in range(NSEQ):
                    sp.wait_ge(q["snew_ready"], g * NSEQ + n + 1)
                    alone(sp)
                    sp.dma_start(st_out[bass.ds(g * GW, GW), n, :].rearrange("(f p) n -> p f n", p=P),
                                 st[:, n % 4, :, :]).then_inc(q["state_stored"], 16)
                    if n + 4 < NSEQ:
                        sp.wait_ge(q["state_stored"], g * (16 * NSEQ) + 16 * (n + 1))
                        alone(sp)
                        load_state(n + 4)
                sp.wait_ge(q["fin_ready"], g + 1)
                alone(sp)
                sp.wait_ge(q["state_stored"], g * (16 * NSEQ) + 16 * NSEQ)
                alone(sp)
                sp.dma_start(st_prompt[bass.ds(g * GW, GW), :].rearrange("(f p) n -> p f n", p=P),
                             h0T[:, 0, :].rearrange("p (f n) -> p f n", f=XF)).then_inc(q["fin_stored"], 16)
                store_y(LC)
            sp.wait_ge(q["yT_stored"], 16 * NT * NG)
            for f in range(2):
                sp.wait_ge(wx_landed[f], NG * 48 + 16)
            sp.wait_ge(q["fin_stored"], 16 * NG)
            sp.wait_ge(q["tail_ready"], CONVF // 4)
            sp.dma_start(o["conv_prompt"].rearrange("x b k (c n) -> (x b k) c n", c=3), tail_rows[0:CK - 1, :, :]).then_inc(q["fin_stored"], 16)
            sp.dma_start(o["conv_sample"].rearrange("x s k (c n) -> (x s k) c n", c=3), tail_rows[CK - 1:TAIL, :, :]).then_inc(q["fin_stored"], 16)
            sp.wait_ge(q["fin_stored"], 16 * NG + 32)
            out_sync(sp)
            ple_sync(sp, 0, 1, False)
            section3_sync(sp)
            section4_sync(sp)
            section5_sync(sp)
            ple_sync(sp, 1, 4, True)

        @block.gpsimd
        def _(pool):
            pool.memset(mhalf[:, :], -0.5).then_inc(q["memset_done"], 1)
            pool.memset(ss[:, :], 1.0).then_inc(q["memset_done"], 1)
            pool.memset(ones[:, :], 1.0).then_inc(q["memset_done"], 1)
            pool.memset(raw[:, :, 0:CK - 1], 0.0).then_inc(q["memset_done"], 1)
            pool.wait_ge(q["memset_done"], 4)
            norm_gpsimd(pool, 0)
            pool.wait_ge(q["dt_ready"], 2)
            pool.wait_ge(q["const_loaded"], 16)
            pool.wait_ge(q["vec_loaded"], 64)

            def decay_sums(g, c, n):
                r = ROWS[c]
                alone(pool)
                tri = con("tri" if c < LC else "tri8", r)[:, 0:r]
                out = mix[0:r, c % 2, 0:HG * r].rearrange("p (h l) -> p h l", h=HG)
                pool.tensor_tensor(out, over(tri, r, HG, r), bc(dta[0:r, c, bass.ds(g * HG, HG)], r, HG, r),
                                   ALU.mult).then_inc(q["sum_ready"], 1)

            with pool.Fori(0, NG) as g:
                for c in range(NT):
                    n = g * NT + c
                    r = ROWS[c]
                    if c == 0:
                        pool.wait_ge(q["yd_full"], n)
                        decay_sums(g, 0, n)
                    v = xt[0:r, :].rearrange("p (h d) -> p h d", h=HG)
                    pool.wait_ge(q["xdt_ready"], n + 1)
                    alone(pool)
                    pool.tensor_tensor(v, v,
                                       bc(vec[0:r, bass.ds(g * HG + 2 * NH, HG)], r, HG, HD), ALU.mult).then_inc(q["skip_ready"], 1)
                    if c:
                        pool.wait_ge(q["st_full"], g * LC + c)
                    else:
                        pool.wait_ge(q["snew_full"], g * NSEQ)
                    alone(pool)
                    pool.tensor_tensor(xdtd[0:r, :].rearrange("p (h d) -> p h d", h=HG),
                                       xdt[0:r, :].rearrange("p (h d) -> p h d", h=HG),
                                       bc(dend[0:r, c, bass.ds(g * HG, HG)], r, HG, HD), ALU.mult).then_inc(q["xdtd_ready"], 1)
                    if c + 1 < NT:
                        if c:
                            pool.wait_ge(q["yd_full"], n)
                        decay_sums(g, c + 1, n + 1)
                    pool.wait_ge(q["msy_ready"], n + 1)
                    pool.tensor_tensor(ybuf[0:r, 2:3], ybuf[0:r, 1:2], mhalf[0:r, 0:1], ALU.pow).then_inc(q["ry_ready"], 1)
            out_gpsimd(pool)
            ple_gpsimd(pool, 0, 1)
            section3_gpsimd(pool)
            section4_gpsimd(pool)
            section5_gpsimd(pool)
            ple_gpsimd(pool, 1, 4)

        @block.scalar
        def _(act):
            act.wait_ge(q["memset_done"], 4)
            act.wait_ge(q["res_loaded"], 32)
            norm_scalar(act, 0, low=uL1)
            act.wait_ge(q["vec_loaded"], 64)
            act.copy(wdth[:, :, :], wdt[:, :, :]).then_inc(wh_ready, 1)
            act.wait_ge(q["turned_full"], 1)
            act.copy(cw[:, :], bank[:, 4, 0:(CK + 1) * CONVF]).then_inc(q["turned_ready"], 1)
            for j in range(2):
                act.wait_ge(q["turned_full"], j + 2)
                w = NSEQ * (CK - 1)
                act.copy(sct[:, 12 * j:12 * j + 12, :].rearrange("p f w -> p (f w)"), bank[:, 5 + j, 0:12 * w]).then_inc(q["turned_ready"], 1)
            act.wait_ge(q["dt_full"], 1)
            for j, (c0, c1) in enumerate(zip(CUTS, CUTS[1:])):
                last = act.copy(dtT[:, c0:c1], bank[:, j, 0:c1 - c0])
            last.then_inc(q["turned_ready"], 1)
            chain = Chain(act, q["achain"])
            act.wait_ge(q["dt_ready"], 1)
            chain(act.activation(tiny[:, 1, :], tiny[:, 0, :], ACT.Abs))
            chain(act.activation(tiny[:, 2, :], tiny[:, 1, :], ACT.Exp, scale=-1.0))
            act.activation(tiny[:, 3, :], tiny[:, 2, :], ACT.Ln, bias=1.0).then_inc(q["acum_ready"], 1)
            act.activation(vec[:, NH:2 * NH], vec[:, NH:2 * NH], ACT.Exp).then_inc(q["acum_ready"], 1)
            act.wait_ge(q["acum_full"], 2)
            for b, dst in ((5, ea), (6, dec)):
                act.activation(dst[:, 0:PT, :], bank[:, b, 0:PT * NH].rearrange("p (t h) -> p t h", t=PT), ACT.Exp)
                act.activation(dst[0:SAMP, PT, :], bank[0:SAMP, b, PT * NH:NT * NH], ACT.Exp).then_inc(q["acum_ready"], 1)
            act.wait_ge(q["dt_ready"], 3)
            act.activation(dend[:, :, :].rearrange("p t h -> p (t h)"), tiny[:, 4, :], ACT.Exp).then_inc(q["acum_ready"], 1)
            act.wait_ge(q["memset_done"], 4)
            act.wait_ge(q["turned_ready"], 3)
            W = CK + 1

            def high_x(g, f):
                act.wait_ge(wx_landed[f % 2], g * 48 + 16 * (f // 2 + 1))
                act.copy(wxh[:, f % 2, :, :], wx[:, f % 2, :, :]).then_inc(wh_ready, 1)

            high_x(0, 0)
            with act.Fori(0, NG) as g:
                cwv = cw[:, :].rearrange("p (k f) -> p f k", k=W)
                act.wait_ge(q["conv_done"], g * CF)
                act.copy(cwg[:, 0:XF, :], cwv[:, bass.ds(g * XF, XF), :])
                act.copy(cwg[:, XF, :], cwv[:, bass.ds(g + NG * XF, 1), :].rearrange("p f k -> p (f k)"))
                act.copy(cwg[:, XF + 1, :], cwv[:, bass.ds(g + NG * XF + NG, 1), :].rearrange("p f k -> p (f k)")).then_inc(q["cwg_ready"], 1)
                act.wait_ge(q["state_stored"], g * (16 * NSEQ))
                for f in range(CF + 1):
                    if f + 1 < CF:
                        high_x(g, f + 1)
                    if f == CF - 2:
                        act.wait_ge(q["wz_landed"], g * 16 + 16)
                        act.copy(wzh[:, :, :], wz[:, :, :]).then_inc(wh_ready, 1)
                    if f < CF:
                        ft = [g * XF + f, g + NG * XF, g + NG * XF + NG][max(0, f - XF + 1)]
                        act.wait_ge(q["conv_done"], g * CF + max(0, f - 1))
                        rs = raw[:, f % 2, SOFF:RAWW].rearrange("p (s w) -> p s w", s=NSEQ)
                        act.copy(rs[:, :, 0:CK - 1], sct[:, bass.ds(ft, 1), :].rearrange("p f (s w) -> p (f s) w", s=NSEQ))
                        act.wait_ge(q["xg_full"], g * CF + f + 1)
                        b = 3 * (f % 2)
                        for j, (c0, c1) in enumerate(zip(CUTS, CUTS[1:])):
                            c1 = min(c1, SEQ)
                            act.copy(raw[:, f % 2, CK - 1 + c0:CK - 1 + c1], bank[:, b + j, 0:c1 - c0])
                        act.copy(rs[:, :, CK - 1:], bank[:, b + 2, SEQ - CUTS[2]:TOK - CUTS[2]].rearrange("p (s w) -> p s w", s=NSEQ)).then_inc(q["raw_ready"], 1)
                    if f:
                        act.wait_ge(q["conv_done"], g * CF + f)
                        act.activation(xbc[:, f - 1, :], xbc[:, f - 1, :], ACT.Silu).then_inc(q["conv_ready"], 1)

                act.wait_ge(wx_landed[0], g * 48 + 64)
                act.copy(wxh[:, 0, :, :], wx[:, 0, :, :]).then_inc(wh_ready, 1)

                def turn(c, n):
                    r = ROWS[c]
                    act.wait_ge(q["yT_full"], n + 1)
                    act.wait_ge(q["yT_stored"], n * 16)
                    act.copy(yT[:, :, 0:r], bank[:, 0, :].rearrange("p (f r) -> p f r", f=XF)[:, :, 0:r]).then_inc(q["yT_ready"], 1)

                for c in range(NT):
                    n = g * NT + c
                    r = ROWS[c]
                    act.wait_ge(q["x_full"], n + 1)
                    act.wait_ge(q["gated"], n)
                    act.copy(xt[0:r, :], bank[0:r, 0, :]).then_inc(q["xt_ready"], 1)
                    act.wait_ge(q["bc_full"], n + 1)
                    if c:
                        act.wait_ge(q["st_full"], g * LC + c)
                    else:
                        act.wait_ge(q["bseq_ready"], g)
                    act.copy(btok[0:r, :], bank[0:r, 1, 0:DS]).then_inc(q["btok_ready"], 1)
                    act.wait_ge(q["seg_full"], n + 1)
                    if c < LC:
                        act.activation(mix[:, c % 2, :], bank[:, 2:4, :].rearrange("p b n -> p (b n)"), ACT.Exp).then_inc(q["e_ready"], 1)
                    else:
                        act.activation(mix[0:r, c % 2, 0:HG * r], bank[0:r, 2, :], ACT.Exp).then_inc(q["e_ready"], 1)
                    act.wait_ge(q["z_full"], n + 1)
                    act.activation(zs[0:r, :], bank[P - r:P, 4, :], ACT.Silu).then_inc(q["z_ready"], 1)
                    if c:
                        turn(c - 1, n - 1)
                    if c == LC:
                        for sq in range(NSEQ):
                            act.wait_ge(q["h0_full"], g * NSEQ + sq + 1)
                            if sq == 0:
                                act.wait_ge(q["fin_stored"], g * 16)
                            else:
                                if sq >= 2:
                                    act.wait_ge(q["yo_used"], g * NSEQ + sq - 1)
                            act.copy(h0T[:, sq % 2, :], bank[:, 7, :]).then_inc(q["h0_ready"], 1)
                    act.wait_ge(q["gated"], n + 1)
                    act.wait_ge(q["ssy_ready"], n)
                    act.activation(square[0:r, 0:GW], y[0:r, :], ACT.Square, accum_out=ybuf[0:r, 0:1]).then_inc(q["ssy_ready"], 1)
                act.wait_ge(q["fin_full"], g + 1)
                act.wait_ge(q["yo_used"], g * NSEQ + NSEQ)
                act.copy(h0T[:, 0, :], bank[:, 7, :]).then_inc(q["fin_ready"], 1)
                turn(NT - 1, g * NT + NT - 1)
            for j in range(CONVF // 4):
                act.wait_ge(q["tail_full"], j + 1)
                act.copy(tail_rows[:, j // 2, 512 * (j % 2):512 * (j % 2) + 512], bank[0:TAIL, 4 + j % 2, :]).then_inc(q["tail_ready"], 1)
            out_scalar(act)
            ple_scalar(act, 0, 1)
            section3_scalar(act)
            section4_scalar(act)
            section5_scalar(act)
            ple_scalar(act, 1, 4)

        @block.vector
        def _(dve):
            chain = Chain(dve, q["vchain"])
            norm_vector(dve, 0, low=uL1)
            dve.wait_ge(wh_ready, 1)
            dve.tensor_tensor(wdtl[:, :, :], wdt[:, :, :], wdth[:, :, :].bitcast(F32), ALU.subtract).then_inc(wl_ready, 1)
            n = NT * NH
            dve.wait_ge(q["dt_full"], 2)
            dve.wait_ge(q["vec_loaded"], 64)
            chain(dve.memset(tiny[:, :, :], 0.0))
            for t in range(NT):
                r = ROWS[t]
                last = dve.tensor_tensor(tiny[0:r, 0, t * NH:(t + 1) * NH], bank[0:r, DTBANK[t // 4], (t % 4 + 1) * P - NH:(t % 4 + 1) * P], vec[0:r, 0:NH], ALU.add)
            last.then_inc(q["dt_ready"], 1)
            dve.wait_ge(q["dt_ready"], 1)
            dve.wait_ge(q["acum_ready"], 2)
            w, e, x = tiny[:, 1, :], tiny[:, 2, :], tiny[:, 0, :]
            chain(dve.tensor_scalar(w, e, 1.0, None, ALU.add))
            chain(dve.tensor_scalar(tiny[:, 4, :], w, -1.0, None, ALU.add))
            chain(dve.tensor_tensor(tiny[:, 4, :], e, tiny[:, 4, :], ALU.subtract))
            chain(dve.reciprocal(w, w))
            chain(dve.tensor_tensor(w, w, tiny[:, 4, :], ALU.mult))
            chain(dve.tensor_tensor(w, w, tiny[:, 3, :], ALU.add))
            flat = dtv[:, :, :].rearrange("p t h -> p (t h)")
            chain(dve.scalar_tensor_tensor(flat, x, 0.0, w, ALU.max, ALU.add))
            chain(dve.tensor_scalar(vec[:, NH:2 * NH], vec[:, NH:2 * NH], -1.0, None, ALU.mult))
            dve.tensor_tensor(dta[:, :, :], dtv[:, :, :], over(vec[:, NH:2 * NH], P, NT, NH), ALU.mult).then_inc(q["dt_ready"], 1)
            dve.wait_ge(q["acum_full"], 2)
            dve.wait_ge(q["acum_ready"], 4)
            for r, c0, c1 in ((P, 0, PT * NH), (SAMP, PT * NH, n)):
                chain(dve.tensor_copy(tiny[0:r, 4, c0:c1], bank[0:r, 6, c0:c1]))
                last = dve.tensor_tensor(tiny[0:r, 4, c0:c1], tiny[0:r, 4, c0:c1], bank[0:r, 5, c0:c1], ALU.subtract)
            last.then_inc(q["dt_ready"], 1)
            dve.wait_ge(q["turned_ready"], 3)

            def low_x(g, f):
                dve.wait_ge(wh_ready, g * IN_SPLITS + (f + 2))
                dve.tensor_tensor(wxl[:, f % 2, :, :], wx[:, f % 2, :, :], wxh[:, f % 2, :, :].bitcast(F32), ALU.subtract).then_inc(wl_ready, 1)

            low_x(0, 0)
            with dve.Fori(0, NG) as g:
                chain.enter(g, VSTEPS)
                dve.wait_ge(q["cwg_ready"], g + 1)
                dve.wait_ge(q["fin_full"], g)
                chain(dve.memset(hT[:, :], 0.0))
                dve.wait_ge(q["state_stored"], g * (16 * NSEQ))
                chain(dve.memset(raw[:, :, 0:CK - 1], 0.0))
                for f in range(CF):
                    if f + 1 < CF:
                        low_x(g, f + 1)
                    if f == CF - 2:
                        dve.wait_ge(wh_ready, g * IN_SPLITS + (IN_SPLITS + 1))
                        dve.tensor_tensor(wzl[:, :, :], wz[:, :, :], wzh[:, :, :].bitcast(F32), ALU.subtract).then_inc(wl_ready, 1)
                    ft = [g * XF + f, g + NG * XF, g + NG * XF + NG][max(0, f - XF + 1)]
                    dve.wait_ge(q["raw_ready"], g * CF + f + 1)
                    rs = raw[:, f % 2, SOFF:RAWW].rearrange("p (s w) -> p s w", s=NSEQ)
                    dst = xbc[:, f, SEQ:TOK].rearrange("p (s w) -> p s w", s=NSEQ)
                    dve.tensor_copy(tail[:, bass.ds(ft, 1), 0:CK - 1], raw[:, f % 2, SOFF - (CK - 1):SOFF].unsqueeze(1))
                    dve.tensor_copy(tail[:, bass.ds(ft, 1), CK - 1:].rearrange("p f (s w) -> p (f s) w", s=NSEQ), rs[:, :, DSEQ:])
                    for k in range(CK):
                        wk = cwg[:, f, k:k + 1]
                        parts = ((xbc[:, f, 0:SEQ], raw[:, f % 2, k:k + SEQ]), (dst, rs[:, :, k:k + DSEQ]))
                        for m, (d, src) in enumerate(parts):
                            if k == 0:
                                ins = dve.tensor_scalar(d, src, wk, cwg[:, f, CK:CK + 1], ALU.mult, ALU.add)
                            else:
                                ins = dve.scalar_tensor_tensor(d, src, wk, d, ALU.mult, ALU.add)
                        if k < CK - 1:
                            chain(ins)
                    ins.then_inc(q["conv_done"], 1)
                low_x(g + 1, 0)
                dve.wait_ge(q["nw_landed"], g * 16 + 16)
                for c in range(NT):
                    m = g * NT + c
                    r = ROWS[c]
                    hv = lambda t: t.rearrange("p (h d) -> p h d", h=HG)
                    hs = bass.ds(g * HG, HG)
                    dve.wait_ge(q["btok_ready"], m + 1)
                    dve.tensor_tensor(cbm[0:r, 0:r], bank[0:r, 1, DS:DS + r], con("tri" if c < LC else "tri8", r)[:, 0:r], ALU.mult).then_inc(q["cbm_ready"], 1)
                    dve.wait_ge(q["xt_ready"], m + 1)
                    dve.wait_ge(q["yd_full"], m)
                    dve.wait_ge(q["xdtd_ready"], m)
                    dve.tensor_tensor(hv(xdt[0:r, :]), hv(xt[0:r, :]), bc(dtv[0:r, c, hs], r, HG, HD), ALU.mult).then_inc(q["xdt_ready"], 1)
                    dve.wait_ge(q["e_ready"], m + 1)
                    dve.wait_ge(q["cbm_ready"], m + 1)
                    mv = mix[0:r, c % 2, 0:HG * r].rearrange("p (h l) -> p h l", h=HG)
                    dve.tensor_tensor(mv, mv, over(cbm[0:r, 0:r], r, HG, r), ALU.mult).then_inc(q["m_ready"], 1)
                    if c == LC:
                        dve.wait_ge(q["btok_ready"], m + 1)
                        dve.tensor_tensor(bseq[:, :, :], over(btok[0:r, :], r, NSEQ, DS), bc(con("inseq", r), r, NSEQ, DS), ALU.mult).then_inc(q["bseq_ready"], 1)
                        chain(dve.memset(cseq[:, :, :], 0.0))
                        for sq in range(NSEQ):
                            ins = dve.tensor_copy(cseq[:, sq, sq * DSEQ:(sq + 1) * DSEQ], xbc[:, XF + 1, SEQ + sq * DSEQ:SEQ + (sq + 1) * DSEQ])
                        dve.tensor_copy(hv(dexp[:, :]), bc(dec[0:r, c, hs], r, HG, HD)).then_inc(q["dexp_ready"], 1)
                        dve.wait_ge(q["sdec_full"], g + 1)
                        chain(dve.tensor_copy(sdec[:, :, :], bank[:, 6, 0:XF * NSEQ].rearrange("p (f s) -> p f s", f=XF)))
                        for sq in range(NSEQ):
                            dve.wait_ge(q["snew_full"], g * NSEQ + sq + 1)
                            sv = st[:, sq % 4, :, :]
                            chain(dve.tensor_tensor(sv, sv, bc(sdec[:, :, sq], P, XF, DS), ALU.mult))
                            dve.tensor_tensor(sv, sv, bank[:, 1 + 2 * (sq % 2), :].rearrange("p (f n) -> p f n", f=XF), ALU.add).then_inc(q["snew_ready"], 1)
                    dve.wait_ge(q["yd_full"], m + 1)
                    dve.wait_ge(q["yn_ready"], m)
                    dve.wait_ge(q["yT_full"], m)
                    chain(dve.tensor_tensor(hv(y[0:r, :]), hv(bank[0:r, 5, :]), bc(ea[0:r, c, hs], r, HG, HD), ALU.mult))
                    chain(dve.tensor_tensor(y[0:r, :], y[0:r, :], bank[0:r, 6, :], ALU.add))
                    dve.wait_ge(q["skip_ready"], m + 1)
                    chain(dve.tensor_tensor(y[0:r, :], y[0:r, :], xt[0:r, :], ALU.add))
                    dve.wait_ge(q["z_ready"], m + 1)
                    dve.tensor_tensor(y[0:r, :], y[0:r, :], zs[0:r, :], ALU.mult).then_inc(q["gated"], 1)
                    if c < LC:
                        dve.wait_ge(q["st_full"], g * LC + c + 1)
                        chain(dve.tensor_tensor(hv(hT[:, :]), hv(hT[:, :]), bc(dec[:, c, hs], P, HG, HD), ALU.mult))
                        dve.tensor_tensor(hT[:, :], hT[:, :], bank[:, 7, :], ALU.add).then_inc(q["hT_ready"], 1)
                    dve.wait_ge(q["ssy_ready"], m + 1)
                    dve.tensor_scalar(ybuf[0:r, 1:2], ybuf[0:r, 0:1], 1.0 / GW, EPS, ALU.mult, ALU.add).then_inc(q["msy_ready"], 1)
                    dve.wait_ge(q["ry_ready"], m + 1)
                    dve.scalar_tensor_tensor(y[0:r, :], y[0:r, :], ybuf[0:r, 2:3], nwg[0:r, :], ALU.mult, ALU.mult).then_inc(q["yn_ready"], 1)
                chain.leave(NG)
            out_vector(dve)
            ple_vector(dve, 0, 1)
            section3_vector(dve, chain)
            section4_vector(dve, chain)
            section5_vector(dve, chain)
            ple_vector(dve, 1, 4)

        @block.tensor
        def _(pe):
            pe.wait_ge(q["const_loaded"], 16)
            norm_tensor(pe, 0, low=uL1)
            pe.wait_ge(q["cw_loaded"], 48)
            pe.transpose(bank[:, 4, 0:(CK + 1) * CONVF], cw_rows, ident[0:(CK + 1) * CONVF, 0:(CK + 1) * CONVF]).then_inc(q["turned_full"], 1)
            w = NSEQ * (CK - 1)
            for f in range(CONVF):
                last = pe.transpose(bank[:, 5 + f // 12, (f % 12) * w:(f % 12 + 1) * w], sc_rows[:, f // 8, (f % 8) * P:(f % 8 + 1) * P], ident[0:w, 0:w])
                if f % 12 == 11:
                    last.then_inc(q["turned_full"], 1)
            pe.wait_ge(uT_ready, 2 * NT)
            pe.wait_ge(uL_ready, NT)
            pe.wait_ge(wl_ready, 1)
            for j, (c0, c1) in enumerate(zip(CUTS, CUTS[1:])):
                for k in range(KT):
                    to = bank[:, j, 0:c1 - c0]
                    pe.matmul(to, wdth[:, k, :], uH[:, k, c0:c1], start=(k == 0), stop=False)
                    pe.matmul(to, wdth[:, k, :], uL1[:, k, c0:c1], start=False, stop=False)
                    last = pe.matmul(to, wdtl[:, k, :], uH[:, k, c0:c1], start=False, stop=(k == KT - 1))
            last.then_inc(q["dt_full"], 1)
            pe.wait_ge(q["turned_ready"], 4)
            for t in range(NT):
                last = pe.transpose(bank[0:ROWS[t], DTBANK[t // 4], t % 4 * P:(t % 4 + 1) * P], dtT[:, cols(t)], ident)
            last.then_inc(q["dt_full"], 1)
            pe.wait_ge(q["dt_ready"], 2)
            pe.wait_ge(q["turned_ready"], 3)
            pe.wait_ge(q["memset_done"], 4)
            for b, full, part in ((5, "tri", "tri8"), (6, None, "same8")):
                for t in range(NT):
                    r = ROWS[t]
                    m = (con(full) if full else ones[:, :]) if t < PT else con(part, r)[:, 0:r]
                    last = pe.matmul(bank[0:r, b, t * NH:(t + 1) * NH], m, dta[0:r, t, :], start=True, stop=True)
                last.then_inc(q["acum_full"], 1)
            pe.wait_ge(q["acum_ready"], 5)
            with pe.Fori(0, NG) as g:
                pe.wait_ge(q["yT_ready"], g * NT)
                pe.wait_ge(q["fin_ready"], g)
                for f in range(CF):
                    pe.wait_ge(wl_ready, g * IN_SPLITS + (f + 2))
                    if f > 1:
                        pe.wait_ge(q["raw_ready"], g * CF + f - 1)
                    for j, (c0, c1) in enumerate(zip(CUTS, CUTS[1:])):
                        for k in range(KT):
                            to = bank[:, 3 * (f % 2) + j, 0:c1 - c0]
                            pe.matmul(to, wxh[:, f % 2, k, :], uH[:, k, c0:c1], start=(k == 0), stop=False)
                            pe.matmul(to, wxh[:, f % 2, k, :], uL1[:, k, c0:c1], start=False, stop=False)
                            last = pe.matmul(to, wxl[:, f % 2, k, :], uH[:, k, c0:c1], start=False, stop=(k == KT - 1))
                    last.then_inc(q["xg_full"], 1)
                pe.wait_ge(q["raw_ready"], g * CF + CF)

                def multiply_z(c, n):
                    if c == 0:
                        pe.wait_ge(wl_ready, g * IN_SPLITS + (IN_SPLITS + 1))
                    pe.wait_ge(q["z_ready"], n)
                    if c == LC:
                        alone(pe)
                    ts = slice(min(c * P, TOK - P), min(c * P, TOK - P) + P)
                    for k in range(KT):
                        pe.matmul(bank[:, 4, :], uH[:, k, ts], wzh[:, k, :], start=(k == 0), stop=False)
                        pe.matmul(bank[:, 4, :], uH[:, k, ts], wzl[:, k, :], start=False, stop=False)
                        last = pe.matmul(bank[:, 4, :], uL1[:, k, ts], wzh[:, k, :], start=False, stop=(k == KT - 1))
                    last.then_inc(q["z_full"], 1)

                multiply_z(0, g * NT)
                pe.wait_ge(q["conv_ready"], g * CF + CF)

                def turn_y(c, n):
                    r = ROWS[c]
                    pe.wait_ge(q["yn_ready"], n + 1)
                    alone(pe)
                    for f in range(XF):
                        last = pe.transpose(bank[:, 0, f * P:f * P + r], y[0:r, f * P:(f + 1) * P], ident[0:r, 0:r])
                    last.then_inc(q["yT_full"], 1)

                for c in range(NT):
                    n = g * NT + c
                    r = ROWS[c]
                    cs = cols(c)
                    if c > 1:
                        pe.wait_ge(q["yT_ready"], n - 1)
                    if c == LC:
                        alone(pe)
                    for f in range(XF):
                        last = pe.transpose(bank[0:r, 0, f * P:(f + 1) * P], xbc[:, f, cs], ident)
                    last.then_inc(q["x_full"], 1)
                    pe.wait_ge(q["btok_ready"], n)
                    pe.wait_ge(q["cbm_ready"], n)
                    if c == LC:
                        alone(pe)
                    pe.transpose(bank[0:r, 1, 0:DS], xbc[:, XF, cs], ident)
                    pe.matmul(bank[0:r, 1, DS:DS + r], xbc[:, XF, cs], xbc[:, XF + 1, cs], start=True, stop=True).then_inc(q["bc_full"], 1)
                    pe.wait_ge(q["sum_ready"], n + 1)
                    if c == LC:
                        alone(pe)
                    if c < LC:
                        for half in range(2):
                            last = pe.matmul(bank[:, 2 + half, :], con("after"), mix[:, c % 2, 512 * half:512 * (half + 1)], start=True, stop=True)
                    else:
                        last = pe.matmul(bank[0:r, 2, :], con("after8", r)[:, 0:r], mix[0:r, c % 2, 0:HG * r], start=True, stop=True)
                    last.then_inc(q["seg_full"], 1)
                    if c:
                        multiply_z(c, n)
                    if c:
                        pe.wait_ge(q["xt_ready"], n + 1)
                        turn_y(c - 1, n - 1)
                    pe.wait_ge(q["gated"], n)
                    pe.wait_ge(q["m_ready"], n + 1)
                    pe.wait_ge(q["xdt_ready"], n + 1)
                    if c == LC:
                        pe.wait_ge(q["hT_ready"], g * LC + LC)
                        pe.wait_ge(q["dexp_ready"], g + 1)
                        alone(pe)
                        for f in range(XF):
                            last = pe.matmul(bank[:, 6, f * NSEQ:(f + 1) * NSEQ], dexp[:, f * P:(f + 1) * P], con("first", r), start=True, stop=True)
                        last.then_inc(q["sdec_full"], 1)
                        pe.wait_ge(q["bseq_ready"], g + 1)
                        pe.wait_ge(q["xdtd_ready"], n + 1)
                        pe.wait_ge(q["btok_ready"], n + 1)
                        pe.wait_ge(q["cbm_ready"], n + 1)
                        pe.wait_ge(q["e_ready"], n + 1)

                        def turn_state(sq):
                            pe.wait_ge(st_landed[sq % 4], g * 32 + 16 * (sq // 4 + 1))
                            if sq:
                                pe.wait_ge(q["h0_ready"], g * NSEQ + sq)
                            for f in range(XF):
                                last = pe.transpose(bank[:, 7, f * P:(f + 1) * P], st[:, sq % 4, f, :], ident)
                            last.then_inc(q["h0_full"], 1)

                        turn_state(0)
                        for sq in range(NSEQ):
                            if sq > 1:
                                pe.wait_ge(q["snew_ready"], g * NSEQ + sq - 1)
                            alone(pe)
                            for f in range(XF):
                                last = pe.matmul(bank[:, 1 + 2 * (sq % 2), f * P:(f + 1) * P], xdtd[0:r, f * P:(f + 1) * P], bseq[:, sq, :], start=True, stop=True)
                            last.then_inc(q["snew_full"], 1)
                            if sq + 1 < NSEQ:
                                turn_state(sq + 1)
                            pe.wait_ge(q["h0_ready"], g * NSEQ + sq + 1)
                            alone(pe)
                            pe.matmul(bank[0:r, 5, :], cseq[:, sq, :], h0T[:, sq % 2, :], start=(sq == 0), stop=(sq == NSEQ - 1)).then_inc(q["yo_used"], 1)
                        pe.wait_ge(q["snew_ready"], g * NSEQ + NSEQ)
                    else:
                        if c:
                            pe.wait_ge(q["hT_ready"], g * LC + c)
                        else:
                            pe.wait_ge(q["raw_ready"], g * CF + CF)
                        pe.matmul(bank[:, 5, :], xbc[:, XF + 1, cs], hT[:, :], start=True, stop=True)
                    if c == LC:
                        alone(pe)
                    for hh in range(HG):
                        last = pe.matmul(bank[0:r, 6, hh * HD:(hh + 1) * HD], mix[0:r, c % 2, hh * r:(hh + 1) * r],
                                         xdt[0:r, hh * HD:(hh + 1) * HD], start=True, stop=True)
                    last.then_inc(q["yd_full"], 1)
                    if c < LC:
                        pe.wait_ge(q["xdtd_ready"], n + 1)
                        pe.wait_ge(q["btok_ready"], n + 1)
                        pe.matmul(bank[:, 7, :], btok[:, :], xdtd[:, :], start=True, stop=True).then_inc(q["st_full"], 1)
                pe.wait_ge(q["h0_ready"], g * NSEQ + NSEQ)
                for f in range(XF):
                    last = pe.transpose(bank[:, 7, f * P:(f + 1) * P], hT[:, f * P:(f + 1) * P], ident)
                last.then_inc(q["fin_full"], 1)
                turn_y(NT - 1, g * NT + NT - 1)
            for j in range(CONVF // 4):
                if j > 1:
                    pe.wait_ge(q["tail_ready"], j - 1)
                for i in range(4):
                    last = pe.transpose(bank[0:TAIL, 4 + j % 2, i * P:(i + 1) * P], tail[:, 4 * j + i, :], ident)
                last.then_inc(q["tail_full"], 1)
            out_tensor(pe)
            ple_tensor(pe, 0, 1)
            section3_tensor(pe)
            section4_tensor(pe)
            section5_tensor(pe)
            ple_tensor(pe, 1, 4)


_INS = ["x_prompt", "x_sample", "state_ssm", "state_conv", "cache_kv_g1", "cache_kv_g2", "cache_kv_g3",
        "p_prompt", "p_sample", "norm_w", "m_in_w", "m_conv_w", "m_conv_b", "m_dt_bias", "m_A_log", "m_D",
        "m_norm_w", "m_out_w", "kv_norm_w", "kv_w", "k_norm_w", "a_in_w", "a_q_norm_w", "a_out_w",
        "ple_w", "ple_gate_w", "ple_norm_w"]
KV = (2, KVH, HD)
_OUTS = {"y_prompt": (1, SEQ, D), "y_sample": (NSEQ, DSEQ, D), "ssm_prompt": (1, 1, NH, HD, DS),
         "conv_prompt": (1, 1, CK - 1, CONVF * P), "ssm_sample": (1, NSEQ, NH, HD, DS),
         "conv_sample": (1, NSEQ, CK - 1, CONVF * P),
         "kv_prompt_g1": (1, 128) + KV, "kv_prompt_g2": (1, 512) + KV, "kv_prompt_g3": (1, 1024) + KV,
         "kv_sample_g1": (NSEQ, DSEQ) + KV, "kv_sample_g2": (NSEQ, DSEQ) + KV, "kv_sample_g3": (NSEQ, DSEQ) + KV}
_SCRATCH = {"yT": (DI, TOK), "kv": (TOK, 2, NGR, KVH * HD), "q": (TOK, NGR, D), "gate": (TOK, D), "u": (NGR, SEQ, D), "ms": (NGR, SEQ, 2 * AH),
            "os": (SAMP, D)}


def kernel(**inputs):
    import concourse.bacc as bacc
    from concourse.bass_utils import run_bass_kernel_spmd

    nc = bacc.Bacc("TRN2", target_bir_lowering=False, num_devices=1)
    arrays, a = {}, {}
    for name in _INS:
        x = np.ascontiguousarray(inputs[name])
        arrays[f"in_{name}"] = x
        a[name] = nc.dram_tensor(f"in_{name}", x.shape, mybir.dt.from_np(x.dtype), kind="ExternalInput").ap()
    table = np.concatenate([v for v in shape_constants().values()], 1)
    arrays["in_consts"] = table
    a["consts"] = nc.dram_tensor("in_consts", table.shape, F32, kind="ExternalInput").ap()
    o = {n: nc.dram_tensor(f"out_{n}", shape, F32, kind="ExternalOutput").ap() for n, shape in _OUTS.items()}
    s = {n: nc.dram_tensor(f"scratch_{n}", shape, F32).ap() for n, shape in _SCRATCH.items()}
    trunk_kernel(nc, a, o, s)
    r = run_bass_kernel_spmd(nc, [arrays], core_ids=[0])
    return tuple(r.results[0][f"out_{n}"] for n in _OUTS)
```
